# Optimizing a Trainium2 kernel written in Bass

```python
import jax, jax.numpy as jnp
from jax import lax
import numpy as np

D_MODEL = 1024
BATCH = 1
SEQ = 512
DEPTH = 1

NSA_HEADS = 8
NSA_KV_GROUPS = 2
NSA_HEAD_DIM = 64
CMP_BLOCK = 32
CMP_STRIDE = 16
CMP_HIDDEN = 128
SEL_BLOCK = 64
SEL_TOPK = 8
WINDOW = 512
Q_BLOCK = 128
GLA_HEADS = 4
GLA_DK = 64
GLA_DV = 128
GLA_CHUNK = 64
GLA_LOWRANK = 16
GLA_TAU = 16.0
D_FF = 2816
EPS = 1e-6
NEG_INF = -1e30
FORCE = 1e9

NSA_Q_W = NSA_HEADS * NSA_HEAD_DIM
NSA_KV_W = NSA_KV_GROUPS * NSA_HEAD_DIM
GLA_K_W = GLA_HEADS * GLA_DK
GLA_V_W = GLA_HEADS * GLA_DV
D_MIX = NSA_Q_W + GLA_V_W
IN_SPLITS = (NSA_Q_W, NSA_KV_W, NSA_KV_W, NSA_KV_W, NSA_KV_W, NSA_KV_W, NSA_KV_W, NSA_HEADS * 3, GLA_K_W, GLA_K_W, GLA_V_W, GLA_V_W, GLA_LOWRANK)
D_IN_PROJ = sum(IN_SPLITS)


def rmsnorm(x, g):
    xf = x.astype(jnp.float32)
    y = xf * lax.rsqrt(jnp.mean(xf * xf, axis=-1, keepdims=True) + EPS)
    return (y * g.astype(jnp.float32)).astype(x.dtype)

def swiglu_ffn(x, w_gate, w_up, w_down):
    return (jax.nn.silu(x @ w_gate) * (x @ w_up)) @ w_down

def split_columns(y, sizes):
    offsets = [int(o) for o in np.cumsum(sizes)[:-1]]
    return jnp.split(y, offsets, axis=-1)

def compress_blocks(kv, pe, w1, w2):
    B, T, G, dh = kv.shape
    n_cmp = (T - CMP_BLOCK) // CMP_STRIDE + 1
    idx = jnp.arange(n_cmp)[:, None] * CMP_STRIDE + jnp.arange(CMP_BLOCK)[None, :]
    blocks = kv[:, idx] + pe[None, None, :, None, :]
    blocks = blocks.transpose(0, 1, 3, 2, 4).reshape(B, n_cmp, G, CMP_BLOCK * dh)
    return jax.nn.gelu(blocks @ w1) @ w2

def nsa_attention(q, k_cmp, v_cmp, k_slc, v_slc, k_win, v_win, gates, pe_k, w1_k, w2_k, pe_v, w1_v, w2_v):
    B, T, H, dh = q.shape
    G = NSA_KV_GROUPS
    R = H // G
    f32 = jnp.float32
    scale = dh ** -0.5
    slopes = jnp.exp2(-8.0 * jnp.arange(1, H + 1, dtype=f32) / H).reshape(G, R)

    kc = compress_blocks(k_cmp, pe_k, w1_k, w2_k)
    vc = compress_blocks(v_cmp, pe_v, w1_v, w2_v)
    n_cmp = kc.shape[1]
    cmp_start = jnp.arange(n_cmp, dtype=jnp.int32) * CMP_STRIDE
    cmp_end = cmp_start + CMP_BLOCK - 1
    cmp_center = cmp_start.astype(f32) + (CMP_BLOCK - 1) / 2.0

    n_sel_blocks = T // SEL_BLOCK
    top_n = min(SEL_TOPK, n_sel_blocks)
    sel_start = jnp.arange(n_sel_blocks, dtype=jnp.int32) * SEL_BLOCK
    overlap = ((cmp_start[:, None] < sel_start[None, :] + SEL_BLOCK)
               & (cmp_start[:, None] + CMP_BLOCK > sel_start[None, :])).astype(f32)
    k_blk = k_slc.reshape(B, n_sel_blocks, SEL_BLOCK, G, dh).transpose(0, 3, 1, 2, 4)
    v_blk = v_slc.reshape(B, n_sel_blocks, SEL_BLOCK, G, dh).transpose(0, 3, 1, 2, 4)

    k_pad = jnp.pad(k_win, ((0, 0), (WINDOW, 0), (0, 0), (0, 0)))
    v_pad = jnp.pad(v_win, ((0, 0), (WINDOW, 0), (0, 0), (0, 0)))

    n_qb = T // Q_BLOCK
    q_blocks = q.reshape(B, n_qb, Q_BLOCK, G, R, dh).transpose(1, 0, 2, 3, 4, 5)
    g_blocks = gates.reshape(B, n_qb, Q_BLOCK, G, R, 3).transpose(1, 0, 2, 3, 4, 5)
    b_ix = jnp.arange(B)[:, None, None, None]
    g_ix = jnp.arange(G)[None, :, None, None]
    win_off = jnp.arange(WINDOW + Q_BLOCK, dtype=jnp.int32) - WINDOW
    sel_off = jnp.arange(SEL_BLOCK, dtype=jnp.int32)
    j_blk = jnp.arange(n_sel_blocks, dtype=jnp.int32)

    def block_fn(args):
        qb, gb, blk = args
        t = blk * Q_BLOCK + jnp.arange(Q_BLOCK, dtype=jnp.int32)
        tf = t.astype(f32)
        qs = qb * scale

        s = jnp.einsum('bqgrd,bngd->bgrqn', qs, kc).astype(f32)
        s = s - slopes[:, :, None, None] * (tf[:, None] - cmp_center[None, :])
        valid_c = cmp_end[None, :] <= t[:, None]
        s = jnp.where(valid_c, s, NEG_INF)
        p_c = jax.nn.softmax(s, axis=-1) * valid_c
        o_cmp = jnp.einsum('bgrqn,bngd->bqgrd', p_c.astype(vc.dtype), vc)

        imp = jnp.einsum('bgrqn,ns->bgqs', p_c, overlap)
        cur = t // SEL_BLOCK
        forced = (j_blk[None, :] == 0) | (j_blk[None, :] == cur[:, None]) | (j_blk[None, :] == cur[:, None] - 1)
        causal_blk = j_blk[None, :] <= cur[:, None]
        imp = jnp.where(forced, FORCE, imp)
        imp = jnp.where(causal_blk, imp, -FORCE)
        _, sel = lax.top_k(imp, top_n)
        k_sel = k_blk[b_ix, g_ix, sel]
        v_sel = v_blk[b_ix, g_ix, sel]
        kpos = sel[..., None] * SEL_BLOCK + sel_off
        dist = t[None, None, :, None, None] - kpos
        s = jnp.einsum('bqgrd,bgqnkd->bgrqnk', qs, k_sel).astype(f32)
        s = s - slopes[None, :, :, None, None, None] * dist[:, :, None].astype(f32)
        s = jnp.where((dist >= 0)[:, :, None], s, NEG_INF)
        p_s = jax.nn.softmax(s.reshape(B, G, R, Q_BLOCK, top_n * SEL_BLOCK), axis=-1).reshape(s.shape)
        o_slc = jnp.einsum('bgrqnk,bgqnkd->bqgrd', p_s.astype(v_sel.dtype), v_sel)

        kw = lax.dynamic_slice_in_dim(k_pad, blk * Q_BLOCK, WINDOW + Q_BLOCK, axis=1)
        vw = lax.dynamic_slice_in_dim(v_pad, blk * Q_BLOCK, WINDOW + Q_BLOCK, axis=1)
        kpos_w = blk * Q_BLOCK + win_off
        dist_w = t[:, None] - kpos_w[None, :]
        mask_w = (dist_w >= 0) & (dist_w < WINDOW) & (kpos_w[None, :] >= 0)
        s = jnp.einsum('bqgrd,bkgd->bgrqk', qs, kw).astype(f32)
        s = s - slopes[:, :, None, None] * dist_w.astype(f32)
        s = jnp.where(mask_w, s, NEG_INF)
        p_w = jax.nn.softmax(s, axis=-1)
        o_win = jnp.einsum('bgrqk,bkgd->bqgrd', p_w.astype(vw.dtype), vw)

        o = gb[..., 0:1] * o_cmp + gb[..., 1:2] * o_slc + gb[..., 2:3] * o_win
        return o.reshape(B, Q_BLOCK, H * dh)

    out = lax.map(block_fn, (q_blocks, g_blocks, jnp.arange(n_qb, dtype=jnp.int32)))
    return out.transpose(1, 0, 2, 3).reshape(B, T, H * dh)

def gla_attention(q, k, v, log_a):
    B, T, Hh, dk = q.shape
    dv = v.shape[-1]
    C = GLA_CHUNK
    N = T // C
    f32 = jnp.float32

    def chunks(z):
        return z.astype(f32).reshape(B, N, C, Hh, z.shape[-1]).transpose(1, 0, 3, 2, 4)

    qc = chunks(q) * (dk ** -0.5)
    kc = chunks(k)
    vc = chunks(v)
    b = jnp.cumsum(chunks(log_a), axis=3)
    b_last = b[:, :, :, -1:]
    q_in = qc * jnp.exp(b)
    k_in = kc * jnp.exp(-b)
    k_st = kc * jnp.exp(b_last - b)
    tril = jnp.tril(jnp.ones((C, C), dtype=bool))
    A = jnp.where(tril, jnp.einsum('nbhid,nbhjd->nbhij', q_in, k_in), 0.0)
    o_intra = jnp.einsum('nbhij,nbhjv->nbhiv', A, vc)

    def step(S, xs):
        qi, ki, vi, bl = xs
        o = jnp.einsum('bhid,bhdv->bhiv', qi, S)
        S = S * jnp.exp(bl)[:, :, 0, :, None] + jnp.einsum('bhjd,bhjv->bhdv', ki, vi)
        return S, o

    S0 = jnp.zeros((B, Hh, dk, dv), f32)
    _, o_inter = lax.scan(step, S0, (q_in, k_st, vc, b_last))
    o = o_intra + o_inter
    return o.transpose(1, 0, 3, 2, 4).reshape(B, T, Hh, dv)

def hybrid_mixer(h, w_in, pe_k, w1_k, w2_k, pe_v, w1_v, w2_v, w_a2, b_a, gla_g, w_out):
    B, T, _ = h.shape
    proj = h @ w_in
    (q, kc, vc, ks, vs, kw, vw, g_nsa, gq, gk, gv, gr, ga) = split_columns(proj, IN_SPLITS)
    kv = lambda z: z.reshape(B, T, NSA_KV_GROUPS, NSA_HEAD_DIM)
    gates = jax.nn.sigmoid(g_nsa.astype(jnp.float32)).astype(h.dtype).reshape(B, T, NSA_HEADS, 3)
    o_nsa = nsa_attention(q.reshape(B, T, NSA_HEADS, NSA_HEAD_DIM), kv(kc), kv(vc), kv(ks), kv(vs), kv(kw), kv(vw),
                          gates, pe_k, w1_k, w2_k, pe_v, w1_v, w2_v)

    log_a = jax.nn.log_sigmoid((ga @ w_a2 + b_a).astype(jnp.float32)) / GLA_TAU
    o_gla = gla_attention(gq.reshape(B, T, GLA_HEADS, GLA_DK), gk.reshape(B, T, GLA_HEADS, GLA_DK),
                          gv.reshape(B, T, GLA_HEADS, GLA_DV), log_a.reshape(B, T, GLA_HEADS, GLA_DK))
    o_gla = rmsnorm(o_gla, gla_g) * jax.nn.silu(gr.astype(jnp.float32)).reshape(B, T, GLA_HEADS, GLA_DV)
    o_gla = o_gla.reshape(B, T, GLA_V_W).astype(h.dtype)

    return jnp.concatenate([o_nsa, o_gla], axis=-1) @ w_out

def first_inputs(seed: int = 0) -> dict:
    key = jax.random.key(seed)
    ks = jax.random.split(key, 24)
    f32 = jnp.float32

    def nrm(k, shape, scale):
        return jax.random.normal(k, shape, f32) * scale

    def gain(k, n):
        return 1.0 + 0.02 * jax.random.normal(k, (DEPTH, n), f32)

    L = DEPTH
    return {
        'x': nrm(ks[0], (BATCH, SEQ, D_MODEL), 1.0),
        'ffn1_norm': gain(ks[1], D_MODEL),
        'ffn1_w_gate': nrm(ks[2], (L, D_MODEL, D_FF), D_MODEL ** -0.5),
        'ffn1_w_up': nrm(ks[3], (L, D_MODEL, D_FF), D_MODEL ** -0.5),
        'ffn1_w_down': nrm(ks[4], (L, D_FF, D_MODEL), D_FF ** -0.5),
        'mix_norm': gain(ks[5], D_MODEL),
        'w_in': nrm(ks[6], (L, D_MODEL, D_IN_PROJ), D_MODEL ** -0.5),
        'nsa_pe_k': nrm(ks[7], (L, CMP_BLOCK, NSA_HEAD_DIM), 0.02),
        'nsa_w1_k': nrm(ks[8], (L, CMP_BLOCK * NSA_HEAD_DIM, CMP_HIDDEN), (CMP_BLOCK * NSA_HEAD_DIM) ** -0.5),
        'nsa_w2_k': nrm(ks[9], (L, CMP_HIDDEN, NSA_HEAD_DIM), CMP_HIDDEN ** -0.5),
        'nsa_pe_v': nrm(ks[10], (L, CMP_BLOCK, NSA_HEAD_DIM), 0.02),
        'nsa_w1_v': nrm(ks[11], (L, CMP_BLOCK * NSA_HEAD_DIM, CMP_HIDDEN), (CMP_BLOCK * NSA_HEAD_DIM) ** -0.5),
        'nsa_w2_v': nrm(ks[12], (L, CMP_HIDDEN, NSA_HEAD_DIM), CMP_HIDDEN ** -0.5),
        'gla_w_a2': nrm(ks[13], (L, GLA_LOWRANK, GLA_K_W), GLA_LOWRANK ** -0.5),
        'gla_b_a': nrm(ks[14], (L, GLA_K_W), 0.1),
        'gla_norm': gain(ks[15], GLA_DV),
        'w_out': nrm(ks[16], (L, D_MIX, D_MODEL), D_MIX ** -0.5),
        'ffn2_norm': gain(ks[17], D_MODEL),
        'ffn2_w_gate': nrm(ks[18], (L, D_MODEL, D_FF), D_MODEL ** -0.5),
        'ffn2_w_up': nrm(ks[19], (L, D_MODEL, D_FF), D_MODEL ** -0.5),
        'ffn2_w_down': nrm(ks[20], (L, D_FF, D_MODEL), D_FF ** -0.5),
        'final_norm': 1.0 + 0.02 * jax.random.normal(ks[21], (D_MODEL,), f32),
    }

def first_block(x, ffn1_norm, ffn1_w_gate, ffn1_w_up, ffn1_w_down, mix_norm, w_in,
              nsa_pe_k, nsa_w1_k, nsa_w2_k, nsa_pe_v, nsa_w1_v, nsa_w2_v,
              gla_w_a2, gla_b_a, gla_norm, w_out,
              ffn2_norm, ffn2_w_gate, ffn2_w_up, ffn2_w_down, final_norm):
    for l in range(DEPTH):
        x = x + 0.5 * swiglu_ffn(rmsnorm(x, ffn1_norm[l]), ffn1_w_gate[l], ffn1_w_up[l], ffn1_w_down[l])
        x = x + hybrid_mixer(rmsnorm(x, mix_norm[l]), w_in[l],
                             nsa_pe_k[l], nsa_w1_k[l], nsa_w2_k[l], nsa_pe_v[l], nsa_w1_v[l], nsa_w2_v[l],
                             gla_w_a2[l], gla_b_a[l], gla_norm[l], w_out[l])
        x = x + 0.5 * swiglu_ffn(rmsnorm(x, ffn2_norm[l]), ffn2_w_gate[l], ffn2_w_up[l], ffn2_w_down[l])
    return rmsnorm(x, final_norm)


D_POOL = D_MODEL
POOL_GROUPS = 4
POOL_GROUP_DIM = D_POOL // POOL_GROUPS
POOL_WINDOWS = (2, 4, 8, 16)
D_MLSTM = D_MODEL
MLSTM_HEADS = 4
HEAD_DIM = D_MLSTM // MLSTM_HEADS
N_DIRS = 2
CONV_WIDTH = 5
CHUNK = 128
N_BRANCHES = 2
NEG_INIT = -1e30
SPLIT_SIZES = (D_POOL, D_POOL, D_MLSTM, D_MLSTM, D_MLSTM, D_MLSTM, D_MLSTM,
               2 * N_DIRS * MLSTM_HEADS, D_MODEL, D_MODEL)
D_IN = 2 * D_POOL + 5 * D_MLSTM + 2 * N_DIRS * MLSTM_HEADS + N_BRANCHES * D_MODEL


def rms_norm(x, g):
    xf = x.astype(jnp.float32)
    y = xf * lax.rsqrt(jnp.mean(xf * xf, axis=-1, keepdims=True) + EPS)
    return (y * g.astype(jnp.float32)).astype(x.dtype)

def multiscale_pool(u):
    B, S, _ = u.shape
    uf = u.astype(jnp.float32)
    cs = jnp.concatenate([jnp.zeros((B, 1, D_POOL), jnp.float32), jnp.cumsum(uf, axis=1)], axis=1)
    t = jnp.arange(S)
    outs = []
    for g, w in enumerate(POOL_WINDOWS):
        lo = jnp.clip(t - w // 2, 0, S - 1)
        hi = jnp.clip(t + (w - 1 - w // 2), 0, S - 1)
        sl = slice(g * POOL_GROUP_DIM, (g + 1) * POOL_GROUP_DIM)
        csg = cs[:, :, sl]
        window_sum = jnp.take(csg, hi + 1, axis=1) - jnp.take(csg, lo, axis=1)
        count = (hi - lo + 1).astype(jnp.float32)[None, :, None]
        outs.append(window_sum / count - uf[:, :, sl])
    return jnp.concatenate(outs, axis=-1)

def centred_depthwise_conv(x, w, b):
    C = x.shape[-1]
    y = lax.conv_general_dilated(
        x, w[:, None, :].astype(x.dtype), window_strides=(1,),
        padding=[(CONV_WIDTH // 2, CONV_WIDTH // 2)],
        dimension_numbers=('NWC', 'WIO', 'NWC'), feature_group_count=C)
    return y + b.astype(x.dtype)

def mlstm_direction(q, k, v, i_pre, f_pre):
    B, H, S, Dh = q.shape
    nc = S // CHUNK
    qc = q.reshape(B, H, nc, CHUNK, Dh) * (Dh ** -0.5)
    kc = k.reshape(B, H, nc, CHUNK, Dh)
    vc = v.reshape(B, H, nc, CHUNK, Dh)
    log_f = jax.nn.log_sigmoid(f_pre).reshape(B, H, nc, CHUNK)
    log_i = i_pre.reshape(B, H, nc, CHUNK)
    b = jnp.cumsum(log_f, axis=-1)
    b_last = b[..., -1]

    w_end = b_last[..., None] - b + log_i
    m_chunk = jnp.max(w_end, axis=-1)
    kw = kc * jnp.exp(w_end - m_chunk[..., None])[..., None]
    c_chunk = jnp.einsum('bhcld,bhcle->bhcde', kw, vc)
    n_chunk = jnp.sum(kw, axis=3)

    def step(carry, xs):
        c_st, n_st, m_st = carry
        c_add, n_add, m_add, bl, q_blk = xs
        num_inter = jnp.einsum('bhld,bhde->bhle', q_blk, c_st)
        den_inter = jnp.einsum('bhld,bhd->bhl', q_blk, n_st)
        m_new = jnp.maximum(bl + m_st, m_add)
        keep = jnp.exp(bl + m_st - m_new)
        add = jnp.exp(m_add - m_new)
        c_new = keep[..., None, None] * c_st + add[..., None, None] * c_add
        n_new = keep[..., None] * n_st + add[..., None] * n_add
        return (c_new, n_new, m_new), (num_inter, den_inter, m_st)

    init = (jnp.zeros((B, H, Dh, Dh), jnp.float32),
            jnp.zeros((B, H, Dh), jnp.float32),
            jnp.full((B, H), NEG_INIT, jnp.float32))
    xs = (jnp.moveaxis(c_chunk, 2, 0), jnp.moveaxis(n_chunk, 2, 0), jnp.moveaxis(m_chunk, 2, 0),
          jnp.moveaxis(b_last, 2, 0), jnp.moveaxis(qc, 2, 0))
    _, (num_inter, den_inter, m_prev) = lax.scan(step, init, xs)
    num_inter = jnp.moveaxis(num_inter, 0, 2)
    den_inter = jnp.moveaxis(den_inter, 0, 2)
    m_prev = jnp.moveaxis(m_prev, 0, 2)

    mask = jnp.tril(jnp.ones((CHUNK, CHUNK), dtype=bool))
    log_d = jnp.where(mask, b[..., :, None] - b[..., None, :] + log_i[..., None, :], -jnp.inf)
    log_inter = b + m_prev[..., None]
    m_t = jnp.maximum(jnp.max(log_d, axis=-1), log_inter)
    d = jnp.exp(log_d - m_t[..., None])
    inter_scale = jnp.exp(log_inter - m_t)
    scores = jnp.einsum('bhcld,bhcsd->bhcls', qc, kc) * d
    num = jnp.einsum('bhcls,bhcsd->bhcld', scores, vc) + inter_scale[..., None] * num_inter
    den = jnp.sum(scores, axis=-1) + inter_scale * den_inter
    h = num / jnp.maximum(jnp.abs(den), jnp.exp(-m_t))[..., None]
    return h.reshape(B, H, S, Dh)

def hybrid_layer(x, norm_pre_g, w_in, conv_qk_w, conv_qk_b, b_igate, b_fgate, pool_mix_w,
                 pool_scale, mlstm_norm_g, w_proj_pool, w_proj_mlstm, b_merge, w_out, norm_post_g):
    B, S, _ = x.shape
    h = rms_norm(x, norm_pre_g)
    proj = jnp.einsum('bsd,de->bse', h, w_in.astype(h.dtype))
    split_points = [int(p) for p in np.cumsum(SPLIT_SIZES)[:-1]]
    u_a, z_a, q, k, v, o, z_b, gates, g_a, g_b = jnp.split(proj, split_points, axis=-1)

    pooled = multiscale_pool(u_a)
    mixed = jnp.einsum('bsgc,gcd->bsgd', pooled.reshape(B, S, POOL_GROUPS, POOL_GROUP_DIM),
                       pool_mix_w.astype(jnp.float32)).reshape(B, S, D_POOL)
    y_a = (mixed * pool_scale.astype(jnp.float32)).astype(x.dtype) * jax.nn.silu(z_a)

    qk = jax.nn.silu(centred_depthwise_conv(jnp.concatenate([q, k], axis=-1), conv_qk_w, conv_qk_b))
    q, k = jnp.split(qk, 2, axis=-1)

    def to_heads(t):
        return t.astype(jnp.float32).reshape(B, S, MLSTM_HEADS, HEAD_DIM).transpose(0, 2, 1, 3)

    qh, kh, vh = to_heads(q), to_heads(k), to_heads(v)
    gates = gates.astype(jnp.float32).reshape(B, S, N_DIRS, 2, MLSTM_HEADS)
    i_pre = (gates[:, :, :, 0, :] + b_igate.astype(jnp.float32)).transpose(2, 0, 3, 1)
    f_pre = (gates[:, :, :, 1, :] + b_fgate.astype(jnp.float32)).transpose(2, 0, 3, 1)
    h_fwd = mlstm_direction(qh, kh, vh, i_pre[0], f_pre[0])
    flip = lambda t: jnp.flip(t, axis=2)
    h_bwd = flip(mlstm_direction(flip(qh), flip(kh), flip(vh), flip(i_pre[1]), flip(f_pre[1])))
    hb = h_fwd + h_bwd
    hb = hb * lax.rsqrt(jnp.mean(hb * hb, axis=-1, keepdims=True) + EPS)
    hb = hb.transpose(0, 2, 1, 3).reshape(B, S, D_MLSTM) * mlstm_norm_g.astype(jnp.float32)
    y_b = hb.astype(x.dtype) * jax.nn.sigmoid(o) * jax.nn.silu(z_b)

    p_a = jnp.einsum('bsc,cd->bsd', y_a, w_proj_pool.astype(y_a.dtype))
    p_b = jnp.einsum('bsc,cd->bsd', y_b, w_proj_mlstm.astype(y_b.dtype))
    merged = jax.nn.sigmoid(g_a + b_merge[0]) * p_a + jax.nn.sigmoid(g_b + b_merge[1]) * p_b
    out = jnp.einsum('bsd,de->bse', merged, w_out.astype(merged.dtype))
    return x + rms_norm(out, norm_post_g)

def second_inputs(seed: int = 0) -> dict:
    key = jax.random.key(seed)
    ks = jax.random.split(key, 16)
    n = jax.random.normal
    f32 = jnp.float32
    x = n(ks[0], (BATCH, SEQ, D_MODEL), f32)
    norm_pre_g = 1.0 + 0.1 * n(ks[1], (DEPTH, D_MODEL), f32)
    w_in = n(ks[2], (DEPTH, D_MODEL, D_IN), f32) * D_MODEL ** -0.5
    conv_qk_w = n(ks[3], (DEPTH, CONV_WIDTH, 2 * D_MLSTM), f32) * CONV_WIDTH ** -0.5
    conv_qk_b = 0.02 * n(ks[4], (DEPTH, 2 * D_MLSTM), f32)
    b_igate = 0.1 * n(ks[5], (DEPTH, N_DIRS, MLSTM_HEADS), f32)
    b_fgate = jnp.linspace(3.0, 6.0, MLSTM_HEADS, dtype=f32)[None, None, :] + 0.1 * n(ks[6], (DEPTH, N_DIRS, MLSTM_HEADS), f32)
    pool_mix_w = n(ks[7], (DEPTH, POOL_GROUPS, POOL_GROUP_DIM, POOL_GROUP_DIM), f32) * POOL_GROUP_DIM ** -0.5
    pool_scale = 1.0 + 0.1 * n(ks[8], (DEPTH, D_POOL), f32)
    mlstm_norm_g = 1.0 + 0.1 * n(ks[9], (DEPTH, D_MLSTM), f32)
    w_proj_pool = n(ks[10], (DEPTH, D_POOL, D_MODEL), f32) * D_POOL ** -0.5
    w_proj_mlstm = n(ks[11], (DEPTH, D_MLSTM, D_MODEL), f32) * D_MLSTM ** -0.5
    b_merge = 0.1 * n(ks[12], (DEPTH, N_BRANCHES, D_MODEL), f32)
    w_out = n(ks[13], (DEPTH, D_MODEL, D_MODEL), f32) * D_MODEL ** -0.5
    norm_post_g = 1.0 + 0.1 * n(ks[14], (DEPTH, D_MODEL), f32)
    return {"x": x, "norm_pre_g": norm_pre_g, "w_in": w_in, "conv_qk_w": conv_qk_w,
            "conv_qk_b": conv_qk_b, "b_igate": b_igate, "b_fgate": b_fgate,
            "pool_mix_w": pool_mix_w, "pool_scale": pool_scale, "mlstm_norm_g": mlstm_norm_g,
            "w_proj_pool": w_proj_pool, "w_proj_mlstm": w_proj_mlstm, "b_merge": b_merge,
            "w_out": w_out, "norm_post_g": norm_post_g}

def second_block(x, norm_pre_g, w_in, conv_qk_w, conv_qk_b, b_igate, b_fgate, pool_mix_w, pool_scale,
              mlstm_norm_g, w_proj_pool, w_proj_mlstm, b_merge, w_out, norm_post_g):
    for l in range(DEPTH):
        x = hybrid_layer(x, norm_pre_g[l], w_in[l], conv_qk_w[l], conv_qk_b[l], b_igate[l], b_fgate[l],
                         pool_mix_w[l], pool_scale[l], mlstm_norm_g[l], w_proj_pool[l], w_proj_mlstm[l],
                         b_merge[l], w_out[l], norm_post_g[l])
    return x


def setup_inputs(seed=0):
    out = dict(first_inputs(seed))
    for name, value in second_inputs(seed + 1).items():
        if name != "x":
            out[name + "_2"] = value
    return out


def reference(
    x, ffn1_norm, ffn1_w_gate, ffn1_w_up, ffn1_w_down, mix_norm, w_in, nsa_pe_k, nsa_w1_k,
    nsa_w2_k, nsa_pe_v, nsa_w1_v, nsa_w2_v, gla_w_a2, gla_b_a, gla_norm, w_out, ffn2_norm,
    ffn2_w_gate, ffn2_w_up, ffn2_w_down, final_norm, norm_pre_g_2, w_in_2, conv_qk_w_2,
    conv_qk_b_2, b_igate_2, b_fgate_2, pool_mix_w_2, pool_scale_2, mlstm_norm_g_2,
    w_proj_pool_2, w_proj_mlstm_2, b_merge_2, w_out_2, norm_post_g_2,
):
    x = first_block(
        x, ffn1_norm, ffn1_w_gate, ffn1_w_up, ffn1_w_down, mix_norm, w_in, nsa_pe_k, nsa_w1_k,
        nsa_w2_k, nsa_pe_v, nsa_w1_v, nsa_w2_v, gla_w_a2, gla_b_a, gla_norm, w_out, ffn2_norm,
        ffn2_w_gate, ffn2_w_up, ffn2_w_down, final_norm,
    )
    return second_block(
        x, norm_pre_g_2, w_in_2, conv_qk_w_2, conv_qk_b_2, b_igate_2, b_fgate_2, pool_mix_w_2,
        pool_scale_2, mlstm_norm_g_2, w_proj_pool_2, w_proj_mlstm_2, b_merge_2, w_out_2,
        norm_post_g_2,
    )


_drawn_inputs = setup_inputs


def setup_inputs(seed=0):
    import zlib

    import numpy as np

    out = dict(_drawn_inputs(seed))
    spreads = {}
    factors = {'ffn1_norm': 3.915,
     'nsa_pe_k': 64.0,
     'nsa_pe_v': 32.961,
     'gla_norm': 21.793,
     'ffn2_norm': 5.996,
     'conv_qk_b_2': 8.0,
     'b_igate_2': 51.494,
     'nsa_w1_k': 5.354,
     'nsa_w2_k': 5.082}
    for name, (base, spread) in spreads.items():
        noise = np.random.default_rng([zlib.crc32(name.encode()), seed]).standard_normal(out[name].shape)
        drawn = base * np.exp(spread * noise) if base else spread * noise
        out[name] = __import__('jax').numpy.asarray(drawn.astype(out[name].dtype))
    for name, factor in factors.items():
        out[name] = (out[name] * factor).astype(out[name].dtype)
    return out
```

```python
from contextlib import ExitStack

import concourse.bass as bass
import numpy as np
from concourse import mybir

F32 = mybir.dt.float32
F32R = mybir.dt.float32r
I32 = mybir.dt.int32
ALU = mybir.AluOpType
ACT = mybir.ActivationFunctionType
AX = mybir.AxisListType

P = 128
T = 512
D = 1024
DC = D // P
TT = T // P
FF = 2816
FT = FF // P
EPS = 1e-6
NEG = -1e30

NH, NG, DH = 8, 2, 64
HPG = NH // NG
CMP_BLOCK, CMP_STRIDE, CMP_HID = 32, 16, 128
NCMP = (T - CMP_BLOCK) // CMP_STRIDE + 1
GH, GDK, GDV, GC = 4, 64, 128, 64
LOWR = 16
MH, MD, MC = 4, 256, 128
NCH = T // MC
POOL_W = (2, 4, 8, 16)
CONV = 5

MT_Q, MT_GQ, MT_KC, MT_VC, MT_KS, MT_VS, MT_KW, MT_VW = 0, 4, 6, 7, 8, 9, 10, 11
MT_GK, MT_GV, MT_GR, MT_GATE = 12, 14, 18, 22
MTILES = 23

FFN_UNITS = 2 * FT + FT
U_FFN1 = 0
U_PROJ = U_FFN1 + FFN_UNITS
U_MIXOUT = U_PROJ + MTILES
U_FFN2 = U_MIXOUT + DC
U_GATES = U_FFN2 + FFN_UNITS
HEAD_UNITS = 10
U_HEADS = U_GATES + 1
U_PB = U_HEADS + MH * HEAD_UNITS
U_POOL = U_PB + 2 * DC
U_MIX2 = U_POOL + 2 * DC
U_PA = U_MIX2 + 2
U_OUT = U_PA + 2 * DC
NUNITS = U_OUT + DC

CONSTS = {}
_at = 0
for _name, _width in (("ident", P), ("ones", P), ("eps", 1), ("one", 1), ("zero", 1), ("dist", T), ("keep", T),
                      ("gmask", P), ("cvalid", TT * NCMP), ("slope", NH), ("upper", P), ("lower", P),
                      ):
    CONSTS[_name] = (_at, _width)
    _at += _width
CONST_COLS = _at

PARAMS = {}
_at = 0
for _name, _width in (("g_ffn1", DC), ("g_mix", DC), ("g_ffn2", DC), ("g_final", DC), ("g_pre", DC),
                      ("g_post", DC), ("b_a", 2), ("g_gla", 1), ("pool_scale", DC), ("conv_w", 16 * CONV),
                      ("conv_b", 16), ("g_mlstm", DC), ("b_merge", 2 * DC), ("b_if", 1), ("pe", 32),
                      ("w2", 2 * DH), ("w_a2", GH * GDK)):
    PARAMS[_name] = (_at, _width)
    _at += _width
PARAM_COLS = _at


class Chain:

    def __init__(self, engine, sem):
        self.engine, self.sem, self.n, self.offset = engine, sem, 0, 0

    def link(self, instruction):
        self.n += 1
        instruction.then_inc(self.sem, 1)
        self.engine.wait_ge(self.sem, self.n + self.offset)

    def enter(self, i, per):
        self.offset, self.per, self.first = i * per, per, self.n

    def leave(self, count):
        assert self.n - self.first == self.per, (self.n - self.first, self.per)
        self.n, self.offset = self.first + count * self.per, 0


def build(nc, dram, out):
    with ExitStack() as ctx:
        def sb(name, shape, dt=F32, scope=ctx):
            return scope.enter_context(nc.sbuf_tensor(name, shape, dt))

        def sem(name):
            return ctx.enter_context(nc.semaphore(name))

        ps = ctx.enter_context(nc.psum_tensor("ps", [P, 8, T], F32))
        x = sb("x", [P, DC, T])
        h_hi = sb("h_hi", [P, DC, T], F32R)
        h_lo = sb("h_lo", [P, DC, T], F32R)
        w_raw = sb("w_raw", [P, 2, D])
        w_hi = sb("w_hi", [P, 2, D], F32R)
        w_lo = sb("w_lo", [P, 2, D], F32R)
        scr = sb("scr", [P, DC, T])
        rstd = sb("rstd", [P, T])
        const = sb("const", [P, CONST_COLS])
        param = sb("param", [P, PARAM_COLS])

        def c_(name):
            at, width = CONSTS[name]
            return const[:, at:at + width]

        def p_(name, a=0, b=None):
            at, width = PARAMS[name]
            return param[:, at + a:at + (width if b is None else b)]

        ident, ones = c_("ident"), c_("ones")

        ffn = ExitStack()
        hid_hi = sb("hid_hi", [P, FT, T], F32R, ffn)
        hid_lo = sb("hid_lo", [P, FT, T], F32R, ffn)
        silu = sb("silu", [P, 2, T], F32, ffn)
        hid = sb("hid", [P, 2, T], F32, ffn)
        ffn.close()

        mixer = ExitStack()
        proj = sb("proj", [P, MTILES, T], F32, mixer)
        v_tok = sb("v_tok", [P, TT, 2, NG * DH], F32, mixer)
        gate_tok = sb("gate_tok", [P, TT, 3 * NH], F32, mixer)
        nsa = ExitStack()
        w1 = sb("w1", [P, 2, CMP_BLOCK // 2, CMP_HID], F32, nsa)
        cbias = sb("cbias", [P, TT * NH * NCMP], F32, nsa)
        gel = sb("gel", [P, 2, NG * NCMP], F32, nsa)
        kc_t = sb("kc_t", [P, NCMP], F32, nsa)
        vc_tok = sb("vc_tok", [NCMP, NG, DH], F32, nsa)
        c_max = sb("c_max", [P, TT * NH], F32, nsa)
        c_sum = sb("c_sum", [P, TT * NH], F32, nsa)
        pc_t = sb("pc_t", [NCMP, NH, T], F32, nsa)
        pc_st = sb("pc_st", [NCMP, NG, T], F32, nsa)
        q_st = sb("q_st", [P, T], F32, nsa)
        bias = sb("bias", [P, NG, T], F32, nsa)
        nmax = sb("nmax", [P, 2], F32, nsa)
        psum_l = sb("psum_l", [P, 2], F32, nsa)
        nsa.close()
        gla = ExitStack()
        q_in = sb("q_in", [P, 2, T], F32, gla)
        k_in = sb("k_in", [P, 2, T], F32, gla)
        decay = sb("decay", [P, 2, T], F32, gla)
        kst_tok = sb("kst_tok", [P, TT, GH * GDK], F32, gla)
        gv_tok = sb("gv_tok", [P, TT, GH * GDV], F32, gla)
        intra = sb("intra", [P, 2, P], F32, gla)
        state = sb("state", [P, 2, 2, GDV], F32, gla)
        gla.close()
        mixer.close()

        second = ExitStack()
        y_hi = sb("y_hi", [P, DC, T], F32R, second)
        y_lo = sb("y_lo", [P, DC, T], F32R, second)
        heads = ExitStack()
        qk_pad = sb("qk_pad", [P, 2, T + CONV - 1], F32, heads)
        qk = sb("qk", [P, 4, T], F32, heads)
        k_tok = sb("k_tok", [P, NCH, MD], F32, heads)
        v_aug = sb("v_aug", [P, NCH, MD + P], F32, heads)
        d_mat = sb("d_mat", [P, 2, T], F32, heads)
        q_sc = sb("q_sc", [P, 2, 2, T], F32, heads)
        floor = sb("floor", [P, 2, T], F32, heads)
        k_w = sb("k_w", [P, 2, MD], F32, heads)
        c_state = sb("c_state", [P, 2, 2, MD + P], F32, heads)
        h_sum = sb("h_sum", [P, 2, T], F32, heads)
        h_tmp = sb("h_tmp", [P, 2, P], F32, heads)
        den = sb("den", [P, 2, P], F32, heads)
        row_m = sb("row_m", [64, T], F32, heads)
        row_i = sb("row_i", [64, T], F32, heads)
        row_f = sb("row_f", [64, T], F32, heads)
        edge = sb("edge", [64, 5, NCH], F32, heads)
        a_tok = sb("a_tok", [P, NCH, 64], F32, heads)
        wk_tok = sb("wk_tok", [P, NCH, 64], F32, heads)
        keep_bc = sb("keep_bc", [P, 2 * MH * NCH], F32, heads)
        sel = sb("sel", [64, 2, P], F32, heads)
        heads.close()
        merged = sb("merged", [P, DC, T], F32, second)
        gate = sb("gate", [P, 2, T], F32, second)
        pooling = ExitStack()
        silu_z = sb("silu_z", [P, DC, T], F32, pooling)
        inv_count = sb("inv_count", [P, len(POOL_W), T], F32, pooling)
        u_pad = sb("u_pad", [P, 2, T + 16], F32, pooling)
        win = sb("win", [P, 2, T + 16], F32, pooling)
        pooling.close()
        m_hi = sb("m_hi", [P, DC, T], F32R, second)
        m_lo = sb("m_lo", [P, DC, T], F32R, second)
        second.close()

        dup = scr[:, 0:4, :]
        rows = scr[:, 4:8, :].rearrange("p a t -> p (a t)")[:, 0:2 * 16 * NG * NCMP].rearrange(
            "p (s l g n) -> p s l g n", s=2, l=16, g=NG)
        c_score = scr[:, 0:2, :].rearrange("p a t -> p (a t)")[:, 0:TT * NH * NCMP].rearrange(
            "p (q h n) -> p q h n", q=TT, h=NH)

        prob_t, score, prob = scr[:, 2:4, :], scr[:, 4:6, :], scr[:, 6:8, :]

        proj_done = sem("proj_done")
        w1_in = sem("w1_in")
        dup_in = sem("dup_in")
        tok_ready, tok_done = sem("tok_ready"), sem("tok_done")
        gate_done = sem("gate_done")
        rows_done = sem("rows_done")
        cmp_pe = sem("cmp_pe")
        gel_done = sem("gel_done")
        kvc_done = sem("kvc_done")
        cexp_ready, cexp_done, cprob_done = sem("cexp_ready"), sem("cexp_done"), sem("cprob_done")
        pct_done = [sem("pct_done_even"), sem("pct_done_odd")]
        stage_done, bias_done = sem("stage_done"), sem("bias_done")
        score_ready, neg_done, exp_done = sem("score_ready"), sem("neg_done"), sem("exp_done")
        prob_done, turn_ready, prob_t_done = sem("prob_done"), sem("turn_ready"), sem("prob_t_done")
        pv_done = sem("pv_done")
        o_hi_done, o_lo_done = sem("o_hi_done"), sem("o_lo_done")
        z_ready, gln_done, b_done, eb_done = sem("z_ready"), sem("gln_done"), sem("b_done"), sem("eb_done")
        kst_diff, kst_exp, kst_done = sem("kst_diff"), sem("kst_exp"), sem("kst_done")
        kst_turned, gv_turned = sem("kst_turned"), sem("gv_turned")
        kst_copied, gv_copied = sem("kst_copied"), sem("gv_copied")
        a_ready, a_done, a_used = sem("a_ready"), sem("a_done"), sem("a_used")
        add_ready, state_done = sem("add_ready"), sem("state_done")
        gsq_done, gssq_done, grms_done = sem("gsq_done"), sem("gssq_done"), sem("grms_done")
        rl_done = sem("rl_done")
        score_turn = sem("score_turn")
        gr_done, go_done, go_hi, go_lo = sem("gr_done"), sem("go_done"), sem("go_hi"), sem("go_lo")
        raw_full = [sem("raw_full0"), sem("raw_full1")]
        w_hi_done, w_lo_done = sem("w_hi_done"), sem("w_lo_done")
        unit_done = sem("unit_done")
        small_in = sem("small_in")
        x_in = sem("x_in")
        sq_done = sem("sq_done")
        sqsum_done = sem("sqsum_done")
        ssq_done = sem("ssq_done")
        rms_done = sem("rms_done")
        rstd_done = sem("rstd_done")
        hn_done, hn_hi_done, hn_lo_done = sem("hn_done"), sem("hn_hi_done"), sem("hn_lo_done")
        silu_done = sem("silu_done")
        hid_done, hid_hi_done, hid_lo_done = sem("hid_done"), sem("hid_hi_done"), sem("hid_lo_done")
        x_done = sem("x_done")
        dve_chain = sem("dve_chain")
        act_chain = sem("act_chain")
        out_sem = sem("out_sem")

        ITEMS = [(b, qt, g) for b in range(2) for qt in range(TT) for g in range(NG)]
        NI = len(ITEMS)
        HEADS_OF = [(h, h // 2, h % 2) for h in range(GH)]

        x_out = sem("x_out")
        rows_in, g_ready, row_z, row_l = sem("rows_in"), sem("g_ready"), sem("row_z"), sem("row_l")
        row_args, row_exp = sem("row_args"), sem("row_exp")
        edge_done, edge_exp = sem("edge_done"), sem("edge_exp")
        tokrow_ready, tokrow_done = sem("tokrow_ready"), sem("tokrow_done")
        ev_done = sem("ev_done")
        conv_done, qk_done = sem("conv_done"), sem("qk_done")
        kt_ready, kt_done = sem("kt_ready"), sem("kt_done")
        vt_ready, vt_done = sem("vt_ready"), sem("vt_done")
        sel_done = sem("sel_done")
        sc_ready, nm_ready, dlog_done = sem("sc_ready"), sem("nm_ready"), sem("dlog_done")
        dexp_done, sct_done = sem("dexp_done"), sem("sct_done")
        in_ready, qs_done, fl_ready, fl_done = sem("in_ready"), sem("qs_done"), sem("fl_ready"), sem("fl_done")
        kw_done, cadd_ready, c_done = sem("kw_done"), sem("cadd_ready"), sem("c_done")
        num_ready, num_done = sem("num_ready"), sem("num_done")
        hsq_done, hssq_done, hrms_done = sem("hsq_done"), sem("hssq_done"), sem("hrms_done")
        y_done, y_hi_done, y_lo_done = sem("y_done"), sem("y_hi_done"), sem("y_lo_done")
        mg_sig, mg_done = sem("mg_sig"), sem("mg_done")
        inv_in, upad_done, pool_done, sz_done = sem("inv_in"), sem("upad_done"), sem("pool_done"), sem("sz_done")
        m_hi_done, m_lo_done = sem("m_hi_done"), sem("m_lo_done")
        out_done, sum_done = sem("out_done"), sem("sum_done")
        STEPS = [(s, d) for s in range(NCH) for d in range(2)]

        FIRST_OF = [n for n, (s, d) in enumerate(STEPS) if s < NCH // 2]
        MLSTM_LINKS = 4 * (CONV - 1) + 3 * len(STEPS) + len(STEPS) // 2 + 1 + 4

        def chunk_of(s, d):
            return s if d == 0 else NCH - 1 - s

        block = ctx.enter_context(nc.Block())

        def unit(c, per=0, i=0):
            assert per % 2 == 0
            return c + per * i, c // 2 + per // 2 * i, c % 2

        @block.sync
        def _(sp):
            for n, (dst, src) in enumerate(((const, "const"), (param, "param"))):
                sp.dma_start(dst[:, :], dram[src]).then_inc(small_in, 16)
            for c in range(DC):
                sp.dma_start(x[:, c, :], dram["x"][c * P:(c + 1) * P, :]).then_inc(x_in, 16)
            for u in range(2):
                sp.dma_start(w_raw[:, u, :], dram["units"][u]).then_inc(raw_full[u], 16)
            with sp.Fori(1, (NUNITS + 1) // 2) as i:
                for slot in range(2):
                    sp.wait_ge(w_lo_done, 2 * i + slot - 1)
                    sp.dma_start(w_raw[:, slot, :],
                                 dram["units"][bass.ds(2 * i + slot, 1)].rearrange("u p n -> p (u n)")
                                 ).then_inc(raw_full[slot], 16)
            for c in range(DC):
                sp.wait_ge(x_out, c + 1)
                sp.dma_start(out[c * P:(c + 1) * P, :], x[:, c, :]).then_inc(out_sem, 16)
            sp.wait_ge(out_sem, 16 * DC)

        @block.gpsimd
        def _(pool):
            with pool.Fori(0, NUNITS // 2) as i:
                for slot in range(2):
                    pool.wait_ge(w_hi_done, 2 * i + slot + 1)
                    nc.gpsimd.tensor_tensor(w_lo[:, slot, :], w_raw[:, slot, :], w_hi[:, slot, :].bitcast(F32),
                                            ALU.subtract).then_inc(w_lo_done, 1)

        @block.tensor
        def _(pe):
            def tile_unit(un, bank, hi, lo, chunks=None):
                u, _, slot = un
                pe.wait_ge(w_lo_done, u + 1)
                for k in range(DC):
                    if chunks is not None:
                        pe.wait_ge(*chunks(k))
                    whi, wlo = w_hi[:, slot, k * P:(k + 1) * P], w_lo[:, slot, k * P:(k + 1) * P]
                    nc.tensor.matmul(ps[:, bank, :], whi, hi[:, k, :], start=(k == 0), stop=False)
                    nc.tensor.matmul(ps[:, bank, :], whi, lo[:, k, :], start=False, stop=False)
                    mm = nc.tensor.matmul(ps[:, bank, :], wlo, hi[:, k, :], start=False, stop=(k == DC - 1))
                mm.then_inc(unit_done, 1)

            def norm(n):
                pe.wait_ge(sqsum_done, n + 1)
                nc.tensor.matmul(ps[:, 0, :], ones, scr[:, 0, :], start=True, stop=False)
                for c in range(DC // 2, DC):
                    pe.wait_ge(sq_done, DC * n + c + 1)
                    mm = nc.tensor.matmul(ps[:, 0, :], ones, scr[:, c, :], start=False, stop=(c == DC - 1))
                mm.then_inc(ssq_done, 1)

            def ffn(u0, n, norm_of):
                def pair(i, chunks=None):
                    for f in range(2):
                        pe.wait_ge(hid_done, FT * n + 2 * i + f + 1)
                        for m in range(2):
                            tile_unit(unit(u0 + 2 * f + m, 4, i), 4 + 2 * f + m, h_hi, h_lo,
                                      chunks if f == m == 0 else None)

                pair(0, lambda k: (hn_lo_done, DC * norm_of + k + 1))
                with pe.Fori(1, FT // 2) as i:
                    pair(i)

                def down(un, kp, half, start=False, stop=False):
                    u, _, slot = un
                    pe.wait_ge(w_lo_done, u + 1)
                    for kk in range(2):
                        mv_hi = hid_hi[:, bass.ds(2 * kp + kk, 1), :].rearrange("p a t -> p (a t)")
                        mv_lo = hid_lo[:, bass.ds(2 * kp + kk, 1), :].rearrange("p a t -> p (a t)")
                        for dd in range(4):
                            at = (kk * 4 + dd) * P
                            acc = ps[:, half * 4 + dd, :]
                            nc.tensor.matmul(acc, w_hi[:, slot, at:at + P], mv_hi, start=start and kk == 0, stop=False)
                            nc.tensor.matmul(acc, w_hi[:, slot, at:at + P], mv_lo, start=False, stop=False)
                            mm = nc.tensor.matmul(acc, w_lo[:, slot, at:at + P], mv_hi, start=False,
                                                  stop=stop and kk == 1)
                    mm.then_inc(unit_done, 1)

                ud = u0 + 2 * FT
                kps = FT // 2
                pe.wait_ge(hid_lo_done, FT * (n + 1) - 2)
                for j in range(2):
                    down(unit(ud + j), j, 0, start=(j == 0))
                with pe.Fori(1, kps // 2) as i:
                    for j in range(2):
                        down(unit(ud + j, 2, i), 2 * i + j, 0)
                pe.wait_ge(hid_lo_done, FT * (n + 1))
                down(unit(ud + kps - 1), kps - 1, 0, stop=True)
                down(unit(ud + kps), 0, 1, start=True)
                with pe.Fori(0, kps // 2 - 1) as i:
                    for j in range(2):
                        down(unit(ud + kps + 1 + j, 2, i), 2 * i + j + 1, 1)
                for j in range(2):
                    down(unit(ud + 2 * kps - 2 + j), kps - 2 + j, 1, stop=(j == 1))

            def project():
                def two(i, chunks=None):
                    for j in range(2):
                        pe.wait_ge(proj_done, 2 * i + j + 1)
                        tile_unit(unit(U_PROJ + j, 2, i), 2 + j, h_hi, h_lo, chunks if j == 0 else None)

                two(0, lambda k: (hn_lo_done, DC + k + 1))
                with pe.Fori(1, MTILES // 2) as i:
                    two(i)
                pe.wait_ge(proj_done, MTILES)
                tile_unit(unit(U_PROJ + MTILES - 1), 2, h_hi, h_lo)

            def compressed():
                pe.wait_ge(proj_done, 2 + MTILES)
                for tt in range(TT):
                    at = slice(tt * P, (tt + 1) * P)
                    nc.tensor.transpose(ps[:, 4, tt * 3 * NH:(tt + 1) * 3 * NH], proj[0:3 * NH, MT_GATE, at],
                                        ident[0:3 * NH, 0:3 * NH])
                    nc.tensor.transpose(ps[:, 5, at], proj[:, MT_VS, at], ident)
                    mm = nc.tensor.transpose(ps[:, 6, at], proj[:, MT_VW, at], ident)
                mm.then_inc(tok_ready, 1)
                pe.wait_ge(w1_in, 32)
                for s in range(2):
                    for lp in range(CMP_BLOCK // 2):
                        if lp == 0:
                            pe.wait_ge(rows_done, s + 1)
                        mm = nc.tensor.matmul(ps[:, 7 - 4 * s, 0:NG * NCMP], w1[:, s, lp, :],
                                              rows[:, s, lp, :, :].rearrange("p g n -> p (g n)"),
                                              start=(lp == 0), stop=(lp == CMP_BLOCK // 2 - 1))
                    mm.then_inc(cmp_pe, 1)
                pe.wait_ge(gel_done, 1)
                for g in range(NG):
                    at = slice(g * NCMP, (g + 1) * NCMP)
                    nc.tensor.matmul(ps[g * DH:(g + 1) * DH, 0, 0:NCMP], p_("w2", 0, DH), gel[:, 0, at],
                                     start=True, stop=True)
                pe.wait_ge(gel_done, 2)
                for g in range(NG):
                    at = slice(g * NCMP, (g + 1) * NCMP)
                    mm = nc.tensor.matmul(ps[0:NCMP, 1, g * DH:(g + 1) * DH], gel[:, 1, at], p_("w2", DH, 2 * DH),
                                          start=True, stop=True)
                mm.then_inc(cmp_pe, 1)
                pe.wait_ge(kvc_done, 1)
                for qt in range(TT):
                    for h in range(NH):
                        g, j = h // HPG, h % HPG
                        r = slice(g * DH, (g + 1) * DH)
                        at = (qt * HPG + j) * 32
                        mm = nc.tensor.matmul(ps[:, 2 + g, at:at + NCMP], proj[r, MT_Q + j, qt * P:(qt + 1) * P],
                                              kc_t[r, :], start=True, stop=True)
                mm.then_inc(cmp_pe, 1)
                pe.wait_ge(cprob_done, 1)
                pe.wait_ge(tok_done, 3)
                for h in range(NH):
                    if h >= 4:
                        pe.wait_ge(pct_done[h % 2], h // 2 - 1)
                    for qt in range(TT):
                        mm = nc.tensor.transpose(ps[0:NCMP, 4 + h % 4, qt * P:(qt + 1) * P], c_score[:, qt, h, :], ident)
                    mm.then_inc(cmp_pe, 1)

            def attention():
                with pe.Fori(0, HPG) as j:
                    def scores(n):
                        b, qt, g = ITEMS[n]
                        r, w = slice(g * DH, (g + 1) * DH), (qt + 1) * P
                        if n >= 2:
                            pe.wait_ge(neg_done, NI * j + n - 1)
                        mm = nc.tensor.matmul(ps[:, n % 2, 0:w], q_st[r, qt * P:(qt + 1) * P],
                                              proj[r, (MT_KS, MT_KW)[b], 0:w], start=True, stop=True)
                        mm.then_inc(score_ready, 1)

                    def turn(n):
                        b, qt, g = ITEMS[n]
                        pe.wait_ge(prob_done, NI * j + n + 1)
                        if n >= 2:
                            pe.wait_ge(prob_t_done, NI * j + n - 1)
                        for kt in range(qt + 1):
                            at = slice(kt * P, (kt + 1) * P)
                            mm = nc.tensor.transpose(ps[:, 2 + n % 2, at], prob[:, n % 2, at], ident)
                        mm.then_inc(turn_ready, 1)

                    def values(n):
                        b, qt, g = ITEMS[n]
                        pe.wait_ge(prob_t_done, NI * j + n + 1)
                        for kt in range(qt + 1):
                            mm = nc.tensor.matmul(ps[g * DH:(g + 1) * DH, 4, qt * P:(qt + 1) * P],
                                                  v_tok[:, kt, b, g * DH:(g + 1) * DH],
                                                  prob_t[:, n % 2, kt * P:(kt + 1) * P],
                                                  start=False, stop=False, skip_group_check=True)
                        mm.then_inc(pv_done, 1)

                    pe.wait_ge(stage_done, j + 1)
                    scores(0)
                    scores(1)
                    pe.wait_ge(o_lo_done, j + 1)
                    for g in range(NG):
                        nc.tensor.matmul(ps[g * DH:(g + 1) * DH, 4, :], vc_tok[:, g, :], pc_st[:, g, :],
                                         start=True, stop=False, skip_group_check=True)
                    for n in range(NI):
                        turn(n)
                        if n + 2 < NI:
                            scores(n + 2)
                        if n >= 1:
                            values(n - 1)
                    values(NI - 1)

            def linear():
                pe.wait_ge(o_lo_done, HPG + 1)
                r = slice(32, 32 + LOWR)
                for m in range(2):
                    nc.tensor.matmul(ps[:, 6 + m, :], p_("w_a2", m * P, (m + 1) * P)[r], proj[r, MT_GATE, :],
                                     start=True, stop=True).then_inc(z_ready, 1)
                for h in range(GH):
                    for tt in range(TT):
                        at = slice(tt * P, (tt + 1) * P)
                        mm = nc.tensor.transpose(ps[:, h, at], proj[:, MT_GV + h, at], ident)
                    mm.then_inc(gv_turned, 1)
                for m in range(2):
                    pe.wait_ge(kst_done, m + 1)
                    for tt in range(TT):
                        at = slice(tt * P, (tt + 1) * P)
                        mm = nc.tensor.transpose(ps[:, 4 + m, at], scr[:, 4 * m, at], ident)
                    mm.then_inc(kst_turned, 1)
                pe.wait_ge(gv_copied, GH)
                pe.wait_ge(kst_copied, 2)
                for tt in range(TT):
                    tok = slice(tt * P, (tt + 1) * P)
                    for h, m, half in HEADS_OF:
                        n = tt * GH + h
                        r = slice(half * GDK, (half + 1) * GDK)
                        if n >= 2:
                            pe.wait_ge(a_done, n - 1)
                        nc.tensor.matmul(ps[:, n % 2, 0:P], k_in[r, m, tok], q_in[r, m, tok],
                                         start=True, stop=True).then_inc(a_ready, 1)
                        if h >= 1:
                            gla_intra(tt, h - 1)
                    gla_intra(tt, GH - 1)
                    for c in range(2):
                        n = 2 * tt + c
                        if n < T // GC - 1:
                            if n >= 2:
                                pe.wait_ge(state_done, n - 1)
                            ck = slice(c * GC, (c + 1) * GC)
                            for h, m, half in HEADS_OF:
                                r = slice(half * GDK, (half + 1) * GDK)
                                mm = nc.tensor.matmul(ps[r, 2 + n % 2, m * GDV:(m + 1) * GDV],
                                                      kst_tok[ck, tt, m * P + half * GDK:m * P + (half + 1) * GDK],
                                                      gv_tok[ck, tt, h * GDV:(h + 1) * GDV], start=True, stop=True)
                            mm.then_inc(add_ready, 1)
                        if n >= 1:
                            pe.wait_ge(state_done, n)
                            for h, m, half in HEADS_OF:
                                r = slice(half * GDK, (half + 1) * GDK)
                                at = slice(n * GC, (n + 1) * GC)
                                mm = nc.tensor.matmul(ps[:, 4 + h, at], state[r, m, n % 2, :], q_in[r, m, at],
                                                      start=False, stop=False, skip_group_check=True)
                            mm.then_inc(a_used, 1)
                for h in range(GH):
                    pe.wait_ge(gsq_done, h + 1)
                    if h >= 2:
                        pe.wait_ge(grms_done, h - 1)
                    nc.tensor.matmul(ps[:, h % 2, :], ones, scr[:, h, :], start=True, stop=True
                                     ).then_inc(gssq_done, 1)

            def gla_intra(tt, h):
                n = tt * GH + h
                pe.wait_ge(a_done, n + 1)
                nc.tensor.matmul(ps[:, 4 + h, tt * P:(tt + 1) * P], gv_tok[:, tt, h * GDV:(h + 1) * GDV],
                                 intra[:, n % 2, :], start=(tt == 0), stop=False, skip_group_check=True
                                 ).then_inc(pv_done, 1)

            def to_stream(u0, n, hi, lo, ready):
                def two(i, chunks=None):
                    for j in range(2):
                        pe.wait_ge(x_done, DC * n + 2 * i + j - 1)
                        tile_unit(unit(u0 + j, 2, i), 2 + j, hi, lo, chunks if j == 0 else None)

                two(0, ready)
                with pe.Fori(1, DC // 2) as i:
                    two(i)

            def gates():
                pe.wait_ge(ssq_done, 5)
                tile_unit(unit(U_GATES), 4, h_hi, h_lo, lambda k: (hn_lo_done, 3 * DC + k + 1))
                pe.wait_ge(row_args, 1)
                pe.wait_ge(row_exp, 1)
                for n, (src, bank) in enumerate(((scr[0:64, 3, :], 5), (scr[0:64, 2, :], 6))):
                    for c in range(NCH):
                        mm = nc.tensor.transpose(ps[:, bank, c * 64:(c + 1) * 64], src[:, c * MC:(c + 1) * MC],
                                                 ident[0:64, 0:64])
                    mm.then_inc(tokrow_ready, 1)
                pe.wait_ge(edge_exp, 1)
                for d in range(2):
                    for h in range(MH):
                        r, at = 32 * d + h, (d * MH + h) * NCH
                        mm = nc.tensor.matmul(ps[:, 7, at:at + NCH], ident[0:64, r:r + 1].to_broadcast([64, P]),
                                              edge[:, 4, :], start=True, stop=True)
                mm.then_inc(tokrow_ready, 1)

            def mlstm_head(h):
                for j in range(HEAD_UNITS):
                    pe.wait_ge(ev_done, HEAD_UNITS * h + j + 1)
                    tile_unit(unit(U_HEADS + j, HEAD_UNITS, h), j % 2, h_hi, h_lo)
                for e in range(2):
                    pe.wait_ge(qk_done, 4 * h + 3 + e)
                    for c in range(NCH):
                        at = slice(c * MC, (c + 1) * MC)
                        mm = nc.tensor.transpose(ps[:, 2 + e, at], qk[:, 2 + e, at], ident)
                    mm.then_inc(kt_ready, 1)
                for e in range(2):
                    for c in range(NCH):
                        at = slice(c * MC, (c + 1) * MC)
                        mm = nc.tensor.transpose(ps[:, 4 + e, at], scr[:, e, at], ident)
                    mm.then_inc(vt_ready, 1)
                for c in range(NCH):
                    at = slice(c * MC, (c + 1) * MC)
                    for e in range(2):
                        mm = nc.tensor.matmul(ps[:, 6, at], qk[:, 2 + e, at], qk[:, e, at],
                                              start=(c == 0 and e == 0), stop=False, skip_group_check=True)
                mm.then_inc(sc_ready, 1)
                pe.wait_ge(kt_done, 2 * h + 2)
                for d in range(2):
                    pe.wait_ge(sel_done, h + 1)
                    if d:
                        pe.wait_ge(dlog_done, 2 * h + 1)
                    nc.tensor.matmul(ps[:, 7, :], sel[:, d, :], row_m[:, :], start=True, stop=True).then_inc(nm_ready, 1)
                    if d:
                        pe.wait_ge(qs_done, 2 * h + 1)
                    nc.tensor.matmul(ps[:, 2, :], sel[:, d, :], row_i[:, :], start=True, stop=True).then_inc(in_ready, 1)
                    if d:
                        pe.wait_ge(fl_done, 2 * h + 1)
                    nc.tensor.matmul(ps[:, 3, :], sel[:, d, :], row_f[:, :], start=True, stop=True).then_inc(fl_ready, 1)
                pe.wait_ge(vt_done, 2 * h + 2)
                pe.wait_ge(sct_done, 2 * h + 2)
                for n, (s, d) in enumerate(STEPS):
                    c = chunk_of(s, d)
                    if s < NCH - 1:
                        pe.wait_ge(kw_done, 6 * h + n + 1)
                        if n:
                            pe.wait_ge(c_done, 6 * h + n)
                        for e in range(2):
                            mm = nc.tensor.matmul(ps[:, 4 + e, 0:MD + P], k_w[:, d, e * P:(e + 1) * P], v_aug[:, c, :],
                                                  start=True, stop=True)
                        mm.then_inc(cadd_ready, 1)
                    if s == 0:
                        pe.wait_ge(qs_done, 2 * h + d + 1)
                    if n >= 2:
                        pe.wait_ge(num_done, 8 * h + n - 1)
                    at = slice(c * MC, (c + 1) * MC)
                    for e in range(3):
                        o = ps[:, 6 + d, e * P:(e + 1) * P]
                        mm = nc.tensor.matmul(o, v_aug[:, c, e * P:(e + 1) * P], d_mat[:, d, at], start=(e == 0),
                                              stop=False, skip_group_check=True)
                        for f in range(2 if s else 0):
                            mm = nc.tensor.matmul(o, c_state[:, d, f, e * P:(e + 1) * P], q_sc[:, d, f, at],
                                                  start=False, stop=False, skip_group_check=True)
                    mm.then_inc(num_ready, 1)
                for e in range(2):
                    pe.wait_ge(hsq_done, 2 * h + e + 1)
                    mm = nc.tensor.matmul(ps[:, 3, :], ones, d_mat[:, e, :], start=(e == 0), stop=(e == 1))
                mm.then_inc(hssq_done, 1)

            def merge(u0, done):
                with pe.Fori(0, DC // 2) as i:
                    for j in range(2):
                        pe.wait_ge(mg_done, done + 2 * i + j + 1)
                        tile_unit(unit(u0 + 2 * j, 4, i), 4 + 2 * j, h_hi, h_lo)
                        pe.wait_ge(y_lo_done, 3 * DC if done else DC)
                        tile_unit(unit(u0 + 2 * j + 1, 4, i), 5 + 2 * j, y_hi, y_lo)

            def pooled():
                with pe.Fori(0, DC) as i:
                    for j in range(2):
                        pe.wait_ge(ev_done, HEAD_UNITS * MH + 2 * i + j + 1)
                        tile_unit(unit(U_POOL + j, 2, i), 2 + j, h_hi, h_lo)
                pe.wait_ge(mg_done, DC + 2)
                pe.wait_ge(ev_done, HEAD_UNITS * MH + 2 * DC + 2)
                pe.wait_ge(y_lo_done, 2 * DC)
                for n in range(2):
                    u, _, slot = unit(U_MIX2 + n)
                    pe.wait_ge(w_lo_done, u + 1)
                    for g in range(2):
                        for dt in range(2):
                            for ck in range(2):
                                at = (g * 4 + dt * 2 + ck) * P
                                src, acc = (2 * n + g) * 2 + ck, ps[:, 4 - 4 * n + 2 * g + dt, :]
                                whi, wlo = w_hi[:, slot, at:at + P], w_lo[:, slot, at:at + P]
                                nc.tensor.matmul(acc, whi, y_hi[:, src, :], start=(ck == 0), stop=False)
                                nc.tensor.matmul(acc, whi, y_lo[:, src, :], start=False, stop=False)
                                mm = nc.tensor.matmul(acc, wlo, y_hi[:, src, :], start=False, stop=(ck == 1))
                    mm.then_inc(unit_done, 1)
                pe.wait_ge(y_done, DC + 4)

            def output():
                pe.wait_ge(mg_done, 2 * DC + 2)
                def two(i, chunks=None):
                    for j in range(2):
                        pe.wait_ge(out_done, 2 * i + j + 1)
                        tile_unit(unit(U_OUT + j, 2, i), 2 + j, m_hi, m_lo, chunks if j == 0 else None)

                two(0, lambda k: (m_lo_done, k + 1))
                with pe.Fori(1, DC // 2) as i:
                    two(i)
                norm(5)

            pe.wait_ge(small_in, 32)
            norm(0)
            ffn(U_FFN1, 0, 0)
            norm(1)
            project()
            compressed()
            attention()
            linear()
            to_stream(U_MIXOUT, 2, h_hi, h_lo, lambda k: (o_lo_done, 5) if k < 4 else (go_lo, k - 3))
            norm(2)
            ffn(U_FFN2, 1, 2)
            norm(3)
            norm(4)
            gates()
            with pe.Fori(0, MH) as h:
                mlstm_head(h)
            merge(U_PB, 0)
            pooled()
            merge(U_PA, DC)
            output()

        @block.scalar
        def _(act):
            def head(un):
                u, turn, slot = un
                act.wait_ge(raw_full[slot], 16 * (turn + 1))
                act.wait_ge(unit_done, u - 1)
                nc.scalar.activation(w_hi[:, slot, :], w_raw[:, slot, :], ACT.Copy).then_inc(w_hi_done, 1)

            def squares(n, lo, hi):
                for c in range(lo, hi):
                    if n:
                        act.wait_ge(x_done, DC * n + c + 1)
                    nc.scalar.activation(scr[:, c, :], x[:, c, :], ACT.Square).then_inc(sq_done, 1)

            def norm(n, parts=True, at=None):
                at = n if at is None else at
                act.wait_ge(ssq_done, n + 1)
                nc.scalar.activation(rstd[:, :], ps[:, 0, :], ACT.Sqrt, scale=1.0 / D, bias=c_("eps")).then_inc(rms_done, 1)
                for c in range(DC if parts else 0):
                    act.wait_ge(hn_done, DC * at + c + 1)
                    nc.scalar.activation(h_hi[:, c, :], scr[:, c, :], ACT.Copy).then_inc(hn_hi_done, 1)

            def ffn(u0, n, next_norm):
                with act.Fori(0, FT // 2) as i:
                    for f in range(2):
                        head(unit(u0 + 2 * f + 2, 4, i))
                        act.wait_ge(unit_done, u0 + 4 * i + 2 * f + 1)
                        act.wait_ge(hid_done, FT * n + 2 * i + f + 1)
                        nc.scalar.activation(silu[:, f, :], ps[:, 4 + 2 * f, :], ACT.Silu).then_inc(silu_done, 1)
                        head(unit(u0 + 2 * f + 3, 4, i))
                        act.wait_ge(hid_done, FT * n + 2 * i + f + 3)
                        nc.scalar.activation(hid_hi[:, bass.ds(2 * i + f, 1), :].rearrange("p a t -> p (a t)"),
                                             hid[:, f, :], ACT.Copy).then_inc(hid_hi_done, 1)
                ud = u0 + 2 * FT
                kps = FT // 2
                with act.Fori(0, kps // 2) as i:
                    for j in range(2):
                        head(unit(ud + 2 + j, 2, i))
                head(unit(ud + kps + 1))
                squares(next_norm, 0, 4)
                head(unit(ud + kps + 2))
                with act.Fori(0, kps // 2 - 1) as i:
                    for j in range(2):
                        head(unit(ud + kps + 3 + j, 2, i))
                for j in range(2):
                    head(unit(ud + 2 * kps + j))
                squares(next_norm, 4, 8)

            def project():
                act.wait_ge(unit_done, U_PROJ)
                act.dma_start(w1[:, :, :, :].rearrange("p s l n -> p (s l n)"), dram["w1"]).then_inc(w1_in, 16)
                act.dma_start(cbias[:, :], dram["cbias"]).then_inc(w1_in, 16)

                def two(i, scale):
                    for j in range(2):
                        head(unit(U_PROJ + j + 2, 2, i))
                        act.wait_ge(unit_done, U_PROJ + 2 * i + j + 1)
                        nc.scalar.activation(proj[:, bass.ds(2 * i + j, 1), :].rearrange("p a t -> p (a t)"),
                                             ps[:, 2 + j, :], ACT.Copy, scale=scale).then_inc(proj_done, 1)

                with act.Fori(0, MT_KC // 2) as i:
                    two(i, DH ** -0.5)
                with act.Fori(MT_KC // 2, MTILES // 2) as i:
                    two(i, 1.0)
                head(unit(U_PROJ + MTILES + 1))
                act.wait_ge(unit_done, U_PROJ + MTILES)
                nc.scalar.activation(proj[:, MTILES - 1, :], ps[:, 2, :], ACT.Copy).then_inc(proj_done, 1)

            def compressed():
                act.wait_ge(hn_lo_done, 2 * DC)
                act.wait_ge(proj_done, 2 + MT_VC + 1)
                for s in range(2):
                    for g in range(NG):
                        for half in range(2):
                            act.dma_start(dup[half * DH:(half + 1) * DH, 2 * s + g, :],
                                          proj[g * DH:(g + 1) * DH, MT_KC + s, :]).then_inc(dup_in, 16)
                act.wait_ge(tok_ready, 1)
                nc.scalar.activation(gate_tok[:, :, :].rearrange("p q c -> p (q c)"), ps[:, 4, 0:TT * 3 * NH],
                                     ACT.Sigmoid).then_inc(gate_done, 1)
                for s in range(2):
                    act.wait_ge(cmp_pe, s + 1)
                    nc.scalar.activation(gel[:, s, :], ps[:, 7 - 4 * s, 0:NG * NCMP],
                                         ACT.Gelu_apprx_tanh).then_inc(gel_done, 1)
                act.wait_ge(cexp_ready, 1)
                flat = c_score.rearrange("p q h n -> p (q h n)")
                nc.scalar.activation(flat, flat, ACT.Exp).then_inc(cexp_done, 1)
                for h in range(1, NH, 2):
                    act.wait_ge(cmp_pe, 5 + h)
                    nc.scalar.activation(pc_t[:, h, :], ps[0:NCMP, 4 + h % 4, :], ACT.Copy).then_inc(pct_done[1], 1)

            def attention():
                with act.Fori(0, HPG) as j:
                    act.wait_ge(pct_done[0], NH // 2)
                    act.wait_ge(pct_done[1], NH // 2)
                    nc.scalar.activation(q_st[:, :], proj[:, bass.ds(MT_Q + j, 1), :].rearrange("p a t -> p (a t)"),
                                         ACT.Copy)
                    nc.scalar.activation(
                        pc_st[:, :, :], pc_t[:, :, :].rearrange("p (g j) t -> p g j t", g=NG)[:, :, bass.ds(j, 1), :]
                        .rearrange("p g a t -> p g (a t)"), ACT.Copy).then_inc(stage_done, 1)

                    def copy(n):
                        w = (ITEMS[n][1] + 1) * P
                        act.wait_ge(turn_ready, NI * j + n + 1)
                        if n >= 2:
                            act.wait_ge(pv_done, NI * j + n - 1)
                        nc.scalar.activation(prob_t[:, n % 2, 0:w], ps[:, 2 + n % 2, 0:w], ACT.Copy
                                             ).then_inc(prob_t_done, 1)

                    for n in range(NI):
                        w = (ITEMS[n][1] + 1) * P
                        act.wait_ge(neg_done, NI * j + n + 1)
                        if n >= 2:
                            act.wait_ge(turn_ready, NI * j + n - 1)
                        nc.scalar.activation(prob[:, n % 2, 0:w], score[:, n % 2, 0:w], ACT.Exp, scale=-1.0,
                                             bias=nmax[:, n % 2:n % 2 + 1],
                                             accum_out=psum_l[:, n % 2:n % 2 + 1]).then_inc(exp_done, 1)
                        if n >= 1:
                            copy(n - 1)
                    copy(NI - 1)
                    act.wait_ge(pv_done, NI * j + NI)
                    nc.scalar.activation(h_hi[:, bass.ds(j, 1), :].rearrange("p a t -> p (a t)"), ps[:, 4, :],
                                         ACT.Copy).then_inc(o_hi_done, 1)

            def linear():
                for m in range(2):
                    act.wait_ge(z_ready, m + 1)
                    act.wait_ge(cprob_done, 1)
                    s = [scr[:, 4 * m + k, :] for k in range(4)]
                    z = ps[:, 6 + m, :]
                    ba = p_("b_a", m, m + 1)
                    nc.scalar.activation(s[0], z, ACT.Identity, bias=ba)
                    link(nc.scalar.activation(s[1], z, ACT.Abs, bias=ba))
                    link(nc.scalar.activation(s[2], s[1], ACT.Exp, scale=-1.0))
                    nc.scalar.activation(s[1], s[2], ACT.Ln, bias=c_("one")).then_inc(gln_done, 1)
                for m in range(2):
                    b = scr[:, 4 * m + 3, :]
                    act.wait_ge(b_done, m + 1)
                    nc.scalar.activation(decay[:, m, :], b, ACT.Exp, scale=1.0 / 16).then_inc(eb_done, 1)
                    nc.scalar.activation(scr[:, 4 * m + 1, :], b, ACT.Exp, scale=-1.0 / 16).then_inc(eb_done, 1)
                    act.wait_ge(kst_diff, m + 1)
                    nc.scalar.activation(scr[:, 4 * m + 2, :], scr[:, 4 * m + 2, :], ACT.Exp,
                                         scale=1.0 / 16).then_inc(kst_exp, 1)
                for h in range(GH):
                    act.wait_ge(gv_turned, h + 1)
                    nc.scalar.activation(gv_tok[:, :, h * GDV:(h + 1) * GDV],
                                         ps[:, h, :].rearrange("p (q d) -> p q d", q=TT), ACT.Copy
                                         ).then_inc(gv_copied, 1)
                act.wait_ge(a_used, 2 * TT - 1)
                act.wait_ge(pv_done, NI * HPG + GH * TT)
                for h in range(GH):
                    nc.scalar.activation(scr[:, h, :], ps[:, 4 + h, :], ACT.Square).then_inc(gsq_done, 1)
                for h in range(GH):
                    act.wait_ge(gssq_done, h + 1)
                    nc.scalar.activation(scr[:, 4 + h, :], ps[:, h % 2, :], ACT.Sqrt, scale=1.0 / GDV, bias=c_("eps")
                                         ).then_inc(grms_done, 1)
                for h in range(GH):
                    nc.scalar.activation(proj[:, MT_GR + h, :], proj[:, MT_GR + h, :], ACT.Silu).then_inc(gr_done, 1)
                for h in range(GH):
                    act.wait_ge(go_done, h + 1)
                    nc.scalar.activation(h_hi[:, 4 + h, :], scr[:, h, :], ACT.Copy).then_inc(go_hi, 1)

            def to_stream(u0, n):
                with act.Fori(0, DC // 2) as i:
                    for j in range(2):
                        head(unit(u0 + j + 2, 2, i))
                        act.wait_ge(x_done, DC * n + 2 * i + j + 1)
                        at = bass.ds(2 * i + j, 1)
                        nc.scalar.activation(scr[:, at, :], x[:, at, :], ACT.Square).then_inc(sq_done, 1)

            def gates():
                head(unit(U_GATES + 2))
                act.wait_ge(hn_lo_done, 4 * DC)
                act.dma_start(scr[:, 6:8, :].rearrange("p a t -> p (a t)"), dram["row_const"]).then_inc(rows_in, 16)
                act.wait_ge(unit_done, U_GATES + 1)
                z, bif = ps[:, 4, :], p_("b_if")
                nc.scalar.activation(scr[:, 0, :], z, ACT.Identity, bias=bif)
                link(nc.scalar.activation(scr[:, 1, :], z, ACT.Abs, bias=bif))
                link(nc.scalar.activation(scr[:, 2, :], scr[:, 1, :], ACT.Exp, scale=-1.0))
                nc.scalar.activation(scr[:, 1, :], scr[:, 2, :], ACT.Ln, bias=c_("one")).then_inc(row_l, 1)
                act.wait_ge(edge_done, 1)
                nc.scalar.activation(edge[:, 4, :], edge[:, 4, :], ACT.Exp).then_inc(edge_exp, 1)
                act.wait_ge(row_args, 1)
                nc.scalar.activation(scr[0:64, 2, :], scr[0:64, 2, :], ACT.Exp)
                nc.scalar.activation(row_i[:, :], row_i[:, :], ACT.Exp)
                nc.scalar.activation(row_f[:, :], row_f[:, :], ACT.Exp).then_inc(row_exp, 1)

            def mlstm_head(h):
                def take(j, dst, func):
                    act.wait_ge(unit_done, U_HEADS + HEAD_UNITS * h + j + 1)
                    nc.scalar.activation(dst, ps[:, j % 2, :], func).then_inc(ev_done, 1)

                def activate(j):
                    act.wait_ge(conv_done, 4 * h + j + 1)
                    src = bass.ds(2 * h + j, 1) if j < 2 else bass.ds(2 * h + DC + j - 2, 1)
                    nc.scalar.activation(qk[:, j, :], scr[:, 2 + j % 2, :], ACT.Silu, bias=p_("conv_b")[:, src]
                                         ).then_inc(qk_done, 1)

                for j in range(HEAD_UNITS):
                    head(unit(U_HEADS + j + 2, HEAD_UNITS, h))
                    if j < 4:
                        if j >= 2:
                            act.wait_ge(conv_done, 4 * h + j - 1)
                        take(j, qk_pad[:, j % 2, CONV // 2:CONV // 2 + T], ACT.Copy)
                    elif j < 6:
                        take(j, scr[:, j - 4, :], ACT.Copy)
                    elif j < 8:
                        take(j, scr[:, j - 2, :], ACT.Sigmoid)
                    else:
                        take(j, scr[:, j - 2, :], ACT.Silu)
                    if 2 <= j < 6:
                        activate(j - 2)
                for e in range(2):
                    act.wait_ge(vt_ready, 2 * h + e + 1)
                    nc.scalar.activation(v_aug[:, :, e * P:(e + 1) * P], ps[:, 4 + e, :].rearrange("p (c d) -> p c d", c=NCH),
                                         ACT.Copy).then_inc(vt_done, 1)
                for d in range(2):
                    act.wait_ge(dlog_done, 2 * h + d + 1)
                    nc.scalar.activation(d_mat[:, d, :], d_mat[:, d, :], ACT.Exp).then_inc(dexp_done, 1)
                    act.wait_ge(fl_ready, 2 * h + d + 1)
                    nc.scalar.activation(floor[:, d, :], ps[:, 3, :], ACT.Copy).then_inc(fl_done, 1)
                act.wait_ge(num_done, 8 * h + 8)
                act.wait_ge(num_ready, 8 * h + 8)
                for e in range(2):
                    nc.scalar.activation(d_mat[:, e, :], h_sum[:, e, :], ACT.Square).then_inc(hsq_done, 1)
                act.wait_ge(hssq_done, h + 1)
                nc.scalar.activation(floor[:, 0, :], ps[:, 3, :], ACT.Sqrt, scale=1.0 / MD, bias=c_("eps")
                                     ).then_inc(hrms_done, 1)
                for e in range(2):
                    act.wait_ge(y_done, 2 * h + e + 1)
                    nc.scalar.activation(y_hi[:, bass.ds(2 * h + e, 1), :].rearrange("p a t -> p (a t)"), h_sum[:, e, :],
                                         ACT.Copy).then_inc(y_hi_done, 1)

            def merge(u0, done):
                with act.Fori(0, DC // 2) as i:
                    for j in range(2):
                        head(unit(u0 + 2 * j + 2, 4, i))
                        act.wait_ge(unit_done, u0 + 4 * i + 2 * j + 1)
                        act.wait_ge(mg_done, done + 2 * i + j + 1)
                        bias_at = (DC if done == 0 else 0) + 2 * i + j
                        nc.scalar.activation(gate[:, j, :], ps[:, 4 + 2 * j, :], ACT.Sigmoid,
                                             bias=p_("b_merge")[:, bass.ds(bias_at, 1)]).then_inc(mg_sig, 1)
                        head(unit(u0 + 2 * j + 3, 4, i))
                        if done:
                            act.wait_ge(mg_done, done + 2 * i + j + 3)
                            at = bass.ds(2 * i + j, 1)
                            nc.scalar.activation(m_hi[:, at, :], merged[:, at, :], ACT.Copy).then_inc(m_hi_done, 1)

            def pooled():
                act.wait_ge(mg_done, DC + 2)
                act.dma_start(inv_count[:, :, :].rearrange("p w t -> p (w t)"), dram["inv_count"]).then_inc(inv_in, 16)

                def pool_head(c):
                    act.wait_ge(pool_done, c + 1)
                    nc.scalar.activation(y_hi[:, c, :], scr[:, c, :], ACT.Copy).then_inc(y_hi_done, 1)

                for j in range(DC):
                    head(unit(U_POOL + j + 2))
                    act.wait_ge(unit_done, U_POOL + j + 1)
                    if j >= 2:
                        act.wait_ge(pool_done, j - 1)
                    if j == 0:
                        act.wait_ge(upad_done, 1)
                    nc.scalar.activation(u_pad[:, j % 2, 8:8 + T], ps[:, 2 + j % 2, :], ACT.Copy).then_inc(ev_done, 1)
                    if j >= 1:
                        pool_head(j - 1)
                for j in range(DC):
                    head(unit(U_POOL + DC + j + 2))
                    act.wait_ge(unit_done, U_POOL + DC + j + 1)
                    nc.scalar.activation(silu_z[:, j, :], ps[:, 2 + j % 2, :], ACT.Silu).then_inc(ev_done, 1)
                    if j == 0:
                        pool_head(DC - 1)
                for n in range(2):
                    head(unit(U_MIX2 + n + 2))
                    for c in range(4 * n, 4 * n + 4):
                        act.wait_ge(y_done, 2 * MH + c + 1)
                        nc.scalar.activation(y_hi[:, c, :], scr[:, c, :], ACT.Copy).then_inc(y_hi_done, 1)

            def output():
                for i in range(DC):
                    if U_OUT + i + 2 < NUNITS:
                        head(unit(U_OUT + i + 2))
                    act.wait_ge(out_done, i + 3)
                    nc.scalar.activation(scr[:, i, :], merged[:, i, :], ACT.Square).then_inc(sq_done, 1)
                norm(5, parts=False)

            link = Chain(act, act_chain).link
            act.wait_ge(small_in, 32)
            act.wait_ge(x_in, 16 * DC)
            squares(0, 0, 8)
            for u in range(2):
                act.wait_ge(raw_full[u], 16)
                nc.scalar.activation(w_hi[:, u, :], w_raw[:, u, :], ACT.Copy).then_inc(w_hi_done, 1)
            norm(0)
            ffn(U_FFN1, 0, 1)
            norm(1)
            project()
            compressed()
            attention()
            linear()
            to_stream(U_MIXOUT, 2)
            norm(2)
            ffn(U_FFN2, 1, 3)
            norm(3, parts=False)
            squares(4, 0, 8)
            norm(4, at=3)
            gates()
            with act.Fori(0, MH) as h:
                mlstm_head(h)
            merge(U_PB, 0)
            pooled()
            merge(U_PA, DC)
            output()

        @block.vector
        def _(dve):
            chain = Chain(dve, dve_chain)

            def norm_sum(n):
                for c in range(1, 4):
                    dve.wait_ge(sq_done, DC * n + c + 1)
                    ins = nc.vector.tensor_tensor(scr[:, 0, :], scr[:, 0, :], scr[:, c, :], ALU.add)
                    if c < 3:
                        chain.link(ins)
                ins.then_inc(sqsum_done, 1)

            def norm(n, gain, at=None):
                at = n if at is None else at
                dve.wait_ge(rms_done, n + 1)
                nc.vector.reciprocal(rstd[:, :], rstd[:, :]).then_inc(rstd_done, 1)
                dve.wait_ge(rstd_done, n + 1)

                def tail(c):
                    dve.wait_ge(hn_hi_done, DC * at + c + 1)
                    nc.vector.tensor_tensor(h_lo[:, c, :], scr[:, c, :], h_hi[:, c, :].bitcast(F32),
                                            ALU.subtract).then_inc(hn_lo_done, 1)

                for c in range(DC):
                    nc.vector.scalar_tensor_tensor(scr[:, c, :], x[:, c, :], p_(gain, c, c + 1), rstd[:, :],
                                                   ALU.mult, ALU.mult).then_inc(hn_done, 1)
                    if c >= 1:
                        tail(c - 1)
                tail(DC - 1)

            def ffn(u0, n, next_norm):
                with dve.Fori(0, FT // 2) as i:
                    for f in range(2):
                        dve.wait_ge(unit_done, u0 + 4 * i + 2 * f + 2)
                        dve.wait_ge(silu_done, FT * n + 2 * i + f + 1)
                        nc.vector.tensor_tensor(hid[:, f, :], silu[:, f, :], ps[:, 5 + 2 * f, :],
                                                ALU.mult).then_inc(hid_done, 1)
                        dve.wait_ge(hid_hi_done, FT * n + 2 * i + f + 1)
                        at = bass.ds(2 * i + f, 1)
                        nc.vector.tensor_tensor(hid_lo[:, at, :].rearrange("p a t -> p (a t)"), hid[:, f, :],
                                                hid_hi[:, at, :].rearrange("p a t -> p (a t)").bitcast(F32),
                                                ALU.subtract).then_inc(hid_lo_done, 1)
                for half in range(2):
                    dve.wait_ge(unit_done, u0 + 2 * FT + (half + 1) * (FT // 2))
                    for d in range(4 * half, 4 * half + 4):
                        nc.vector.scalar_tensor_tensor(x[:, d, :], ps[:, d, :], 0.5, x[:, d, :],
                                                       ALU.mult, ALU.add).then_inc(x_done, 1)
                    if half == 0:
                        norm_sum(next_norm)

            def compressed():
                dve.wait_ge(dup_in, 8 * 16)
                for s in range(2):
                    for half in range(2):
                        r = slice(half * DH, (half + 1) * DH)
                        for part in range(2):
                            tok = dup[r, 2 * s:2 * s + 2, :].rearrange("p g (n c) -> p c g n", c=16)
                            src = tok[:, half:16:2, :, part:part + NCMP]
                            pos = p_("pe", s * 16 + part * 8, s * 16 + part * 8 + 8)[r].unsqueeze(2).unsqueeze(3)
                            ins = nc.vector.tensor_tensor(rows[r, s, part * 8:part * 8 + 8, :, :], src,
                                                          pos.to_broadcast([DH, 8, NG, NCMP]), ALU.add)
                    ins.then_inc(rows_done, 1)
                dve.wait_ge(tok_ready, 1)
                for b in range(2):
                    nc.vector.tensor_copy(v_tok[:, :, b, :], ps[:, 5 + b, :].rearrange("p (q d) -> p q d", q=TT)
                                          ).then_inc(tok_done, 1)
                dve.wait_ge(gate_done, 1)
                dve.sem_inc(tok_done, 1)
                dve.wait_ge(cmp_pe, 3)
                nc.vector.tensor_copy(kc_t[:, :], ps[:, 0, 0:NCMP])
                nc.vector.tensor_copy(vc_tok[:, :, :].rearrange("p g d -> p (g d)"), ps[0:NCMP, 1, 0:NG * DH]
                                      ).then_inc(kvc_done, 1)
                dve.wait_ge(cmp_pe, 4)
                dve.wait_ge(w1_in, 32)
                cb = cbias[:, :].rearrange("p (q h n) -> p q h n", q=TT, h=NH)
                for g in range(NG):
                    hs = slice(g * HPG, (g + 1) * HPG)
                    psc = ps[:, 2 + g, :].rearrange("p (q h n) -> p q h n", q=TT, h=HPG)[:, :, :, 0:NCMP]
                    ins = nc.vector.tensor_tensor(c_score[:, :, hs, :], psc, cb[:, :, hs, :], ALU.add)
                chain.link(ins)
                sc3 = c_score.rearrange("p q h n -> p (q h) n")

                def rep_(v):
                    return v.unsqueeze(2).to_broadcast([P, TT * NH, NCMP])

                chain.link(nc.vector.tensor_reduce(c_max[:, :], sc3, AX.X, ALU.max))
                nc.vector.tensor_tensor(sc3, sc3, rep_(c_max[:, :]), ALU.subtract).then_inc(cexp_ready, 1)
                dve.wait_ge(cexp_done, 1)
                chain.link(nc.vector.tensor_reduce(c_sum[:, :], sc3, AX.X, ALU.add))
                chain.link(nc.vector.reciprocal(c_max[:, :], c_sum[:, :]))
                g0 = gate_tok[:, :, :].rearrange("p q (h b) -> p (q h) b", b=3)[:, :, 0]
                chain.link(nc.vector.tensor_tensor(c_sum[:, :], c_max[:, :], g0, ALU.mult))
                valid = c_("cvalid").rearrange("p (q n) -> p q n", q=TT).unsqueeze(2).to_broadcast([P, TT, NH, NCMP])
                chain.link(nc.vector.tensor_tensor(c_score, c_score, valid, ALU.mult))
                nc.vector.tensor_tensor(sc3, sc3, rep_(c_sum[:, :]), ALU.mult).then_inc(cprob_done, 1)
                for h in range(0, NH, 2):
                    dve.wait_ge(cmp_pe, 5 + h)
                    nc.vector.tensor_copy(pc_t[:, h, :], ps[0:NCMP, 4 + h % 4, :]).then_inc(pct_done[0], 1)

            def attention():
                with dve.Fori(0, HPG) as j:
                    for g in range(NG):
                        ins = nc.vector.tensor_scalar(bias[:, g, :], c_("dist"), c_("slope")[:, bass.ds(j + HPG * g, 1)],
                                                      None, ALU.mult)
                    ins.then_inc(bias_done, 1)
                    dve.wait_ge(bias_done, j + 1)

                    def finish(n):
                        b, qt, g = ITEMS[n]
                        w = (qt + 1) * P
                        dve.wait_ge(exp_done, NI * j + n + 1)
                        nc.vector.reciprocal(psum_l[:, n % 2:n % 2 + 1], psum_l[:, n % 2:n % 2 + 1]).then_inc(rl_done, 1)
                        dve.wait_ge(rl_done, NI * j + n + 1)
                        gate = gate_tok[:, qt, bass.ds(3 * j + 3 * HPG * g + b + 1, 1)]
                        nc.vector.tensor_scalar(prob[:, n % 2, 0:w], prob[:, n % 2, 0:w], psum_l[:, n % 2:n % 2 + 1],
                                                gate, ALU.mult, ALU.mult).then_inc(prob_done, 1)

                    for n in range(NI):
                        b, qt, g = ITEMS[n]
                        w = (qt + 1) * P
                        dve.wait_ge(score_ready, NI * j + n + 1)
                        if n >= 2:
                            dve.wait_ge(exp_done, NI * j + n - 1)
                        dve.sem_inc(score_turn, 1)
                        nc.vector.tensor_tensor_reduce(score[:, n % 2, 0:w], ps[:, n % 2, 0:w], bias[:, g, T - w:T],
                                                       -1.0, 3.0e38, ALU.add, ALU.min, nmax[:, n % 2:n % 2 + 1]
                                                       ).then_inc(neg_done, 1)
                        if n >= 1:
                            finish(n - 1)
                    finish(NI - 1)
                    dve.wait_ge(o_hi_done, j + 1)
                    at = bass.ds(j, 1)
                    nc.vector.tensor_tensor(h_lo[:, at, :].rearrange("p a t -> p (a t)"), ps[:, 4, :],
                                            h_hi[:, at, :].rearrange("p a t -> p (a t)").bitcast(F32), ALU.subtract
                                            ).then_inc(o_lo_done, 1)

            def linear():
                nc.vector.memset(intra[:, :, :], 0.0)
                for m in range(2):
                    s = [scr[:, 4 * m + k, :] for k in range(4)]
                    dve.wait_ge(gln_done, m + 1)
                    chain.link(nc.vector.scalar_tensor_tensor(s[2], s[0], 0.0, s[1], ALU.min, ALU.subtract))
                    nc.vector.tensor_tensor_scan(s[3], c_("keep"), s[2], 0.0, ALU.mult, ALU.add).then_inc(b_done, 1)
                for m in range(2):
                    s = [scr[:, 4 * m + k, :] for k in range(4)]
                    dve.wait_ge(b_done, m + 1)
                    b3 = s[3].rearrange("p (n c) -> p n c", c=GC)
                    last = b3[:, :, GC - 1:GC].to_broadcast([P, T // GC, GC])
                    nc.vector.tensor_tensor(s[2].rearrange("p (n c) -> p n c", c=GC), last, b3, ALU.subtract
                                            ).then_inc(kst_diff, 1)
                    dve.wait_ge(eb_done, 2 * m + 2)
                    nc.vector.tensor_tensor(q_in[:, m, :], proj[:, MT_GQ + m, :], decay[:, m, :], ALU.mult)
                    nc.vector.tensor_tensor(k_in[:, m, :], proj[:, MT_GK + m, :], s[1], ALU.mult)
                    dve.wait_ge(kst_exp, m + 1)
                    nc.vector.tensor_tensor(s[0], proj[:, MT_GK + m, :], s[2], ALU.mult).then_inc(kst_done, 1)
                for m in range(2):
                    dve.wait_ge(kst_turned, m + 1)
                    nc.vector.tensor_copy(kst_tok[:, :, m * P:(m + 1) * P],
                                          ps[:, 4 + m, :].rearrange("p (q d) -> p q d", q=TT)).then_inc(kst_copied, 1)
                for tt in range(TT):
                    for h in range(GH):
                        n = tt * GH + h
                        dve.wait_ge(a_ready, n + 1)
                        if n >= 2:
                            dve.wait_ge(pv_done, NI * HPG + n - 1)
                        nc.vector.copy_predicated(intra[:, n % 2, :], c_("gmask").bitcast(I32), ps[:, n % 2, 0:P]
                                                  ).then_inc(a_done, 1)
                    for c in range(2):
                        n = 2 * tt + c
                        if n < T // GC - 1:
                            dve.wait_ge(add_ready, n + 1)
                            if n >= 1:
                                dve.wait_ge(state_done, n)
                            if n >= 2:
                                dve.wait_ge(a_used, n - 1)
                            for m in range(2):
                                new, add = state[:, m, (n + 1) % 2, :], ps[:, 2 + n % 2, m * GDV:(m + 1) * GDV]
                                if n == 0:
                                    ins = nc.vector.tensor_copy(new, add)
                                else:
                                    at = n * GC + GC - 1
                                    ins = nc.vector.scalar_tensor_tensor(new, state[:, m, n % 2, :],
                                                                         decay[:, m, at:at + 1], add, ALU.mult, ALU.add)
                            ins.then_inc(state_done, 1)
                for h in range(GH):
                    dve.wait_ge(grms_done, h + 1)
                    chain.link(nc.vector.reciprocal(scr[:, 4 + h, :], scr[:, 4 + h, :]))
                    chain.link(nc.vector.scalar_tensor_tensor(scr[:, h, :], ps[:, 4 + h, :], p_("g_gla"),
                                                              scr[:, 4 + h, :], ALU.mult, ALU.mult))
                    dve.wait_ge(gr_done, h + 1)
                    nc.vector.tensor_tensor(scr[:, h, :], scr[:, h, :], proj[:, MT_GR + h, :], ALU.mult
                                            ).then_inc(go_done, 1)
                    dve.wait_ge(go_hi, h + 1)
                    nc.vector.tensor_tensor(h_lo[:, 4 + h, :], scr[:, h, :], h_hi[:, 4 + h, :].bitcast(F32),
                                            ALU.subtract).then_inc(go_lo, 1)

            def to_stream(u0, n):
                with dve.Fori(0, DC // 2) as i:
                    for j in range(2):
                        dve.wait_ge(unit_done, u0 + 2 * i + j + 1)
                        at = bass.ds(2 * i + j, 1)
                        xd = x[:, at, :].rearrange("p a t -> p (a t)")
                        nc.vector.tensor_tensor(xd, ps[:, 2 + j, :], xd, ALU.add).then_inc(x_done, 1)
                norm_sum(n)

            def gates():
                fwd, bwd = slice(0, 32), slice(32, 64)
                z, b, a, cm, lf = (scr[:, k, :] for k in (0, 5, 3, 1, 4))
                bl, cl, mb, ma, kp = (edge[:, k, :] for k in range(5))
                nc.vector.memset(v_aug[:, :, MD:MD + P], 1.0)
                nc.vector.memset(qk_pad[:, :, 0:CONV // 2], 0.0)
                nc.vector.memset(qk_pad[:, :, CONV // 2 + T:], 0.0)
                dve.wait_ge(row_l, 1)
                dve.wait_ge(rows_in, 16)
                chain.link(nc.vector.scalar_tensor_tensor(a[64:128], z[64:128], 0.0, cm[64:128], ALU.min, ALU.subtract))
                chain.link(nc.vector.tensor_copy(lf[0:64], a[64:128]))
                keep, reset = scr[:, 6, :], scr[:, 7, :]
                nc.vector.tensor_tensor_scan(b[fwd], keep[fwd], lf[fwd], 0.0, ALU.mult, ALU.add)
                chain.link(nc.vector.tensor_tensor_scan(b[bwd, ::-1], keep[bwd, ::-1], lf[bwd, ::-1], 0.0,
                                                        ALU.mult, ALU.add))
                chain.link(nc.vector.tensor_tensor(a[0:64], z[0:64], b[0:64], ALU.subtract))
                nc.vector.tensor_tensor_scan(cm[fwd], reset[fwd], a[fwd], NEG, ALU.add, ALU.max)
                chain.link(nc.vector.tensor_tensor_scan(cm[bwd, ::-1], reset[bwd, ::-1], a[bwd, ::-1], NEG,
                                                        ALU.add, ALU.max))
                for src, dst in ((b, bl), (cm, cl)):
                    nc.vector.tensor_copy(dst[fwd], src[fwd, MC - 1::MC])
                    nc.vector.tensor_copy(dst[bwd, ::-1], src[bwd, 0::MC])
                chain.link(nc.vector.memset(mb[:, 0:1], NEG))
                for s in range(NCH):
                    one = slice(s, s + 1)
                    chain.link(nc.vector.tensor_tensor(ma[:, one], cl[:, one], mb[:, one], ALU.max))
                    if s + 1 < NCH:
                        chain.link(nc.vector.tensor_tensor(mb[:, s + 1:s + 2], bl[:, one], ma[:, one], ALU.add))
                nc.vector.tensor_tensor(kp, mb, ma, ALU.subtract).then_inc(edge_done, 1)

                def chunks(v, r):
                    return v[r].rearrange("p (c t) -> p c t", c=NCH)

                def spread(v, r):
                    return (v[r, ::-1] if r is bwd else v[r]).unsqueeze(2).to_broadcast([32, NCH, MC])

                for r in (fwd, bwd):
                    ins = nc.vector.tensor_tensor(chunks(row_m, r), chunks(cm, r), spread(mb, r), ALU.max)
                chain.link(ins)
                for r in (fwd, bwd):
                    nc.vector.tensor_tensor(chunks(row_i, r), spread(mb, r), chunks(row_m, r), ALU.subtract)
                    nc.vector.tensor_tensor(chunks(scr[:, 2, :], r), chunks(a, r), spread(ma, r), ALU.subtract)
                chain.link(nc.vector.tensor_tensor(row_f[:, :], b[0:64], row_m[:, :], ALU.add))
                nc.vector.tensor_scalar(row_f[:, :], row_f[:, :], -1.0, 88.0, ALU.mult, ALU.min)
                nc.vector.tensor_scalar(row_m[:, :], row_m[:, :], -1.0, None, ALU.mult).then_inc(row_args, 1)
                dve.wait_ge(row_exp, 1)
                for n, dst in enumerate((a_tok, wk_tok)):
                    dve.wait_ge(tokrow_ready, n + 1)
                    nc.vector.tensor_copy(dst[:, :, :].rearrange("p c r -> p (c r)"), ps[:, 5 + n, 0:NCH * 64])
                dve.wait_ge(tokrow_ready, 3)
                nc.vector.tensor_copy(keep_bc[:, :], ps[:, 7, 0:2 * MH * NCH]).then_inc(tokrow_done, 1)
                dve.wait_ge(tokrow_done, 1)

            def mlstm_head(h):
                chain.enter(h, MLSTM_LINKS)
                for d in range(2):
                    ins = nc.vector.tensor_copy(sel[:, d, :], ident[0:64, bass.ds(h + 32 * d, 1)].to_broadcast([64, P]))
                ins.then_inc(sel_done, 1)
                for j in range(4):
                    dve.wait_ge(ev_done, HEAD_UNITS * h + j + 3)
                    if j >= 2:
                        dve.wait_ge(qk_done, 4 * h + j - 1)
                    acc = scr[:, 2 + j % 2, :]
                    at = (2 * h + j if j < 2 else 2 * h + DC + j - 2) * CONV
                    for k in range(CONV):
                        tap, w = qk_pad[:, j % 2, k:k + T], p_("conv_w")[:, bass.ds(at + k, 1)]
                        if k == 0:
                            ins = nc.vector.tensor_scalar(acc, tap, w, None, ALU.mult)
                        else:
                            ins = nc.vector.scalar_tensor_tensor(acc, tap, w, acc, ALU.mult, ALU.add)
                        if k < CONV - 1:
                            chain.link(ins)
                    ins.then_inc(conv_done, 1)
                for e in range(2):
                    dve.wait_ge(kt_ready, 2 * h + e + 1)
                    nc.vector.tensor_copy(k_tok[:, :, e * P:(e + 1) * P],
                                          ps[:, 2 + e, :].rearrange("p (c d) -> p c d", c=NCH)).then_inc(kt_done, 1)
                dve.wait_ge(kt_done, 2 * h + 2)

                def weigh_keys(n):
                    s, d = STEPS[n]
                    c = chunk_of(s, d)
                    if n >= 2:
                        dve.wait_ge(cadd_ready, 6 * h + n - 1)
                    nc.vector.tensor_scalar(k_w[:, d, :], k_tok[:, c, :], wk_tok[:, c, bass.ds(h + 32 * d, 1)], None,
                                            ALU.mult).then_inc(kw_done, 1)

                weigh_keys(0)
                weigh_keys(1)
                for d in range(2):
                    dve.wait_ge(nm_ready, 2 * h + d + 1)
                    for c in range(NCH):
                        at = slice(c * MC, (c + 1) * MC)
                        ins = nc.vector.scalar_tensor_tensor(d_mat[:, d, at], ps[:, 7, at], a_tok[:, c, bass.ds(h + 32 * d, 1)],
                                                             c_(("upper", "lower")[d]), ALU.add, ALU.add)
                    ins.then_inc(dlog_done, 1)
                    dve.wait_ge(in_ready, 2 * h + d + 1)
                    for e in range(2):
                        ins = nc.vector.scalar_tensor_tensor(q_sc[:, d, e, :], qk[:, e, :], MD ** -0.5, ps[:, 2, :],
                                                             ALU.mult, ALU.mult)
                    ins.then_inc(qs_done, 1)
                for d in range(2):
                    dve.wait_ge(sc_ready, h + 1)
                    dve.wait_ge(dexp_done, 2 * h + d + 1)
                    nc.vector.scalar_tensor_tensor(d_mat[:, d, :], ps[:, 6, :], MD ** -0.5, d_mat[:, d, :],
                                                   ALU.mult, ALU.mult).then_inc(sct_done, 1)
                for n, (s, d) in enumerate(STEPS):
                    c = chunk_of(s, d)
                    if s < NCH - 1:
                        if n + 2 < 6:
                            weigh_keys(n + 2)
                        dve.wait_ge(cadd_ready, 6 * h + n + 1)
                        dve.wait_ge(num_ready, 8 * h + n + 1)
                        for e in range(2):
                            new, add = c_state[:, d, e, :], ps[:, 4 + e, 0:MD + P]
                            if s == 0:
                                ins = nc.vector.tensor_copy(new, add)
                            else:
                                at = bass.ds(h * NCH + d * MH * NCH + s, 1)
                                ins = nc.vector.scalar_tensor_tensor(new, new, keep_bc[:, at], add, ALU.mult, ALU.add)
                        ins.then_inc(c_done, 1)
                    dve.wait_ge(num_ready, 8 * h + n + 1)
                    dve.wait_ge(fl_done, 2 * h + d + 1)
                    at = slice(c * MC, (c + 1) * MC)
                    q_n = ps[:, 6 + d, MD:MD + P]
                    chain.link(nc.vector.scalar_tensor_tensor(den[:, d, :], q_n, -1.0, floor[:, d, at], ALU.mult, ALU.max))
                    chain.link(nc.vector.tensor_tensor(den[:, d, :], den[:, d, :], q_n, ALU.max))
                    chain.link(nc.vector.reciprocal(den[:, d, :], den[:, d, :]))
                    num = ps[:, 6 + d, 0:MD].rearrange("p (e t) -> p e t", e=2)
                    rden = den[:, d, :].unsqueeze(1).to_broadcast([P, 2, MC])
                    if n in FIRST_OF:
                        nc.vector.tensor_tensor(h_sum[:, :, at], num, rden, ALU.mult).then_inc(num_done, 1)
                    else:
                        chain.link(nc.vector.tensor_tensor(h_tmp[:, :, :], num, rden, ALU.mult))
                        nc.vector.tensor_tensor(h_sum[:, :, at], h_sum[:, :, at], h_tmp[:, :, :], ALU.add
                                                ).then_inc(num_done, 1)
                dve.wait_ge(hrms_done, h + 1)
                chain.link(nc.vector.reciprocal(floor[:, 0, :], floor[:, 0, :]))
                for e in range(2):
                    y = h_sum[:, e, :]
                    chain.link(nc.vector.scalar_tensor_tensor(y, y, p_("g_mlstm")[:, bass.ds(2 * h + e, 1)], floor[:, 0, :],
                                                              ALU.mult, ALU.mult))
                    chain.link(nc.vector.tensor_tensor(y, y, scr[:, 4 + e, :], ALU.mult))
                    nc.vector.tensor_tensor(y, y, scr[:, 6 + e, :], ALU.mult).then_inc(y_done, 1)
                for e in range(2):
                    dve.wait_ge(y_hi_done, 2 * h + e + 1)
                    at = bass.ds(2 * h + e, 1)
                    nc.vector.tensor_tensor(y_lo[:, at, :].rearrange("p a t -> p (a t)"), h_sum[:, e, :],
                                            y_hi[:, at, :].rearrange("p a t -> p (a t)").bitcast(F32), ALU.subtract
                                            ).then_inc(y_lo_done, 1)
                chain.leave(MH)

            def merge(u0, done):
                with dve.Fori(0, DC // 2) as i:
                    if done:
                        chain.enter(i, 2)
                    for j in range(2):
                        dve.wait_ge(unit_done, u0 + 4 * i + 2 * j + 2)
                        dve.wait_ge(mg_sig, done + 2 * i + j + 1)
                        at = bass.ds(2 * i + j, 1)
                        m = merged[:, at, :].rearrange("p a t -> p (a t)")
                        if done:
                            chain.link(nc.vector.tensor_tensor(gate[:, j, :], gate[:, j, :], ps[:, 5 + 2 * j, :], ALU.mult))
                            nc.vector.tensor_tensor(m, m, gate[:, j, :], ALU.add).then_inc(mg_done, 1)
                            dve.wait_ge(m_hi_done, 2 * i + j + 1)
                            nc.vector.tensor_tensor(m_lo[:, at, :], merged[:, at, :], m_hi[:, at, :].bitcast(F32),
                                                    ALU.subtract).then_inc(m_lo_done, 1)
                        else:
                            nc.vector.tensor_tensor(m, gate[:, j, :], ps[:, 5 + 2 * j, :], ALU.mult).then_inc(mg_done, 1)
                    if done:
                        chain.leave(DC // 2)

            def pooled():
                nc.vector.memset(u_pad[:, :, 0:8], 0.0)
                nc.vector.memset(u_pad[:, :, 8 + T:], 0.0).then_inc(upad_done, 1)
                dve.wait_ge(inv_in, 16)

                def tail(c, first):
                    dve.wait_ge(y_hi_done, first + c + 1)
                    nc.vector.tensor_tensor(y_lo[:, c, :], scr[:, c, :], y_hi[:, c, :].bitcast(F32), ALU.subtract
                                            ).then_inc(y_lo_done, 1)

                for c in range(DC):
                    g = c // 2
                    w = POOL_W[g]
                    dve.wait_ge(ev_done, HEAD_UNITS * MH + 2 + c + 1)
                    u = u_pad[:, c % 2, :]
                    src, span, turn = u, 1, 0
                    while span < w:
                        dst = win[:, turn, :]
                        chain.link(nc.vector.tensor_tensor(dst[:, 2 * span - 1:], src[:, 2 * span - 1:],
                                                           src[:, span - 1:T + 16 - span], ALU.add))
                        src, span, turn = dst, 2 * span, 1 - turn
                    off = 8 + w // 2 - 1
                    chain.link(nc.vector.tensor_tensor(scr[:, c, :], src[:, off:off + T], inv_count[:, g, :], ALU.mult))
                    nc.vector.tensor_tensor(scr[:, c, :], scr[:, c, :], u[:, 8:8 + T], ALU.subtract).then_inc(pool_done, 1)
                    if c >= 1:
                        tail(c - 1, DC)
                tail(DC - 1, DC)
                for n in range(2):
                    dve.wait_ge(unit_done, U_MIX2 + n + 1)
                    dve.wait_ge(ev_done, HEAD_UNITS * MH + 2 + 2 * DC)
                    for c in range(4 * n, 4 * n + 4):
                        nc.vector.scalar_tensor_tensor(scr[:, c, :], ps[:, 4 - 4 * n + c % 4, :], p_("pool_scale", c, c + 1),
                                                       silu_z[:, c, :], ALU.mult, ALU.mult).then_inc(y_done, 1)
                    for c in range(4 * n, 4 * n + 4):
                        tail(c, 2 * DC)

            def output():
                for i in range(DC):
                    dve.wait_ge(unit_done, U_OUT + i + 1)
                    if i == 0:
                        dve.wait_ge(m_hi_done, DC)
                    nc.vector.tensor_copy(merged[:, i, :], ps[:, 2 + i % 2, :]).then_inc(out_done, 1)
                norm_sum(5)
                dve.wait_ge(rms_done, 6)
                nc.vector.reciprocal(rstd[:, :], rstd[:, :]).then_inc(rstd_done, 1)
                dve.wait_ge(rstd_done, 6)
                dve.wait_ge(ssq_done, 6)
                for c in range(DC):
                    nc.vector.scalar_tensor_tensor(scr[:, c, :], merged[:, c, :], p_("g_post", c, c + 1), rstd[:, :],
                                                   ALU.mult, ALU.mult).then_inc(sum_done, 1)
                    if c >= 1:
                        add(c - 1)
                add(DC - 1)

            def add(c):
                dve.wait_ge(sum_done, c + 1)
                nc.vector.tensor_tensor(x[:, c, :], x[:, c, :], scr[:, c, :], ALU.add).then_inc(x_out, 1)

            for credit in (ev_done, mg_done, out_done):
                dve.sem_inc(credit, 2)
            dve.sem_inc(hid_done, 2)
            dve.sem_inc(proj_done, 2)
            dve.sem_inc(o_lo_done, 1)
            dve.wait_ge(small_in, 32)
            dve.sem_inc(x_done, DC)
            norm_sum(0)
            norm(0, "g_ffn1")
            ffn(U_FFN1, 0, 1)
            norm(1, "g_mix")
            compressed()
            attention()
            linear()
            to_stream(U_MIXOUT, 2)
            norm(2, "g_ffn2")
            ffn(U_FFN2, 1, 3)
            dve.wait_ge(rms_done, 4)
            nc.vector.reciprocal(rstd[:, :], rstd[:, :]).then_inc(rstd_done, 1)
            dve.wait_ge(rstd_done, 4)
            for c in range(DC):
                nc.vector.scalar_tensor_tensor(x[:, c, :], x[:, c, :], p_("g_final", c, c + 1), rstd[:, :],
                                               ALU.mult, ALU.mult).then_inc(x_done, 1)
            norm_sum(4)
            norm(4, "g_pre", at=3)
            gates()
            with dve.Fori(0, MH) as h:
                mlstm_head(h)
            merge(U_PB, 0)
            pooled()
            merge(U_PA, DC)
            output()



def constants():
    c = np.zeros((P, CONST_COLS), np.float32)

    def put(name, value):
        at, width = CONSTS[name]
        c[:, at:at + width] = value

    p = np.arange(P)
    put("ident", np.eye(P))
    put("ones", 1.0)
    put("eps", EPS)
    put("one", 1.0)
    dist = p[:, None] - (np.arange(T)[None, :] - (T - P))
    put("dist", np.where(dist >= 0, dist, 256 * -NEG))
    put("keep", (np.arange(T) % GC != 0)[None, :])
    k, q = p[:, None], p[None, :]
    put("gmask", (k <= q) & (k // GC == q // GC))
    t = np.arange(T).reshape(TT, P).T
    end = np.arange(NCMP) * CMP_STRIDE + CMP_BLOCK - 1
    valid = end[None, None, :] <= t[:, :, None]
    put("cvalid", valid.reshape(P, -1))
    slopes = np.exp2(-8.0 * np.arange(1, NH + 1) / NH)
    put("slope", -slopes[None, :])
    put("upper", np.where(k <= q, 0.0, NEG))
    put("lower", np.where(k >= q, 0.0, NEG))
    center = np.arange(NCMP) * CMP_STRIDE + (CMP_BLOCK - 1) / 2.0
    cbias = -slopes[None, None, :, None] * (t[:, :, None, None] - center[None, None, None, :])
    cbias = np.where(valid[:, :, None, :], cbias, NEG).astype(np.float32).reshape(P, -1)
    tok = np.arange(T)
    inv = np.stack([1.0 / (np.clip(tok + (w - 1 - w // 2), 0, T - 1) - np.clip(tok - w // 2, 0, T - 1) + 1)
                    for w in POOL_W]).astype(np.float32)
    inv = np.ascontiguousarray(np.broadcast_to(inv.reshape(1, -1), (P, len(POOL_W) * T)))
    start = np.where(p[:, None] % 64 < 32, tok % MC == 0, tok % MC == MC - 1)
    row_const = np.concatenate([1.0 - start, np.where(start, NEG, 0.0)], axis=1).astype(np.float32)
    return c, cbias, inv, row_const


def tiled(w):
    K, N = w.shape
    return w.reshape(K // P, P, N // P, P).transpose(2, 1, 0, 3).reshape(N // P, P, K)


def ffNUNITS(w_gate, w_up, w_down):
    gu = np.stack([tiled(w_gate), tiled(w_up)], 1).reshape(2 * FT, P, D)
    down = w_down.reshape(FT // 2, 2, P, 2, 4, P).transpose(3, 0, 2, 1, 4, 5).reshape(FT, P, D)
    return [gu, down]


def columns(v):
    return np.asarray(v).reshape(-1, P).T


def layout(i):
    i = {k: np.asarray(v) for k, v in i.items()}
    split = np.cumsum([NH * DH] + [NG * DH] * 6 + [NH * 3, GH * GDK, GH * GDK, GH * GDV, GH * GDV, LOWR])
    q, kc, vc, ks, vs, kw, vw, gn, gq, gk, gv, gr, ga = np.split(i["w_in"][0], split[:-1], axis=1)
    q = q.reshape(D, NG, HPG, DH).transpose(0, 2, 1, 3).reshape(D, NH * DH)
    small = np.concatenate([gn, gn[:, :8], ga, gq[:, :P - 48]], axis=1)
    proj = np.concatenate([q, gq, kc, vc, ks, vs, kw, vw, gk, gv, gr, small], axis=1)
    w_out = i["w_out"][0]
    w_out = np.concatenate([w_out[:NH * DH].reshape(NG, HPG, DH, D).transpose(1, 0, 2, 3).reshape(NH * DH, D),
                            w_out[NH * DH:]], axis=0)
    w2 = i["w_in_2"][0]
    sizes = [D] * 7 + [16, D, D]
    u_a, z_a, q2, k2, v2, o2, z_b, gates, g_a, g_b = np.split(w2, np.cumsum(sizes)[:-1], axis=1)
    g4 = gates.reshape(D, 2, 2, MH)
    fill = gates[:, :1]
    cols = []
    for kind in range(2):
        for direction in range(2):
            cols += [g4[:, direction, kind], np.repeat(fill, 32 - MH, axis=1)]
    gates_w = np.concatenate(cols, axis=1)
    mix = i["pool_mix_w_2"][0].reshape(2, 2, 2, P, 2, P).transpose(0, 3, 1, 4, 2, 5).reshape(2, P, D)
    ga_t, gb_t = tiled(g_a), tiled(g_b)
    heads = np.stack([tiled(w).reshape(MH, 2, P, D) for w in (q2, k2, v2, o2, z_b)], 1).reshape(-1, P, D)
    units = np.concatenate(
        ffNUNITS(i["ffn1_w_gate"][0], i["ffn1_w_up"][0], i["ffn1_w_down"][0])
        + [tiled(proj), tiled(w_out)]
        + ffNUNITS(i["ffn2_w_gate"][0], i["ffn2_w_up"][0], i["ffn2_w_down"][0])
        + [tiled(gates_w), heads,
           np.stack([gb_t, tiled(i["w_proj_mlstm_2"][0])], 1).reshape(-1, P, D),
           tiled(u_a), tiled(z_a), mix,
           np.stack([ga_t, tiled(i["w_proj_pool_2"][0])], 1).reshape(-1, P, D),
           tiled(i["w_out_2"][0])], axis=0)
    assert units.shape[0] == NUNITS, (units.shape, NUNITS)
    param = np.zeros((P, PARAM_COLS), np.float32)

    def put(name, value, rows=slice(None)):
        at, width = PARAMS[name]
        param[rows, at:at + width] = value

    put("g_ffn1", columns(i["ffn1_norm"][0]))
    put("g_mix", columns(i["mix_norm"][0]))
    put("g_ffn2", columns(i["ffn2_norm"][0]))
    put("g_final", columns(i["final_norm"]))
    put("g_pre", columns(i["norm_pre_g_2"][0]))
    put("g_post", columns(i["norm_post_g_2"][0]))
    put("b_a", columns(i["gla_b_a"][0]))
    put("g_gla", columns(i["gla_norm"][0]))
    put("pool_scale", columns(i["pool_scale_2"][0]))
    put("conv_w", i["conv_qk_w_2"][0].reshape(CONV, 16, P).transpose(2, 1, 0).reshape(P, 16 * CONV))
    put("conv_b", columns(i["conv_qk_b_2"][0]))
    put("g_mlstm", columns(i["mlstm_norm_g_2"][0]))
    put("b_merge", np.concatenate([columns(i["b_merge_2"][0, 0]), columns(i["b_merge_2"][0, 1])], axis=1))
    for direction in range(2):
        put("b_if", i["b_igate_2"][0, direction][:, None], slice(32 * direction, 32 * direction + MH))
        put("b_if", i["b_fgate_2"][0, direction][:, None], slice(64 + 32 * direction, 64 + 32 * direction + MH))
    pe = np.stack([i["nsa_pe_k"][0], i["nsa_pe_v"][0]]).reshape(2, CMP_BLOCK // 2, 2 * DH)
    put("pe", pe.transpose(2, 0, 1).reshape(P, 32))
    put("w2", np.concatenate([i["nsa_w2_k"][0], i["nsa_w2_v"][0]], axis=1))
    put("w_a2", i["gla_w_a2"][0], slice(32, 32 + LOWR))
    w1 = np.stack([i["nsa_w1_k"][0], i["nsa_w1_v"][0]]).reshape(2, CMP_BLOCK // 2, P, CMP_HID)
    w1 = w1.transpose(2, 0, 1, 3).reshape(P, -1)
    const, cbias, inv, row_const = constants()
    return {"x": i["x"][0].T, "units": units, "param": param, "const": const, "w1": w1, "cbias": cbias,
            "inv_count": inv, "row_const": row_const}


def kernel(**inputs):
    import concourse.bacc as bacc
    from concourse.bass_utils import run_bass_kernel_spmd

    nc = bacc.Bacc("TRN2", target_bir_lowering=False, num_devices=1)
    arrays = {f"in_{k}": np.ascontiguousarray(v) for k, v in layout(inputs).items()}
    dram = {k[3:]: nc.dram_tensor(k, a.shape, mybir.dt.from_np(a.dtype), kind="ExternalInput").ap()
            for k, a in arrays.items()}
    out = nc.dram_tensor("out", (D, T), F32, kind="ExternalOutput").ap()
    build(nc, dram, out)
    r = run_bass_kernel_spmd(nc, [arrays], core_ids=[0])
    return np.ascontiguousarray(r.results[0]["out"].T)[None]
```

```python
from contextlib import ExitStack

import concourse.bass as bass
import numpy as np
from concourse import mybir

F32 = mybir.dt.float32
F32R = mybir.dt.float32r
I32 = mybir.dt.int32
ALU = mybir.AluOpType
ACT = mybir.ActivationFunctionType
AX = mybir.AxisListType

P = 128
T = 512
D = 1024
DC = D // P
TT = T // P
FF = 2816
FT = FF // P
EPS = 1e-6
NEG = -1e30

NH, NG, DH = 8, 2, 64
HPG = NH // NG
CMP_BLOCK, CMP_STRIDE, CMP_HID = 32, 16, 128
NCMP = (T - CMP_BLOCK) // CMP_STRIDE + 1
GH, GDK, GDV, GC = 4, 64, 128, 64
LOWR = 16
MH, MD, MC = 4, 256, 128
NCH = T // MC
POOL_W = (2, 4, 8, 16)
CONV = 5

MT_Q, MT_KC, MT_VC, MT_KS, MT_VS, MT_KW, MT_VW, MT_GATE = 0, 4, 5, 6, 7, 8, 9, 10
MT_GQ, MT_GK, MT_GV, MT_GR = 11, 13, 15, 19
MTILES = 23
DEEP = 3
POOL_ADDS = 5
SCORE_BANKS = (0, 1, 7)
MT_FIRST = MT_GATE + 1

FFN_UNITS = 2 * FT + FT
U_FFN1 = 0
U_PROJ = U_FFN1 + FFN_UNITS
U_MIXOUT = U_PROJ + MTILES
U_FFN2 = U_MIXOUT + DC
U_GATES = U_FFN2 + FFN_UNITS
HEAD_UNITS = 10
U_HEADS = U_GATES + 1
U_GB = U_HEADS + MH * HEAD_UNITS
U_PB = U_GB + DC
U_POOL = U_PB + DC
U_MIX2 = U_POOL + 2 * DC
U_PA = U_MIX2 + 2
U_OUT = U_PA + 2 * DC
NUNITS = U_OUT + DC

CONSTS = {}
_at = 0
for _name, _width in (("ident", P), ("ones", P), ("eps", 1), ("one", 1), ("dist", T), ("keep", T),
                      ("gmask", P), ("cvalid", TT * NCMP), ("slope", NH), ("upper", P), ("lower", P),
                      ):
    CONSTS[_name] = (_at, _width)
    _at += _width
CONST_COLS = _at

PARAMS = {}
_at = 0
for _name, _width in (("g_ffn1", DC), ("g_mix", DC), ("g_ffn2", DC), ("g_final", DC), ("g_pre", DC),
                      ("g_post", DC), ("b_a", 2), ("g_gla", 1), ("pool_scale", DC), ("conv_w", 16 * CONV),
                      ("conv_b", 16), ("g_mlstm", DC), ("b_merge", 2 * DC), ("b_if", 1), ("pe", 32),
                      ("w2", 2 * DH), ("w_a2", GH * GDK)):
    PARAMS[_name] = (_at, _width)
    _at += _width
PARAM_COLS = _at


class Chain:

    def __init__(self, engine, sem):
        self.engine, self.sem, self.n, self.offset = engine, sem, 0, 0

    def link(self, instruction):
        self.n += 1
        instruction.then_inc(self.sem, 1)
        self.engine.wait_ge(self.sem, self.n + self.offset)

    def enter(self, i, per):
        self.offset, self.per, self.first = i * per, per, self.n

    def leave(self, count):
        assert self.n - self.first == self.per, (self.n - self.first, self.per)
        self.n, self.offset = self.first + count * self.per, 0


def build(nc, dram, out):
    with ExitStack() as ctx:
        def sb(name, shape, dt=F32, scope=ctx):
            return scope.enter_context(nc.sbuf_tensor(name, shape, dt))

        def sem(name):
            return ctx.enter_context(nc.semaphore(name))

        ps = ctx.enter_context(nc.psum_tensor("ps", [P, 8, T], F32))
        x = sb("x", [P, DC, T])
        h_hi = sb("h_hi", [P, DC, T], F32R)
        h_lo = sb("h_lo", [P, DC, T], F32R)
        w_raw = sb("w_raw", [P, 2, D])
        w_hi = sb("w_hi", [P, 2, D], F32R)
        w_lo = sb("w_lo", [P, 2, D], F32R)
        scr = sb("scr", [P, DC, T])
        r_col = sb("r_col", [P, TT])
        spare = sb("spare", [P, 1])
        g_col = sb("g_col", [P, GH * TT])
        const = sb("const", [P, CONST_COLS])
        param = sb("param", [P, PARAM_COLS])

        def c_(name):
            at, width = CONSTS[name]
            return const[:, at:at + width]

        def p_(name, a=0, b=None):
            at, width = PARAMS[name]
            return param[:, at + a:at + (width if b is None else b)]

        ident, ones = c_("ident"), c_("ones")

        ffn = ExitStack()
        hid_hi = sb("hid_hi", [P, FT, T], F32R, ffn)
        hid_lo = sb("hid_lo", [P, FT, T], F32R, ffn)
        silu = sb("silu", [P, 2, T], F32, ffn)
        hid = sb("hid", [P, 2, T], F32, ffn)
        ffn.close()

        mixer = ExitStack()
        own = ExitStack()
        queries = sb("queries", [P, HPG, T], F32, own)
        own.close()
        o_hi = sb("o_hi", [P, HPG, T], F32R, mixer)
        proj = sb("proj", [P, MTILES - HPG, T], F32, mixer)
        v_tok = sb("v_tok", [P, TT, 2, NG * DH], F32, mixer)
        gate_tok = sb("gate_tok", [P, TT, 3 * NH], F32, mixer)
        o_lo = sb("o_lo", [P, HPG, T], F32R, mixer)
        nsa = ExitStack()
        w1 = sb("w1", [P, 2, CMP_BLOCK // 2, CMP_HID], F32, nsa)
        cbias = sb("cbias", [P, TT * NH * NCMP], F32, nsa)
        gel = sb("gel", [P, 2, NG * NCMP], F32, nsa)
        kc_t = sb("kc_t", [P, NCMP], F32, nsa)
        vc_tok = sb("vc_tok", [NCMP, NG, DH], F32, nsa)
        c_max = sb("c_max", [P, TT * NH], F32, nsa)
        c_sum = sb("c_sum", [P, TT * NH], F32, nsa)
        pc_t = sb("pc_t", [NCMP, NH, T], F32, nsa)
        pc_st = sb("pc_st", [NCMP, NG, T], F32, nsa)
        q_st = sb("q_st", [P, T], F32, nsa)
        bias = sb("bias", [P, NG, T], F32, nsa)
        nmax = sb("nmax", [P, DEEP], F32, nsa)
        psum_l = sb("psum_l", [P, DEEP], F32, nsa)
        nsa.close()
        gla = ExitStack()
        q_in = sb("q_in", [P, 2, T], F32, gla)
        k_in = sb("k_in", [P, 2, T], F32, gla)
        decay = sb("decay", [P, 2, T], F32, gla)
        kst_tok = sb("kst_tok", [P, TT, GH * GDK], F32, gla)
        gv_tok = sb("gv_tok", [P, TT, GH * GDV], F32, gla)
        intra = sb("intra", [P, 2, P], F32, gla)
        state = sb("state", [P, 2, 2, GDV], F32, gla)
        gla.close()
        mixer.close()

        second = ExitStack()
        y_hi = sb("y_hi", [P, DC, T], F32R, second)
        y_lo = sb("y_lo", [P, DC, T], F32R, second)
        merged = sb("merged", [P, DC, T], F32, second)
        heads = ExitStack()
        qk_pad = sb("qk_pad", [P, 2, T + CONV - 1], F32, heads)
        qk = sb("qk", [P, 4, T], F32, heads)
        k_tok = sb("k_tok", [P, NCH, MD], F32, heads)
        v_aug = sb("v_aug", [P, NCH, MD + P], F32, heads)
        d_mat = sb("d_mat", [P, 2, T], F32, heads)
        q_sc = sb("q_sc", [P, 2, 2, T], F32, heads)
        k_w = sb("k_w", [P, 2, MD], F32, heads)
        c_state = sb("c_state", [P, 2, 2, MD + P], F32, heads)
        h_sum = sb("h_sum", [P, 2, T], F32, heads)
        h_tmp = sb("h_tmp", [P, 2, P], F32, heads)
        den = sb("den", [P, 2, P], F32, heads)
        row_m = sb("row_m", [P, T], F32R, heads)
        row_i = sb("row_i", [P, T], F32R, heads)
        row_f = sb("row_f", [P, T], F32R, heads)
        edge = sb("edge", [64, 5, NCH], F32, heads)
        a_tok = sb("a_tok", [P, NCH, 64], F32, heads)
        wk_tok = sb("wk_tok", [P, NCH, 64], F32, heads)
        keep_bc = sb("keep_bc", [P, 2 * MH * NCH], F32, heads)
        sel = sb("sel", [P, 2, P], F32R, heads)
        heads.close()
        gate = sb("gate", [P, 2, T], F32, second)
        pooling = ExitStack()
        silu_z = sb("silu_z", [P, DC, T], F32, pooling)
        inv_count = sb("inv_count", [P, len(POOL_W), T], F32, pooling)
        u_pad = sb("u_pad", [P, 2, T + 16], F32, pooling)
        win = sb("win", [P, 2, T + 16], F32, pooling)
        pooling.close()
        m_hi = sb("m_hi", [P, DC, T], F32R, second)
        m_lo = sb("m_lo", [P, DC, T], F32R, second)
        second.close()

        dup = scr[:, 0:4, :]
        rows = scr[:, 4:8, :].rearrange("p a t -> p (a t)")[:, 0:2 * 16 * NG * NCMP].rearrange(
            "p (s l g n) -> p s l g n", s=2, l=16, g=NG)
        c_score = scr[:, 0:2, :].rearrange("p a t -> p (a t)")[:, 0:TT * NH * NCMP].rearrange(
            "p (q h n) -> p q h n", q=TT, h=NH)

        score, prob, prob_t = scr[:, 0:DEEP, :], scr[:, DEEP:2 * DEEP, :], scr[:, 2 * DEEP:2 * DEEP + 2, :]

        floor = scr[:, 6:8, :]
        rows_of = [d_mat[:, 0, :], d_mat[:, 1, :], h_sum[:, 0, :], h_sum[:, 1, :]] + [
            q_sc[:, k // 2, k % 2, :] for k in range(4)]
        raw_m, raw_i, raw_f = (rows_of[k][0:64] for k in (4, 6, 7))

        proj_done = sem("proj_done")
        w1_in = sem("w1_in")
        dup_in = sem("dup_in")
        tok_ready, tok_done = sem("tok_ready"), sem("tok_done")
        gate_done = sem("gate_done")
        rows_done = sem("rows_done")
        cmp_pe = sem("cmp_pe")
        gel_done = sem("gel_done")
        kvc_done = sem("kvc_done")
        cexp_ready, cexp_done, cprob_done = sem("cexp_ready"), sem("cexp_done"), sem("cprob_done")
        pct_done = [sem("pct_done_even"), sem("pct_done_odd")]
        stage_done, bias_done = sem("stage_done"), sem("bias_done")
        score_ready, neg_done, exp_done = sem("score_ready"), sem("neg_done"), sem("exp_done")
        prob_done, turn_ready, prob_t_done = sem("prob_done"), sem("turn_ready"), sem("prob_t_done")
        pv_done = sem("pv_done")
        o_hi_done, o_lo_done = sem("o_hi_done"), sem("o_lo_done")
        z_ready, gln_done, b_done, eb_done = sem("z_ready"), sem("gln_done"), sem("b_done"), sem("eb_done")
        kst_diff, kst_exp, kst_done = sem("kst_diff"), sem("kst_exp"), sem("kst_done")
        kst_turned, gv_turned = sem("kst_turned"), sem("gv_turned")
        kst_copied, gv_copied = sem("kst_copied"), sem("gv_copied")
        a_ready, a_done, a_used = sem("a_ready"), sem("a_done"), sem("a_used")
        add_ready, state_done = sem("add_ready"), sem("state_done")
        gsq_done, gssq_done, grms_done = sem("gsq_done"), sem("gssq_done"), sem("grms_done")
        grstd_done, gspread_done, gs_gated = sem("grstd_done"), sem("gspread_done"), sem("gs_gated")
        rl_done = sem("rl_done")
        pv_turn = sem("pv_turn")
        score_turn = sem("score_turn")
        gr_done, go_done, go_hi, go_lo = sem("gr_done"), sem("go_done"), sem("go_hi"), sem("go_lo")
        raw_full = [sem("raw_full0"), sem("raw_full1")]
        w_hi_done, w_lo_done = sem("w_hi_done"), sem("w_lo_done")
        unit_done = sem("unit_done")
        small_in = sem("small_in")
        x_in = [sem(f"x_in{c}") for c in range(DC // 2)]
        sq_done = sem("sq_done")
        pair_done = sem("pair_done")
        sqsum_done = sem("sqsum_done")
        ssq_done = sem("ssq_done")
        rms_done = sem("rms_done")
        rstd_done, spread_done = sem("rstd_done"), sem("spread_done")
        hn_done, hn_hi_done = sem("hn_done"), sem("hn_hi_done")
        hn_lo_done = [sem("hn_lo_even"), sem("hn_lo_odd")]
        down_done = sem("down_done")
        silu_done = sem("silu_done")
        hid_done, hid_hi_done, hid_lo_done = sem("hid_done"), sem("hid_hi_done"), sem("hid_lo_done")
        x_done = sem("x_done")
        dve_chain = sem("dve_chain")
        act_chain = sem("act_chain")
        out_sem = sem("out_sem")

        ITEMS = [(b, qt, g) for b in range(2) for qt in range(TT) for g in range(NG)]
        NI = len(ITEMS)
        HEADS_OF = [(h, h // 2, h % 2) for h in range(GH)]

        x_out, x_out_pool = sem("x_out"), sem("x_out_pool")
        rows_in, row_l = sem("rows_in"), sem("row_l")
        row_args, row_exp = sem("row_args"), sem("row_exp")
        edge_done, edge_exp = sem("edge_done"), sem("edge_exp")
        tokrow_ready, tokrow_done = sem("tokrow_ready"), sem("tokrow_done")
        ev_done = sem("ev_done")
        conv_done, qk_done = sem("conv_done"), sem("qk_done")
        kt_ready, kt_done = sem("kt_ready"), sem("kt_done")
        vt_ready, vt_done = sem("vt_ready"), sem("vt_done")
        sel_done = sem("sel_done")
        sc_ready, nm_ready, dlog_done = sem("sc_ready"), sem("nm_ready"), sem("dlog_done")
        dexp_done, sct_done = sem("dexp_done"), sem("sct_done")
        in_ready, qs_done, fl_ready, fl_done = sem("in_ready"), sem("qs_done"), sem("fl_ready"), sem("fl_done")
        kw_done, cadd_ready, c_done = sem("kw_done"), sem("cadd_ready"), sem("c_done")
        num_ready, num_done = sem("num_ready"), sem("num_done")
        hrstd_done, hspread_done = sem("hrstd_done"), sem("hspread_done")
        hsq_done, hssq_done, hrms_done = sem("hsq_done"), sem("hssq_done"), sem("hrms_done")
        og_done = sem("og_done")
        y_done, y_hi_done, y_lo_done = sem("y_done"), sem("y_hi_done"), sem("y_lo_done")
        mg_sig, mg_done = sem("mg_sig"), sem("mg_done")
        inv_in, upad_done, pool_done = sem("inv_in"), sem("upad_done"), sem("pool_done")
        m_hi_done, m_lo_done = sem("m_hi_done"), sem("m_lo_done")
        out_done, sum_done = sem("out_done"), sem("sum_done")
        EV_POOL = HEAD_UNITS * MH + DC
        STEPS = [(s, d) for s in range(NCH) for d in range(2)]

        FIRST_OF = [n for n, (s, d) in enumerate(STEPS) if s < NCH // 2]
        MLSTM_LINKS = 4 * (CONV - 1) + 3 * len(STEPS) + len(STEPS) // 2 + 2

        GATE_B_AT = [(), (0,), (), (1,), (2,), (3,), (4,), (), (5,), (6, 7)]

        GATE_B_AT_ACT = GATE_B_AT[:-1] + [(), GATE_B_AT[-1]]

        def chunk_of(s, d):
            return s if d == 0 else NCH - 1 - s

        def stream_tail(n, c):
            return hn_lo_done[c % 2], DC // 2 * n + c // 2 + 1

        block = ctx.enter_context(nc.Block())

        def unit(c, per=0, i=0):
            assert per % 2 == 0
            return c + per * i, c // 2 + per // 2 * i, c % 2

        @block.sync
        def _(sp):
            for c in range(0, DC, 2):
                sp.dma_start(x[:, c:c + 2, :], dram["x"][c * P:(c + 2) * P, :].rearrange("(a p) t -> p a t", p=P)
                             ).then_inc(x_in[c // 2], 16)
            for u in range(2):
                sp.dma_start(w_raw[:, u, :], dram["units"][u]).then_inc(raw_full[u], 16)
            with sp.Fori(1, (NUNITS + 1) // 2) as i:
                for slot in range(2):
                    sp.wait_ge(w_lo_done, 2 * i + slot - 1)
                    sp.dma_start(w_raw[:, slot, :],
                                 dram["units"][bass.ds(2 * i + slot, 1)].rearrange("u p n -> p (u n)")
                                 ).then_inc(raw_full[slot], 16)
            for c in range(DC):
                if c < POOL_ADDS:
                    sp.wait_ge(x_out_pool, c + 1)
                else:
                    sp.wait_ge(x_out, c - POOL_ADDS + 1)
                sp.dma_start(out[c * P:(c + 1) * P, :], x[:, c, :]).then_inc(out_sem, 16)
            sp.wait_ge(out_sem, 16 * DC)

        @block.gpsimd
        def _(pool):
            def tail(u, slot):
                pool.wait_ge(w_hi_done, u + 1)
                nc.gpsimd.tensor_tensor(w_lo[:, slot, :], w_raw[:, slot, :], w_hi[:, slot, :].bitcast(F32),
                                        ALU.subtract).then_inc(w_lo_done, 1)

            def tails(first, end):
                if first % 2:
                    tail(first, 1)
                    first += 1
                with pool.Fori(first // 2, end // 2) as i:
                    for slot in range(2):
                        tail(2 * i + slot, slot)
                if end % 2:
                    tail(end - 1, 0)

            def stream_tails(n):
                for c in range(1, DC, 2):
                    pool.wait_ge(hn_hi_done, DC * n + c + 1)
                    nc.gpsimd.tensor_tensor(h_lo[:, c, :], scr[:, c, :], h_hi[:, c, :].bitcast(F32), ALU.subtract
                                            ).then_inc(hn_lo_done[1], 1)

            def pair_sums(n):
                for c in (4, 6):
                    pool.wait_ge(sq_done, DC * n + c + 2)
                    nc.gpsimd.tensor_tensor(scr[:, c, :], scr[:, c, :], scr[:, c + 1, :], ALU.add).then_inc(pair_done, 1)

            pair_sums(0)
            tails(U_FFN1, U_FFN1 + 2)
            stream_tails(0)
            tails(U_FFN1 + 2, U_PROJ + 2)
            stream_tails(1)
            tails(U_PROJ + 2, U_FFN2 + 2)
            stream_tails(2)
            tails(U_FFN2 + 2, U_GATES + 2)
            pair_sums(4)
            stream_tails(3)
            tails(U_GATES + 2, NUNITS)
            for c in range(POOL_ADDS):
                pool.wait_ge(sum_done, c + 1)
                nc.gpsimd.tensor_tensor(x[:, c, :], x[:, c, :], scr[:, c, :], ALU.add).then_inc(x_out_pool, 1)

        @block.tensor
        def _(pe):
            def tile_unit(un, bank, hi, lo, chunks=None):
                u, _, slot = un
                pe.wait_ge(w_lo_done, u + 1)
                for k in range(DC):
                    if chunks is not None:
                        pe.wait_ge(*chunks(k))
                    mm = block_of_unit(slot, bank, hi, lo, k)
                mm.then_inc(unit_done, 1)

            def block_of_unit(slot, bank, hi, lo, k):
                whi, wlo = w_hi[:, slot, k * P:(k + 1) * P], w_lo[:, slot, k * P:(k + 1) * P]
                nc.tensor.matmul(ps[:, bank, :], whi, hi[:, k, :], start=(k == 0), stop=False)
                nc.tensor.matmul(ps[:, bank, :], whi, lo[:, k, :], start=False, stop=False)
                return nc.tensor.matmul(ps[:, bank, :], wlo, hi[:, k, :], start=False, stop=(k == DC - 1))

            def add_squares(bank, col, squares, first, last):
                for q in range(TT):
                    mm = nc.tensor.matmul(ps[:, bank, col + q:col + q + 1], squares[:, q * P:(q + 1) * P], ones[:, 0:1],
                                          start=(first and q == 0), stop=last, skip_group_check=True)
                return mm

            def spread_columns(bank, columns):
                for q in range(TT):
                    mm = nc.tensor.matmul(ps[:, bank, q * P:(q + 1) * P], columns[:, q:q + 1].to_broadcast([P, P]),
                                          ident, start=True, stop=True)
                return mm

            def squares_of_half(n, first):
                pe.wait_ge(sqsum_done, n + 1)
                return add_squares(0, 0, scr[:, 0, :], first, not first)

            def norm(n, sum_at):
                if sum_at == "last":
                    for k in range(2):
                        pe.wait_ge(pair_done, (2 if n else 0) + k + 1)
                        add_squares(0, 0, scr[:, 4 + 2 * k, :], k == 0, False)
                    mm = squares_of_half(n, False)
                else:
                    if sum_at == "first":
                        squares_of_half(n, True)
                    for c in range(DC // 2, DC):
                        pe.wait_ge(sq_done, DC * n + c + 1)
                        mm = add_squares(0, 0, scr[:, c, :], False, c == DC - 1)
                mm.then_inc(ssq_done, 1)
                pe.wait_ge(rstd_done, n + 1)
                spread_columns(1, r_col).then_inc(spread_done, 1)

            def ffn(u0, n, norm_of):
                def pair(i, chunks=None):
                    for f in range(2):
                        pe.wait_ge(hid_done, FT * n + 2 * i + f + 1)
                        for m in range(2):
                            tile_unit(unit(u0 + 2 * f + m, 4, i), 4 + 2 * f + m, h_hi, h_lo,
                                      chunks if f == m == 0 else None)

                pair(0, lambda k: stream_tail(norm_of, k))
                with pe.Fori(1, FT // 2) as i:
                    pair(i)

                def down(un, kp, half, start=False, stop=False):
                    u, _, slot = un
                    pe.wait_ge(w_lo_done, u + 1)
                    moving = [(hid_hi[:, bass.ds(2 * kp + kk, 1), :].rearrange("p a t -> p (a t)"),
                               hid_lo[:, bass.ds(2 * kp + kk, 1), :].rearrange("p a t -> p (a t)")) for kk in range(2)]
                    order = [(kk, dd) for kk in range(2) for dd in range(4)]
                    ending = stop
                    if ending:
                        order.sort(key=lambda step: step[1])
                    for kk, dd in order:
                        at, (mv_hi, mv_lo) = (kk * 4 + dd) * P, moving[kk]
                        acc = ps[:, half * 4 + dd, :]
                        nc.tensor.matmul(acc, w_hi[:, slot, at:at + P], mv_hi, start=start and kk == 0, stop=False)
                        nc.tensor.matmul(acc, w_hi[:, slot, at:at + P], mv_lo, start=False, stop=False)
                        mm = nc.tensor.matmul(acc, w_lo[:, slot, at:at + P], mv_hi, start=False,
                                              stop=stop and kk == 1)
                        if stop and kk == 1 and dd < 3:
                            mm.then_inc(down_done, 1)
                    mm.then_inc(unit_done, 1)

                ud = u0 + 2 * FT
                kps = FT // 2
                pe.wait_ge(hid_lo_done, FT * (n + 1) - 2)
                for j in range(2):
                    down(unit(ud + j), j, 0, start=(j == 0))
                with pe.Fori(1, kps // 2) as i:
                    for j in range(2):
                        down(unit(ud + j, 2, i), 2 * i + j, 0)
                pe.wait_ge(hid_lo_done, FT * (n + 1))
                down(unit(ud + kps - 1), kps - 1, 0, stop=True)
                down(unit(ud + kps), 0, 1, start=True)
                with pe.Fori(0, kps // 2 - 1) as i:
                    for j in range(2):
                        down(unit(ud + kps + 1 + j, 2, i), 2 * i + j + 1, 1)
                down(unit(ud + 2 * kps - 2), kps - 2, 1)
                squares_of_half(norm_of + 1, True)
                down(unit(ud + 2 * kps - 1), kps - 1, 1, stop=True)

            def project_one(t, bank):
                pe.wait_ge(proj_done, t + 1)
                tile_unit(unit(U_PROJ + t), bank, h_hi, h_lo)

            def project():
                def two(i, chunks=None):
                    for j in range(2):
                        pe.wait_ge(proj_done, 2 * i + j + 1)
                        tile_unit(unit(U_PROJ + j, 2, i), 2 + j, h_hi, h_lo, chunks if j == 0 else None)

                two(0, lambda k: stream_tail(1, k))
                with pe.Fori(1, MT_FIRST // 2) as i:
                    two(i)
                project_one(MT_FIRST - 1, 2)

            def compressed():
                pe.wait_ge(proj_done, 2 + MT_FIRST)
                for tt in range(TT):
                    at = slice(tt * P, (tt + 1) * P)
                    nc.tensor.transpose(ps[:, 4, tt * 3 * NH:(tt + 1) * 3 * NH], proj[0:3 * NH, MT_GATE - HPG, at],
                                        ident[0:3 * NH, 0:3 * NH])
                    nc.tensor.transpose(ps[:, 5, at], proj[:, MT_VS - HPG, at], ident)
                    mm = nc.tensor.transpose(ps[:, 6, at], proj[:, MT_VW - HPG, at], ident)
                mm.then_inc(tok_ready, 1)
                project_one(MT_GQ, 3)
                pe.wait_ge(w1_in, 32)
                for s in range(2):
                    for lp in range(CMP_BLOCK // 2):
                        if lp == 0:
                            pe.wait_ge(rows_done, s + 1)
                        mm = nc.tensor.matmul(ps[:, 7 - 6 * s, 0:NG * NCMP], w1[:, s, lp, :],
                                              rows[:, s, lp, :, :].rearrange("p g n -> p (g n)"),
                                              start=(lp == 0), stop=(lp == CMP_BLOCK // 2 - 1))
                    mm.then_inc(cmp_pe, 1)
                project_one(MT_GQ + 1, 2)
                pe.wait_ge(gel_done, 1)
                for g in range(NG):
                    at = slice(g * NCMP, (g + 1) * NCMP)
                    nc.tensor.matmul(ps[g * DH:(g + 1) * DH, 0, 0:NCMP], p_("w2", 0, DH), gel[:, 0, at],
                                     start=True, stop=True)
                pe.wait_ge(gel_done, 2)
                for g in range(NG):
                    at = slice(g * NCMP, (g + 1) * NCMP)
                    mm = nc.tensor.matmul(ps[0:NCMP, 1, g * DH:(g + 1) * DH], gel[:, 1, at], p_("w2", DH, 2 * DH),
                                          start=True, stop=True)
                mm.then_inc(cmp_pe, 1)
                project_one(MT_GK, 3)
                pe.wait_ge(proj_done, 2 + MT_GK + 1)
                pe.wait_ge(kvc_done, 1)
                for qt in range(TT):
                    for h in range(NH):
                        g, j = h // HPG, h % HPG
                        r = slice(g * DH, (g + 1) * DH)
                        at = (qt * HPG + j) * 32
                        mm = nc.tensor.matmul(ps[:, 2 + g, at:at + NCMP], queries[r, j, qt * P:(qt + 1) * P],
                                              kc_t[r, :], start=True, stop=True)
                mm.then_inc(cmp_pe, 1)
                project_one(MT_GK + 1, 0)
                pe.wait_ge(cprob_done, 1)
                pe.wait_ge(tok_done, 3)
                for h in range(NH):
                    if h >= 4:
                        pe.wait_ge(pct_done[h % 2], h // 2 - 1)
                    for qt in range(TT):
                        mm = nc.tensor.transpose(ps[0:NCMP, 4 + h % 4, qt * P:(qt + 1) * P], c_score[:, qt, h, :], ident)
                    mm.then_inc(cmp_pe, 1)

            def attention():
                with pe.Fori(0, HPG) as j:
                    def scores(n):
                        b, qt, g = ITEMS[n]
                        r, w = slice(g * DH, (g + 1) * DH), (qt + 1) * P
                        if n >= DEEP:
                            pe.wait_ge(neg_done, NI * j + n - DEEP + 1)
                        mm = nc.tensor.matmul(ps[:, SCORE_BANKS[n % DEEP], 0:w], q_st[r, qt * P:(qt + 1) * P],
                                              proj[r, (MT_KS, MT_KW)[b] - HPG, 0:w], start=True, stop=True)
                        mm.then_inc(score_ready, 1)

                    def turn(n):
                        b, qt, g = ITEMS[n]
                        pe.wait_ge(prob_done, NI * j + n + 1)
                        if n >= 2:
                            pe.wait_ge(prob_t_done, NI * j + n - 1)
                        for kt in range(qt + 1):
                            at = slice(kt * P, (kt + 1) * P)
                            mm = nc.tensor.transpose(ps[:, 2 + n % 2, at], prob[:, n % DEEP, at], ident)
                        mm.then_inc(turn_ready, 1)

                    def values(n):
                        b, qt, g = ITEMS[n]
                        pe.wait_ge(prob_t_done, NI * j + n + 1)
                        for kt in range(qt + 1):
                            mm = nc.tensor.matmul(ps[g * DH:(g + 1) * DH, 4, qt * P:(qt + 1) * P],
                                                  v_tok[:, kt, b, g * DH:(g + 1) * DH],
                                                  prob_t[:, n % 2, kt * P:(kt + 1) * P],
                                                  start=False, stop=False, skip_group_check=True)
                        mm.then_inc(pv_done, 1)

                    pe.wait_ge(stage_done, j + 1)
                    for n in range(DEEP):
                        scores(n)
                    pe.wait_ge(o_lo_done, j + 1)
                    for g in range(NG):
                        nc.tensor.matmul(ps[g * DH:(g + 1) * DH, 4, :], vc_tok[:, g, :], pc_st[:, g, :],
                                         start=True, stop=False, skip_group_check=True)
                    for n in range(NI):
                        turn(n)
                        if n + DEEP < NI:
                            scores(n + DEEP)
                        u, _, slot = unit(U_PROJ + MT_GV + n // DC, 2, j)
                        if n % DC == 0:
                            pe.wait_ge(proj_done, MT_GV + 2 * j + n // DC + 1)
                            pe.wait_ge(w_lo_done, u + 1)
                        mm = block_of_unit(slot, 5 + n // DC, h_hi, h_lo, n % DC)
                        if n % DC == DC - 1:
                            mm.then_inc(unit_done, 1)
                        if n >= 1:
                            values(n - 1)
                    values(NI - 1)

            def linear():
                pe.wait_ge(proj_done, 2 + MTILES)
                r = slice(32, 32 + LOWR)
                for m in range(2):
                    nc.tensor.matmul(ps[:, 6 + m, :], p_("w_a2", m * P, (m + 1) * P)[r], proj[r, MT_GATE - HPG, :],
                                     start=True, stop=True).then_inc(z_ready, 1)
                for h in range(GH):
                    for tt in range(TT):
                        at = slice(tt * P, (tt + 1) * P)
                        mm = nc.tensor.transpose(ps[:, h, at], proj[:, MT_GV - HPG + h, at], ident)
                    mm.then_inc(gv_turned, 1)
                pe.wait_ge(o_lo_done, HPG + 1)
                for m in range(2):
                    pe.wait_ge(kst_done, m + 1)
                    for tt in range(TT):
                        at = slice(tt * P, (tt + 1) * P)
                        mm = nc.tensor.transpose(ps[:, 4 + m, at], scr[:, 4 * m, at], ident)
                    mm.then_inc(kst_turned, 1)
                pe.wait_ge(gv_copied, GH)
                pe.wait_ge(kst_copied, 2)
                for tt in range(TT):
                    tok = slice(tt * P, (tt + 1) * P)
                    for h, m, half in HEADS_OF:
                        n = tt * GH + h
                        r = slice(half * GDK, (half + 1) * GDK)
                        if n >= 2:
                            pe.wait_ge(a_done, n - 1)
                        nc.tensor.matmul(ps[:, n % 2, 0:P], k_in[r, m, tok], q_in[r, m, tok],
                                         start=True, stop=True).then_inc(a_ready, 1)
                        if h >= 1:
                            gla_intra(tt, h - 1)
                    gla_intra(tt, GH - 1)
                    for c in range(2):
                        n = 2 * tt + c
                        if n < T // GC - 1:
                            if n >= 2:
                                pe.wait_ge(state_done, n - 1)
                            ck = slice(c * GC, (c + 1) * GC)
                            for h, m, half in HEADS_OF:
                                r = slice(half * GDK, (half + 1) * GDK)
                                mm = nc.tensor.matmul(ps[r, 2 + n % 2, m * GDV:(m + 1) * GDV],
                                                      kst_tok[ck, tt, m * P + half * GDK:m * P + (half + 1) * GDK],
                                                      gv_tok[ck, tt, h * GDV:(h + 1) * GDV], start=True, stop=True)
                            mm.then_inc(add_ready, 1)
                        if n >= 1:
                            pe.wait_ge(state_done, n)
                            for h, m, half in HEADS_OF:
                                r = slice(half * GDK, (half + 1) * GDK)
                                at = slice(n * GC, (n + 1) * GC)
                                mm = nc.tensor.matmul(ps[:, 4 + h, at], state[r, m, n % 2, :], q_in[r, m, at],
                                                      start=False, stop=False, skip_group_check=True)
                            mm.then_inc(a_used, 1)
                for h in range(GH):
                    pe.wait_ge(gsq_done, h + 1)
                    mm = add_squares(0, h * TT, scr[:, h, :], h == 0, True)
                mm.then_inc(gssq_done, 1)
                pe.wait_ge(grstd_done, 1)
                for h in range(GH):
                    pe.wait_ge(gs_gated, h + 1)
                    spread_columns(4 + h, g_col[:, h * TT:(h + 1) * TT]).then_inc(gspread_done, 1)

            def gla_intra(tt, h):
                n = tt * GH + h
                pe.wait_ge(a_done, n + 1)
                nc.tensor.matmul(ps[:, 4 + h, tt * P:(tt + 1) * P], gv_tok[:, tt, h * GDV:(h + 1) * GDV],
                                 intra[:, n % 2, :], start=(tt == 0), stop=False, skip_group_check=True
                                 ).then_inc(pv_done, 1)

            class Joined:
                def __init__(self, first, second):
                    self.first, self.second = first, second

                def __getitem__(self, at):
                    return (self.first if at[1] < HPG else self.second)[at]

            def to_stream(u0, n, hi, lo, ready):
                def two(i, chunks=None):
                    for j in range(2):
                        pe.wait_ge(x_done, DC * n + 2 * i + j - 1)
                        tile_unit(unit(u0 + j, 2, i), 2 + j, hi, lo, chunks if j == 0 else None)

                two(0, ready)
                with pe.Fori(1, DC // 2) as i:
                    two(i)

            def gates():
                pe.wait_ge(ssq_done, 5)
                tile_unit(unit(U_GATES), 4, h_hi, h_lo, lambda k: stream_tail(3, k))

            def turn_rows():
                pe.wait_ge(row_args, 1)
                pe.wait_ge(row_exp, 1)
                for n, (src, bank) in enumerate(((rows_of[3][0:64], 5), (rows_of[2][0:64], 6))):
                    for c in range(NCH):
                        mm = nc.tensor.transpose(ps[:, bank, c * 64:(c + 1) * 64], src[:, c * MC:(c + 1) * MC],
                                                 ident[0:64, 0:64])
                    mm.then_inc(tokrow_ready, 1)
                pe.wait_ge(edge_exp, 1)
                for d in range(2):
                    for h in range(MH):
                        r, at = 32 * d + h, (d * MH + h) * NCH
                        mm = nc.tensor.matmul(ps[:, 7, at:at + NCH], ident[0:64, r:r + 1].to_broadcast([64, P]),
                                              edge[:, 4, :], start=True, stop=True)
                mm.then_inc(tokrow_ready, 1)

            def mlstm(h, units=True, core=True):
                p = h - 1

                def project(j):
                    if units:
                        pe.wait_ge(ev_done, HEAD_UNITS * h + j + 1)
                        tile_unit(unit(U_HEADS + j, HEAD_UNITS, h), j % 2, h_hi, h_lo)
                    for i in () if units else GATE_B_AT[j]:
                        pe.wait_ge(ev_done, HEAD_UNITS * MH + i + 1)
                        tile_unit(unit(U_GB + i), i % 2, h_hi, h_lo)
                        if i == 6:
                            spread_roots()

                def turn_keys_values():
                    pe.wait_ge(hrms_done, p + 1)
                    pe.wait_ge(qk_done, 4 * p + 4)
                    for e in range(2):
                        for c in range(NCH):
                            at = slice(c * MC, (c + 1) * MC)
                            mm = nc.tensor.transpose(ps[:, 2 + e, at], qk[:, 2 + e, at], ident)
                        mm.then_inc(kt_ready, 1)
                    for e in range(2):
                        for c in range(NCH):
                            at = slice(c * MC, (c + 1) * MC)
                            mm = nc.tensor.transpose(ps[:, 4 + e, at], scr[:, e, at], ident)
                        mm.then_inc(vt_ready, 1)
                    for c in range(NCH):
                        at = slice(c * MC, (c + 1) * MC)
                        for e in range(2):
                            mm = nc.tensor.matmul(ps[:, 6, at], qk[:, 2 + e, at], qk[:, e, at],
                                                  start=(c == 0 and e == 0), stop=False, skip_group_check=True)
                    mm.then_inc(sc_ready, 1)

                def spread_rows(d):
                    pe.wait_ge(kt_done, 2 * p + 2)
                    pe.wait_ge(sel_done, p + 1)
                    if d:
                        pe.wait_ge(dlog_done, 2 * p + 1)
                    nc.tensor.matmul(ps[:, 7, :], sel[:, d, :], row_m[:, :], start=True, stop=True).then_inc(nm_ready, 1)
                    if d:
                        pe.wait_ge(qs_done, 2 * p + 1)
                    nc.tensor.matmul(ps[:, 2, :], sel[:, d, :], row_i[:, :], start=True, stop=True).then_inc(in_ready, 1)
                    if d:
                        pe.wait_ge(fl_done, 2 * p + 1)
                    nc.tensor.matmul(ps[:, 3, :], sel[:, d, :], row_f[:, :], start=True, stop=True).then_inc(fl_ready, 1)

                def step(n):
                    s, d = STEPS[n]
                    c = chunk_of(s, d)
                    if n == 0:
                        pe.wait_ge(vt_done, 2 * p + 2)
                        pe.wait_ge(sct_done, 2 * p + 2)
                    if s < NCH - 1:
                        pe.wait_ge(kw_done, 6 * p + n + 1)
                        if n:
                            pe.wait_ge(c_done, 6 * p + n)
                        for e in range(2):
                            mm = nc.tensor.matmul(ps[:, 4 + e, 0:MD + P], k_w[:, d, e * P:(e + 1) * P], v_aug[:, c, :],
                                                  start=True, stop=True)
                        mm.then_inc(cadd_ready, 1)
                    if s == 0:
                        pe.wait_ge(qs_done, 2 * p + d + 1)
                    if n >= 2:
                        pe.wait_ge(num_done, 8 * p + n - 1)
                    at = slice(c * MC, (c + 1) * MC)
                    for e in range(3):
                        o = ps[:, 6 + d, e * P:(e + 1) * P]
                        mm = nc.tensor.matmul(o, v_aug[:, c, e * P:(e + 1) * P], d_mat[:, d, at], start=(e == 0),
                                              stop=False, skip_group_check=True)
                        for f in range(2 if s else 0):
                            mm = nc.tensor.matmul(o, c_state[:, d, f, e * P:(e + 1) * P], q_sc[:, d, f, at],
                                                  start=False, stop=False, skip_group_check=True)
                    mm.then_inc(num_ready, 1)

                def sum_squares():
                    pe.wait_ge(num_done, 8 * p + 8)
                    for e in range(2):
                        pe.wait_ge(hsq_done, 2 * p + e + 1)
                        mm = add_squares(3, 0, d_mat[:, e, :], e == 0, e == 1)
                    mm.then_inc(hssq_done, 1)

                def spread_roots():
                    pe.wait_ge(hrstd_done, p + 1)
                    spread_columns(7, r_col).then_inc(hspread_done, 1)

                between = {0: [turn_keys_values], 1: [lambda: spread_rows(0)], 2: [lambda: spread_rows(1)],
                           3: [], 4: [lambda: step(0), lambda: step(1)], 5: [lambda: step(2), lambda: step(3)],
                           6: [lambda: step(4)], 7: [lambda: step(5)], 8: [lambda: step(6), lambda: step(7)],
                           9: [sum_squares]}
                for j in range(HEAD_UNITS):
                    for part in between[j] if core else ():
                        part()
                    if not core and j == HEAD_UNITS - 1:
                        turn_rows()
                    project(j)
                if core and units:
                    spread_roots()

            def merge_b():
                pe.wait_ge(y_lo_done, DC)
                with pe.Fori(0, DC // 2) as i:
                    for j in range(2):
                        pe.wait_ge(mg_done, 2 * i + j + 1)
                        tile_unit(unit(U_PB + j, 2, i), 5 + 2 * j, y_hi, y_lo)

            def merge_a():
                with pe.Fori(0, DC // 2) as i:
                    for j in range(2):
                        pe.wait_ge(mg_done, DC + 2 * i + j + 1)
                        tile_unit(unit(U_PA + 2 * j, 4, i), 4 + 2 * j, h_hi, h_lo)
                        pe.wait_ge(y_lo_done, 3 * DC)
                        tile_unit(unit(U_PA + 2 * j + 1, 4, i), 5 + 2 * j, y_hi, y_lo)

            def pooled():
                with pe.Fori(0, DC) as i:
                    for j in range(2):
                        pe.wait_ge(ev_done, EV_POOL + 2 * i + j + 1)
                        tile_unit(unit(U_POOL + j, 2, i), 2 + j, h_hi, h_lo)
                pe.wait_ge(mg_done, DC + 2)
                pe.wait_ge(ev_done, EV_POOL + 2 * DC + 2)
                pe.wait_ge(y_lo_done, 2 * DC)
                for n in range(2):
                    u, _, slot = unit(U_MIX2 + n)
                    pe.wait_ge(w_lo_done, u + 1)
                    for g in range(2):
                        for dt in range(2):
                            for ck in range(2):
                                at = (g * 4 + dt * 2 + ck) * P
                                src, acc = (2 * n + g) * 2 + ck, ps[:, 4 - 4 * n + 2 * g + dt, :]
                                whi, wlo = w_hi[:, slot, at:at + P], w_lo[:, slot, at:at + P]
                                nc.tensor.matmul(acc, whi, y_hi[:, src, :], start=(ck == 0), stop=False)
                                nc.tensor.matmul(acc, whi, y_lo[:, src, :], start=False, stop=False)
                                mm = nc.tensor.matmul(acc, wlo, y_hi[:, src, :], start=False, stop=(ck == 1))
                    mm.then_inc(unit_done, 1)
                pe.wait_ge(y_done, DC + 4)

            def output():
                pe.wait_ge(mg_done, 2 * DC + 2)
                def two(i, chunks=None):
                    for j in range(2):
                        pe.wait_ge(out_done, 2 * i + j + 1)
                        tile_unit(unit(U_OUT + j, 2, i), 2 + j, m_hi, m_lo, chunks if j == 0 else None)

                two(0, lambda k: (m_lo_done, k + 1))
                with pe.Fori(1, DC // 2) as i:
                    two(i)
                norm(5, "first")

            pe.wait_ge(small_in, 32)
            norm(0, "last")
            ffn(U_FFN1, 0, 0)
            norm(1, "before")
            project()
            compressed()
            attention()
            linear()
            to_stream(U_MIXOUT, 2, Joined(o_hi, h_hi), Joined(o_lo, h_lo), lambda k: (o_lo_done, 5) if k < 4 else (go_lo, k - 3))
            norm(2, "first")
            ffn(U_FFN2, 1, 2)
            norm(3, "before")
            norm(4, "last")
            gates()
            mlstm(0, core=False)
            pe.wait_ge(tokrow_done, 1)
            with pe.Fori(1, MH) as h:
                mlstm(h)
            mlstm(MH, units=False)
            merge_b()
            pooled()
            merge_a()
            output()

        @block.scalar
        def _(act):
            def head(un):
                u, turn, slot = un
                act.wait_ge(raw_full[slot], 16 * (turn + 1))
                act.wait_ge(unit_done, u - 1)
                nc.scalar.activation(w_hi[:, slot, :], w_raw[:, slot, :], ACT.Copy).then_inc(w_hi_done, 1)

            def load_root():
                nc.scalar.activation(spare[:, :], c_("one"), ACT.Sqrt)

            def squares(n, lo, hi):
                for c in range(lo, hi):
                    if n:
                        act.wait_ge(x_done, DC * n + c + 1)
                    else:
                        act.wait_ge(x_in[c // 2], 16)
                    nc.scalar.activation(scr[:, c, :], x[:, c, :], ACT.Square).then_inc(sq_done, 1)

            def norm(n, parts=True, at=None):
                at = n if at is None else at
                act.wait_ge(ssq_done, n + 1)
                nc.scalar.activation(r_col[:, :], ps[:, 0, 0:TT], ACT.Sqrt, scale=1.0 / D, bias=c_("eps")).then_inc(rms_done, 1)
                for c in range(DC if parts else 0):
                    act.wait_ge(hn_done, DC * at + c + 1)
                    nc.scalar.activation(h_hi[:, c, :], scr[:, c, :], ACT.Copy).then_inc(hn_hi_done, 1)

            def ffn(u0, n, next_norm):
                with act.Fori(0, FT // 2) as i:
                    for f in range(2):
                        head(unit(u0 + 2 * f + 2, 4, i))
                        act.wait_ge(unit_done, u0 + 4 * i + 2 * f + 1)
                        act.wait_ge(hid_done, FT * n + 2 * i + f + 1)
                        nc.scalar.activation(silu[:, f, :], ps[:, 4 + 2 * f, :], ACT.Silu).then_inc(silu_done, 1)
                        head(unit(u0 + 2 * f + 3, 4, i))
                        act.wait_ge(hid_done, FT * n + 2 * i + f + 3)
                        nc.scalar.activation(hid_hi[:, bass.ds(2 * i + f, 1), :].rearrange("p a t -> p (a t)"),
                                             hid[:, f, :], ACT.Copy).then_inc(hid_hi_done, 1)
                ud = u0 + 2 * FT
                kps = FT // 2
                with act.Fori(0, kps // 2) as i:
                    for j in range(2):
                        head(unit(ud + 2 + j, 2, i))
                head(unit(ud + kps + 1))
                squares(next_norm, 0, 4)
                head(unit(ud + kps + 2))
                with act.Fori(0, kps // 2 - 1) as i:
                    for j in range(2):
                        head(unit(ud + kps + 3 + j, 2, i))
                head(unit(ud + 2 * kps))
                load_root()
                squares(next_norm, 4, 8)
                head(unit(ud + 2 * kps + 1))

            def project():
                act.wait_ge(unit_done, U_PROJ)
                act.dma_start(w1[:, :, :, :].rearrange("p s l n -> p (s l n)"), dram["w1"]).then_inc(w1_in, 16)
                act.dma_start(cbias[:, :], dram["cbias"]).then_inc(w1_in, 16)

                def two(i, dst, first, scale):
                    for j in range(2):
                        head(unit(U_PROJ + j + 2, 2, i))
                        act.wait_ge(unit_done, U_PROJ + 2 * i + j + 1)
                        nc.scalar.activation(dst[:, bass.ds(2 * i + j - first, 1), :].rearrange("p a t -> p (a t)"),
                                             ps[:, 2 + j, :], ACT.Copy, scale=scale).then_inc(proj_done, 1)

                with act.Fori(0, MT_KC // 2) as i:
                    two(i, queries, 0, DH ** -0.5)
                with act.Fori(MT_KC // 2, MT_FIRST // 2) as i:
                    two(i, proj, HPG, 1.0)
                take(MT_FIRST - 1, 2)

            def take(t, bank, scale=1.0):
                head(unit(U_PROJ + t + 2))
                act.wait_ge(unit_done, U_PROJ + t + 1)
                nc.scalar.activation(proj[:, t - HPG, :], ps[:, bank, :], ACT.Copy, scale=scale).then_inc(proj_done, 1)

            def compressed():
                act.wait_ge(hn_lo_done[0], DC)
                act.wait_ge(hn_lo_done[1], DC)
                act.wait_ge(proj_done, 2 + MT_FIRST)
                for s in range(2):
                    for g in range(NG):
                        for half in range(2):
                            act.dma_start(dup[half * DH:(half + 1) * DH, 2 * s + g, :],
                                          proj[g * DH:(g + 1) * DH, MT_KC - HPG + s, :]).then_inc(dup_in, 16)
                act.wait_ge(tok_ready, 1)
                nc.scalar.activation(gate_tok[:, :, :].rearrange("p q c -> p (q c)"), ps[:, 4, 0:TT * 3 * NH],
                                     ACT.Sigmoid).then_inc(gate_done, 1)
                take(MT_GQ, 3, DH ** -0.5)
                for s in range(2):
                    act.wait_ge(cmp_pe, s + 1)
                    nc.scalar.activation(gel[:, s, :], ps[:, 7 - 6 * s, 0:NG * NCMP],
                                         ACT.Gelu_apprx_tanh).then_inc(gel_done, 1)
                take(MT_GQ + 1, 2, DH ** -0.5)
                take(MT_GK, 3)
                act.wait_ge(cexp_ready, 1)
                flat = c_score.rearrange("p q h n -> p (q h n)")
                nc.scalar.activation(flat, flat, ACT.Exp).then_inc(cexp_done, 1)
                take(MT_GK + 1, 0)
                for h in range(1, NH, 2):
                    act.wait_ge(cmp_pe, 5 + h)
                    nc.scalar.activation(pc_t[:, h, :], ps[0:NCMP, 4 + h % 4, :], ACT.Copy).then_inc(pct_done[1], 1)

            def attention():
                with act.Fori(0, HPG) as j:
                    act.wait_ge(pct_done[0], NH // 2)
                    act.wait_ge(pct_done[1], NH // 2)
                    nc.scalar.activation(q_st[:, :], queries[:, bass.ds(j, 1), :].rearrange("p a t -> p (a t)"),
                                         ACT.Copy)
                    nc.scalar.activation(
                        pc_st[:, :, :], pc_t[:, :, :].rearrange("p (g j) t -> p g j t", g=NG)[:, :, bass.ds(j, 1), :]
                        .rearrange("p g a t -> p g (a t)"), ACT.Copy).then_inc(stage_done, 1)

                    def copy(n):
                        w = (ITEMS[n][1] + 1) * P
                        act.wait_ge(turn_ready, NI * j + n + 1)
                        if n >= 2:
                            act.wait_ge(pv_done, NI * j + n - 1)
                        nc.scalar.activation(prob_t[:, n % 2, 0:w], ps[:, 2 + n % 2, 0:w], ACT.Copy
                                             ).then_inc(prob_t_done, 1)

                    def take_beside(k):
                        head(unit(U_PROJ + MT_GV + k + 2, 2, j))
                        act.wait_ge(unit_done, U_PROJ + MT_GV + 2 * j + k + 1)
                        nc.scalar.activation(proj[:, bass.ds(MT_GV - HPG + 2 * j + k, 1), :].rearrange("p a t -> p (a t)"),
                                             ps[:, 5 + k, :], ACT.Copy).then_inc(proj_done, 1)

                    for n in range(NI):
                        w = (ITEMS[n][1] + 1) * P
                        if n == DC + 1:
                            take_beside(0)
                        act.wait_ge(neg_done, NI * j + n + 1)
                        r = n % DEEP
                        if n >= DEEP:
                            act.wait_ge(turn_ready, NI * j + n - DEEP + 1)
                        nc.scalar.activation(prob[:, r, 0:w], score[:, r, 0:w], ACT.Exp, scale=-1.0,
                                             bias=nmax[:, r:r + 1], accum_out=psum_l[:, r:r + 1]).then_inc(exp_done, 1)
                        if n >= 1:
                            copy(n - 1)
                    copy(NI - 1)
                    take_beside(1)
                    act.wait_ge(pv_done, NI * j + NI)
                    act.sem_inc(pv_turn, 1)
                    nc.scalar.activation(o_hi[:, bass.ds(j, 1), :].rearrange("p a t -> p (a t)"), ps[:, 4, :],
                                         ACT.Copy).then_inc(o_hi_done, 1)

            def linear():
                act.wait_ge(cprob_done, 1)
                s = [[scr[:, 4 * m + k, :] for k in range(4)] for m in range(2)]
                for m in range(2):
                    act.wait_ge(z_ready, m + 1)
                    nc.scalar.activation(s[m][0], ps[:, 6 + m, :], ACT.Identity, bias=p_("b_a", m, m + 1))
                    link(nc.scalar.activation(s[m][1], ps[:, 6 + m, :], ACT.Abs, bias=p_("b_a", m, m + 1)))
                for m in range(2):
                    link(nc.scalar.activation(s[m][2], s[m][1], ACT.Exp, scale=-1.0))
                for m in range(2):
                    nc.scalar.activation(s[m][1], s[m][2], ACT.Ln, bias=c_("one")).then_inc(gln_done, 1)
                for m in range(2):
                    b = scr[:, 4 * m + 3, :]
                    act.wait_ge(b_done, m + 1)
                    nc.scalar.activation(decay[:, m, :], b, ACT.Exp, scale=1.0 / 16).then_inc(eb_done, 1)
                    nc.scalar.activation(scr[:, 4 * m + 1, :], b, ACT.Exp, scale=-1.0 / 16).then_inc(eb_done, 1)
                    act.wait_ge(kst_diff, m + 1)
                    nc.scalar.activation(scr[:, 4 * m + 2, :], scr[:, 4 * m + 2, :], ACT.Exp,
                                         scale=1.0 / 16).then_inc(kst_exp, 1)
                for h in range(GH):
                    act.wait_ge(gv_turned, h + 1)
                    nc.scalar.activation(gv_tok[:, :, h * GDV:(h + 1) * GDV],
                                         ps[:, h, :].rearrange("p (q d) -> p q d", q=TT), ACT.Copy
                                         ).then_inc(gv_copied, 1)
                for h in range(GH):
                    nc.scalar.activation(proj[:, MT_GR - HPG + h, :], proj[:, MT_GR - HPG + h, :], ACT.Silu).then_inc(gr_done, 1)
                load_root()
                act.wait_ge(a_used, 2 * TT - 1)
                act.wait_ge(pv_done, NI * HPG + GH * TT)
                for h in range(GH):
                    nc.scalar.activation(scr[:, h, :], ps[:, 4 + h, :], ACT.Square).then_inc(gsq_done, 1)
                act.wait_ge(gssq_done, 1)
                nc.scalar.activation(g_col[:, :], ps[:, 0, 0:GH * TT], ACT.Sqrt, scale=1.0 / GDV, bias=c_("eps")
                                     ).then_inc(grms_done, 1)
                for h in range(GH):
                    act.wait_ge(go_done, h + 1)
                    nc.scalar.activation(h_hi[:, 4 + h, :], scr[:, h, :], ACT.Copy).then_inc(go_hi, 1)

            def to_stream(u0, n):
                with act.Fori(0, DC // 2) as i:
                    for j in range(2):
                        head(unit(u0 + j + 2, 2, i))
                        act.wait_ge(x_done, DC * n + 2 * i + j + 1)
                        at = bass.ds(2 * i + j, 1)
                        nc.scalar.activation(scr[:, at, :], x[:, at, :], ACT.Square).then_inc(sq_done, 1)

            def gates():
                head(unit(U_GATES + 2))
                act.wait_ge(hn_lo_done[0], 2 * DC)
                act.wait_ge(hn_lo_done[1], 2 * DC)
                act.dma_start(q_sc[:, 1, :, :].rearrange("p a t -> p (a t)"), dram["row_const"]).then_inc(rows_in, 16)
                act.wait_ge(unit_done, U_GATES + 1)
                z, bif = ps[:, 4, :], p_("b_if")
                nc.scalar.activation(rows_of[0], z, ACT.Identity, bias=bif)
                link(nc.scalar.activation(rows_of[1], z, ACT.Abs, bias=bif))
                link(nc.scalar.activation(rows_of[2], rows_of[1], ACT.Exp, scale=-1.0))
                nc.scalar.activation(rows_of[1], rows_of[2], ACT.Ln, bias=c_("one")).then_inc(row_l, 1)

            def row_exponentials():
                act.wait_ge(edge_done, 1)
                nc.scalar.activation(edge[:, 4, :], edge[:, 4, :], ACT.Exp).then_inc(edge_exp, 1)
                act.wait_ge(row_args, 1)
                nc.scalar.activation(rows_of[2][0:64], rows_of[2][0:64], ACT.Exp)
                nc.scalar.activation(raw_i, raw_i, ACT.Exp)
                link(nc.scalar.activation(raw_f, raw_f, ACT.Exp))
                nc.scalar.activation(row_m[0:64, :], raw_m, ACT.Copy)
                nc.scalar.activation(row_i[0:64, :], raw_i, ACT.Copy)
                nc.scalar.activation(row_f[0:64, :], raw_f, ACT.Copy).then_inc(row_exp, 1)

            def mlstm(h, units=True, core=True):
                p = h - 1

                def take(j, dst, func):
                    act.wait_ge(unit_done, U_HEADS + HEAD_UNITS * h + j + 1)
                    if dst is None:
                        dst = merged[:, bass.ds(2 * h + j - 6, 1), :].rearrange("p a t -> p (a t)")
                    nc.scalar.activation(dst, ps[:, j % 2, :], func).then_inc(ev_done, 1)

                def activate(j):
                    act.wait_ge(conv_done, 4 * h + j + 1)
                    if core:
                        act.wait_ge(sc_ready, h)
                        act.wait_ge(qs_done, 2 * h)
                    src = bass.ds(2 * h + j, 1) if j < 2 else bass.ds(2 * h + DC + j - 2, 1)
                    nc.scalar.activation(qk[:, j, :], scr[:, 2 + j % 2, :], ACT.Silu, bias=p_("conv_b")[:, src]
                                         ).then_inc(qk_done, 1)

                def project(j):
                    head(unit(U_HEADS + j + 2, HEAD_UNITS, h))
                    if j < 4:
                        if j >= 2:
                            act.wait_ge(conv_done, 4 * h + j - 1)
                        take(j, qk_pad[:, j % 2, CONV // 2:CONV // 2 + T], ACT.Copy)
                    elif j < 6:
                        take(j, scr[:, j - 4, :], ACT.Copy)
                    elif j < 8:
                        take(j, None, ACT.Sigmoid)
                    else:
                        take(j, scr[:, j - 4, :], ACT.Silu)
                    if 2 <= j < 6:
                        activate(j - 2)

                def values():
                    for e in range(2):
                        act.wait_ge(vt_ready, 2 * p + e + 1)
                        nc.scalar.activation(v_aug[:, :, e * P:(e + 1) * P],
                                             ps[:, 4 + e, :].rearrange("p (c d) -> p c d", c=NCH), ACT.Copy
                                             ).then_inc(vt_done, 1)

                def decays(d):
                    act.wait_ge(dlog_done, 2 * p + d + 1)
                    nc.scalar.activation(d_mat[:, d, :], d_mat[:, d, :], ACT.Exp).then_inc(dexp_done, 1)
                    act.wait_ge(fl_ready, 2 * p + d + 1)
                    nc.scalar.activation(floor[:, d, :], ps[:, 3, :], ACT.Copy).then_inc(fl_done, 1)

                def squared():
                    act.wait_ge(num_done, 8 * p + 8)
                    act.wait_ge(num_ready, 8 * p + 8)
                    for e in range(2):
                        nc.scalar.activation(d_mat[:, e, :], h_sum[:, e, :], ACT.Square).then_inc(hsq_done, 1)

                def root():
                    act.wait_ge(hssq_done, p + 1)
                    nc.scalar.activation(r_col[:, :], ps[:, 3, 0:TT], ACT.Sqrt, scale=1.0 / MD, bias=c_("eps")
                                         ).then_inc(hrms_done, 1)

                def y_head():
                    for e in range(2):
                        act.wait_ge(y_done, 2 * p + e + 1)
                        nc.scalar.activation(y_hi[:, bass.ds(2 * p + e, 1), :].rearrange("p a t -> p (a t)"),
                                             h_sum[:, e, :], ACT.Copy).then_inc(y_hi_done, 1)

                before = {0: [values], 1: [lambda: decays(0)], 2: [lambda: decays(1)], 8: [squared], 9: [root],
                          HEAD_UNITS: [y_head]}
                for j in range(HEAD_UNITS + 1):
                    for part in before.get(j, ()) if core else ():
                        part()
                    if units and j < HEAD_UNITS:
                        project(j)
                    if not core and j == 5:
                        row_exponentials()
                    for i in () if units else GATE_B_AT_ACT[j]:
                        head(unit(U_GB + i + 2))
                        act.wait_ge(unit_done, U_GB + i + 1)
                        if i == 6:
                            act.wait_ge(y_done, 2 * MH)
                        nc.scalar.activation(merged[:, i, :], ps[:, i % 2, :], ACT.Sigmoid,
                                             bias=p_("b_merge", DC + i, DC + i + 1)).then_inc(ev_done, 1)

            def merge_b():
                with act.Fori(0, DC // 2) as i:
                    for j in range(2):
                        head(unit(U_PB + j + 2, 2, i))

            def merge_a():
                with act.Fori(0, DC // 2) as i:
                    for j in range(2):
                        head(unit(U_PA + 2 * j + 2, 4, i))
                        act.wait_ge(unit_done, U_PA + 4 * i + 2 * j + 1)
                        act.wait_ge(mg_done, DC + 2 * i + j + 1)
                        nc.scalar.activation(gate[:, j, :], ps[:, 4 + 2 * j, :], ACT.Sigmoid,
                                             bias=p_("b_merge")[:, bass.ds(2 * i + j, 1)]).then_inc(mg_sig, 1)
                        head(unit(U_PA + 2 * j + 3, 4, i))
                        act.wait_ge(mg_done, DC + 2 * i + j + 3)
                        at = bass.ds(2 * i + j, 1)
                        nc.scalar.activation(m_hi[:, at, :], merged[:, at, :], ACT.Copy).then_inc(m_hi_done, 1)

            def pooled():
                act.wait_ge(mg_done, DC + 2)
                act.dma_start(inv_count[:, :, :].rearrange("p w t -> p (w t)"), dram["inv_count"]).then_inc(inv_in, 16)

                def pool_head(c):
                    act.wait_ge(pool_done, c + 1)
                    nc.scalar.activation(y_hi[:, c, :], scr[:, c, :], ACT.Copy).then_inc(y_hi_done, 1)

                for j in range(DC):
                    head(unit(U_POOL + j + 2))
                    act.wait_ge(unit_done, U_POOL + j + 1)
                    if j >= 2:
                        act.wait_ge(pool_done, j - 1)
                    if j == 0:
                        act.wait_ge(upad_done, 1)
                    nc.scalar.activation(u_pad[:, j % 2, 8:8 + T], ps[:, 2 + j % 2, :], ACT.Copy).then_inc(ev_done, 1)
                    if j >= 1:
                        pool_head(j - 1)
                for j in range(DC):
                    head(unit(U_POOL + DC + j + 2))
                    act.wait_ge(unit_done, U_POOL + DC + j + 1)
                    nc.scalar.activation(silu_z[:, j, :], ps[:, 2 + j % 2, :], ACT.Silu).then_inc(ev_done, 1)
                    if j == 0:
                        pool_head(DC - 1)
                for n in range(2):
                    head(unit(U_MIX2 + n + 2))
                    for c in range(4 * n, 4 * n + 4):
                        act.wait_ge(y_done, 2 * MH + c + 1)
                        nc.scalar.activation(y_hi[:, c, :], scr[:, c, :], ACT.Copy).then_inc(y_hi_done, 1)

            def output():
                for i in range(DC):
                    if U_OUT + i + 2 < NUNITS:
                        head(unit(U_OUT + i + 2))
                    if i == DC - 1:
                        load_root()
                    act.wait_ge(out_done, i + 3)
                    nc.scalar.activation(scr[:, i, :], merged[:, i, :], ACT.Square).then_inc(sq_done, 1)
                norm(5, parts=False)

            link = Chain(act, act_chain).link
            act.sem_inc(hrms_done, 1)
            for dst, src in ((param, "param"), (const, "const")):
                act.dma_start(dst[:, :], dram[src]).then_inc(small_in, 16)
            squares(0, 0, 8)
            act.wait_ge(small_in, 32)
            for u in range(2):
                act.wait_ge(raw_full[u], 16)
                nc.scalar.activation(w_hi[:, u, :], w_raw[:, u, :], ACT.Copy).then_inc(w_hi_done, 1)
            norm(0)
            ffn(U_FFN1, 0, 1)
            norm(1)
            project()
            compressed()
            attention()
            linear()
            to_stream(U_MIXOUT, 2)
            norm(2)
            ffn(U_FFN2, 1, 3)
            norm(3, parts=False)
            squares(4, 0, 8)
            norm(4, at=3)
            gates()
            mlstm(0, core=False)
            with act.Fori(1, MH) as h:
                mlstm(h)
            mlstm(MH, units=False)
            merge_b()
            pooled()
            merge_a()
            output()

        @block.vector
        def _(dve):
            chain = Chain(dve, dve_chain)

            def norm_sum(n):
                for c in range(1, 4):
                    dve.wait_ge(sq_done, DC * n + c + 1)
                    ins = nc.vector.tensor_tensor(scr[:, 0, :], scr[:, 0, :], scr[:, c, :], ALU.add)
                    if c < 3:
                        chain.link(ins)
                ins.then_inc(sqsum_done, 1)

            def norm(n, gain, at=None):
                at = n if at is None else at
                dve.wait_ge(rms_done, n + 1)
                nc.vector.reciprocal(r_col[:, :], r_col[:, :]).then_inc(rstd_done, 1)
                dve.wait_ge(spread_done, n + 1)

                def tail(c):
                    dve.wait_ge(hn_hi_done, DC * at + c + 1)
                    nc.vector.tensor_tensor(h_lo[:, c, :], scr[:, c, :], h_hi[:, c, :].bitcast(F32),
                                            ALU.subtract).then_inc(hn_lo_done[0], 1)

                for c in range(DC):
                    nc.vector.scalar_tensor_tensor(scr[:, c, :], x[:, c, :], p_(gain, c, c + 1), ps[:, 1, :],
                                                   ALU.mult, ALU.mult).then_inc(hn_done, 1)
                    if c % 2:
                        tail(c - 1)

            def ffn(u0, n, next_norm):
                with dve.Fori(0, FT // 2) as i:
                    for f in range(2):
                        dve.wait_ge(unit_done, u0 + 4 * i + 2 * f + 2)
                        dve.wait_ge(silu_done, FT * n + 2 * i + f + 1)
                        nc.vector.tensor_tensor(hid[:, f, :], silu[:, f, :], ps[:, 5 + 2 * f, :],
                                                ALU.mult).then_inc(hid_done, 1)
                        dve.wait_ge(hid_hi_done, FT * n + 2 * i + f + 1)
                        at = bass.ds(2 * i + f, 1)
                        nc.vector.tensor_tensor(hid_lo[:, at, :].rearrange("p a t -> p (a t)"), hid[:, f, :],
                                                hid_hi[:, at, :].rearrange("p a t -> p (a t)").bitcast(F32),
                                                ALU.subtract).then_inc(hid_lo_done, 1)
                for half in range(2):
                    for d in range(4 * half, 4 * half + 4):
                        if d % 4 < 3:
                            dve.wait_ge(down_done, 6 * n + 3 * half + d % 4 + 1)
                        else:
                            dve.wait_ge(unit_done, u0 + 2 * FT + (half + 1) * (FT // 2))
                        nc.vector.scalar_tensor_tensor(x[:, d, :], ps[:, d, :], 0.5, x[:, d, :],
                                                       ALU.mult, ALU.add).then_inc(x_done, 1)
                    if half == 0:
                        norm_sum(next_norm)

            def compressed():
                dve.wait_ge(dup_in, 8 * 16)
                for s in range(2):
                    for half in range(2):
                        r = slice(half * DH, (half + 1) * DH)
                        for part in range(2):
                            tok = dup[r, 2 * s:2 * s + 2, :].rearrange("p g (n c) -> p c g n", c=16)
                            src = tok[:, half:16:2, :, part:part + NCMP]
                            pos = p_("pe", s * 16 + part * 8, s * 16 + part * 8 + 8)[r].unsqueeze(2).unsqueeze(3)
                            ins = nc.vector.tensor_tensor(rows[r, s, part * 8:part * 8 + 8, :, :], src,
                                                          pos.to_broadcast([DH, 8, NG, NCMP]), ALU.add)
                    ins.then_inc(rows_done, 1)
                dve.wait_ge(tok_ready, 1)
                for b in range(2):
                    nc.vector.tensor_copy(v_tok[:, :, b, :], ps[:, 5 + b, :].rearrange("p (q d) -> p q d", q=TT)
                                          ).then_inc(tok_done, 1)
                dve.wait_ge(gate_done, 1)
                dve.sem_inc(tok_done, 1)
                dve.wait_ge(cmp_pe, 3)
                nc.vector.tensor_copy(kc_t[:, :], ps[:, 0, 0:NCMP])
                nc.vector.tensor_copy(vc_tok[:, :, :].rearrange("p g d -> p (g d)"), ps[0:NCMP, 1, 0:NG * DH]
                                      ).then_inc(kvc_done, 1)
                dve.wait_ge(cmp_pe, 4)
                dve.wait_ge(w1_in, 32)
                cb = cbias[:, :].rearrange("p (q h n) -> p q h n", q=TT, h=NH)
                for g in range(NG):
                    hs = slice(g * HPG, (g + 1) * HPG)
                    psc = ps[:, 2 + g, :].rearrange("p (q h n) -> p q h n", q=TT, h=HPG)[:, :, :, 0:NCMP]
                    ins = nc.vector.tensor_tensor(c_score[:, :, hs, :], psc, cb[:, :, hs, :], ALU.add)
                chain.link(ins)
                sc3 = c_score.rearrange("p q h n -> p (q h) n")

                def rep_(v):
                    return v.unsqueeze(2).to_broadcast([P, TT * NH, NCMP])

                chain.link(nc.vector.tensor_reduce(c_max[:, :], sc3, AX.X, ALU.max))
                nc.vector.tensor_tensor(sc3, sc3, rep_(c_max[:, :]), ALU.subtract).then_inc(cexp_ready, 1)
                dve.wait_ge(cexp_done, 1)
                chain.link(nc.vector.tensor_reduce(c_sum[:, :], sc3, AX.X, ALU.add))
                chain.link(nc.vector.reciprocal(c_max[:, :], c_sum[:, :]))
                g0 = gate_tok[:, :, :].rearrange("p q (h b) -> p (q h) b", b=3)[:, :, 0]
                chain.link(nc.vector.tensor_tensor(c_sum[:, :], c_max[:, :], g0, ALU.mult))
                valid = c_("cvalid").rearrange("p (q n) -> p q n", q=TT).unsqueeze(2).to_broadcast([P, TT, NH, NCMP])
                chain.link(nc.vector.tensor_tensor(c_score, c_score, valid, ALU.mult))
                nc.vector.tensor_tensor(sc3, sc3, rep_(c_sum[:, :]), ALU.mult).then_inc(cprob_done, 1)
                for h in range(0, NH, 2):
                    dve.wait_ge(cmp_pe, 5 + h)
                    nc.vector.tensor_copy(pc_t[:, h, :], ps[0:NCMP, 4 + h % 4, :]).then_inc(pct_done[0], 1)

            def attention():
                with dve.Fori(0, HPG) as j:
                    for g in range(NG):
                        ins = nc.vector.tensor_scalar(bias[:, g, :], c_("dist"), c_("slope")[:, bass.ds(j + HPG * g, 1)],
                                                      None, ALU.mult)
                    ins.then_inc(bias_done, 1)
                    dve.wait_ge(bias_done, j + 1)

                    def finish(n):
                        b, qt, g = ITEMS[n]
                        w, r = (qt + 1) * P, n % DEEP
                        dve.wait_ge(exp_done, NI * j + n + 1)
                        nc.vector.reciprocal(psum_l[:, r:r + 1], psum_l[:, r:r + 1]).then_inc(rl_done, 1)
                        dve.wait_ge(rl_done, NI * j + n + 1)
                        gate = gate_tok[:, qt, bass.ds(3 * j + 3 * HPG * g + b + 1, 1)]
                        nc.vector.tensor_scalar(prob[:, r, 0:w], prob[:, r, 0:w], psum_l[:, r:r + 1],
                                                gate, ALU.mult, ALU.mult).then_inc(prob_done, 1)

                    for n in range(NI):
                        b, qt, g = ITEMS[n]
                        w, r = (qt + 1) * P, n % DEEP
                        dve.wait_ge(score_ready, NI * j + n + 1)
                        if n >= DEEP:
                            dve.wait_ge(exp_done, NI * j + n - DEEP + 1)
                        dve.sem_inc(score_turn, 1)
                        nc.vector.tensor_tensor_reduce(score[:, r, 0:w], ps[:, SCORE_BANKS[r], 0:w], bias[:, g, T - w:T],
                                                       -1.0, 3.0e38, ALU.add, ALU.min, nmax[:, r:r + 1]
                                                       ).then_inc(neg_done, 1)
                        if n >= 1:
                            finish(n - 1)
                    finish(NI - 1)
                    dve.wait_ge(o_hi_done, j + 1)
                    at = bass.ds(j, 1)
                    nc.vector.tensor_tensor(o_lo[:, at, :].rearrange("p a t -> p (a t)"), ps[:, 4, :],
                                            o_hi[:, at, :].rearrange("p a t -> p (a t)").bitcast(F32), ALU.subtract
                                            ).then_inc(o_lo_done, 1)

            def linear():
                nc.vector.memset(intra[:, :, :], 0.0)
                for m in range(2):
                    s = [scr[:, 4 * m + k, :] for k in range(4)]
                    dve.wait_ge(gln_done, m + 1)
                    chain.link(nc.vector.scalar_tensor_tensor(s[2], s[0], 0.0, s[1], ALU.min, ALU.subtract))
                    nc.vector.tensor_tensor_scan(s[3], c_("keep"), s[2], 0.0, ALU.mult, ALU.add).then_inc(b_done, 1)
                for m in range(2):
                    s = [scr[:, 4 * m + k, :] for k in range(4)]
                    dve.wait_ge(b_done, m + 1)
                    b3 = s[3].rearrange("p (n c) -> p n c", c=GC)
                    last = b3[:, :, GC - 1:GC].to_broadcast([P, T // GC, GC])
                    nc.vector.tensor_tensor(s[2].rearrange("p (n c) -> p n c", c=GC), last, b3, ALU.subtract
                                            ).then_inc(kst_diff, 1)
                    dve.wait_ge(eb_done, 2 * m + 2)
                    nc.vector.tensor_tensor(q_in[:, m, :], proj[:, MT_GQ - HPG + m, :], decay[:, m, :], ALU.mult)
                    nc.vector.tensor_tensor(k_in[:, m, :], proj[:, MT_GK - HPG + m, :], s[1], ALU.mult)
                    dve.wait_ge(kst_exp, m + 1)
                    nc.vector.tensor_tensor(s[0], proj[:, MT_GK - HPG + m, :], s[2], ALU.mult).then_inc(kst_done, 1)
                for m in range(2):
                    dve.wait_ge(kst_turned, m + 1)
                    nc.vector.tensor_copy(kst_tok[:, :, m * P:(m + 1) * P],
                                          ps[:, 4 + m, :].rearrange("p (q d) -> p q d", q=TT)).then_inc(kst_copied, 1)
                for tt in range(TT):
                    for h in range(GH):
                        n = tt * GH + h
                        dve.wait_ge(a_ready, n + 1)
                        if n >= 2:
                            dve.wait_ge(pv_done, NI * HPG + n - 1)
                        nc.vector.copy_predicated(intra[:, n % 2, :], c_("gmask").bitcast(I32), ps[:, n % 2, 0:P]
                                                  ).then_inc(a_done, 1)
                    for c in range(2):
                        n = 2 * tt + c
                        if n < T // GC - 1:
                            dve.wait_ge(add_ready, n + 1)
                            if n >= 1:
                                dve.wait_ge(state_done, n)
                            if n >= 2:
                                dve.wait_ge(a_used, n - 1)
                            for m in range(2):
                                new, add = state[:, m, (n + 1) % 2, :], ps[:, 2 + n % 2, m * GDV:(m + 1) * GDV]
                                if n == 0:
                                    ins = nc.vector.tensor_copy(new, add)
                                else:
                                    at = n * GC + GC - 1
                                    ins = nc.vector.scalar_tensor_tensor(new, state[:, m, n % 2, :],
                                                                         decay[:, m, at:at + 1], add, ALU.mult, ALU.add)
                            ins.then_inc(state_done, 1)
                for h in range(GH):
                    dve.wait_ge(gr_done, h + 1)
                    dve.wait_ge(gsq_done, h + 1)
                    nc.vector.scalar_tensor_tensor(scr[:, 4 + h, :], ps[:, 4 + h, :], p_("g_gla"),
                                                   proj[:, MT_GR - HPG + h, :], ALU.mult, ALU.mult
                                                   ).then_inc(gs_gated, 1)
                dve.wait_ge(grms_done, 1)
                nc.vector.reciprocal(g_col[:, :], g_col[:, :]).then_inc(grstd_done, 1)

                def tail(h):
                    dve.wait_ge(go_hi, h + 1)
                    nc.vector.tensor_tensor(h_lo[:, 4 + h, :], scr[:, h, :], h_hi[:, 4 + h, :].bitcast(F32),
                                            ALU.subtract).then_inc(go_lo, 1)

                dve.wait_ge(gs_gated, GH)
                for h in range(GH):
                    dve.wait_ge(gspread_done, h + 1)
                    nc.vector.tensor_tensor(scr[:, h, :], scr[:, 4 + h, :], ps[:, 4 + h, :], ALU.mult
                                            ).then_inc(go_done, 1)
                    if h >= 1:
                        tail(h - 1)
                tail(GH - 1)

            def to_stream(u0, n):
                def two(i):
                    for j in range(2):
                        dve.wait_ge(unit_done, u0 + 2 * i + j + 1)
                        at = bass.ds(2 * i + j, 1)
                        xd = x[:, at, :].rearrange("p a t -> p (a t)")
                        nc.vector.tensor_tensor(xd, ps[:, 2 + j, :], xd, ALU.add).then_inc(x_done, 1)

                with dve.Fori(0, DC // 2 - 1) as i:
                    two(i)
                norm_sum(n)
                two(DC // 2 - 1)

            def gates():
                fwd, bwd = slice(0, 32), slice(32, 64)
                z, b, a, cm, lf = (rows_of[k] for k in (0, 5, 3, 1, 4))
                nc.vector.memset(v_aug[:, :, MD:MD + P], 1.0)
                nc.vector.memset(qk_pad[:, :, 0:CONV // 2], 0.0)
                nc.vector.memset(qk_pad[:, :, CONV // 2 + T:], 0.0)
                dve.wait_ge(row_l, 1)
                dve.wait_ge(rows_in, 16)
                chain.link(nc.vector.scalar_tensor_tensor(a[64:128], z[64:128], 0.0, cm[64:128], ALU.min, ALU.subtract))
                chain.link(nc.vector.tensor_copy(lf[0:64], a[64:128]))
                keep, reset = rows_of[6], rows_of[7]
                nc.vector.tensor_tensor_scan(b[fwd], keep[fwd], lf[fwd], 0.0, ALU.mult, ALU.add)
                chain.link(nc.vector.tensor_tensor_scan(b[bwd, ::-1], keep[bwd, ::-1], lf[bwd, ::-1], 0.0,
                                                        ALU.mult, ALU.add))
                chain.link(nc.vector.tensor_tensor(a[0:64], z[0:64], b[0:64], ALU.subtract))
                nc.vector.tensor_tensor_scan(cm[fwd], reset[fwd], a[fwd], NEG, ALU.add, ALU.max)
                chain.link(nc.vector.tensor_tensor_scan(cm[bwd, ::-1], reset[bwd, ::-1], a[bwd, ::-1], NEG,
                                                        ALU.add, ALU.max))

            def row_ends():
                fwd, bwd = slice(0, 32), slice(32, 64)
                b, a, cm = (rows_of[k] for k in (5, 3, 1))
                bl, cl, mb, ma, kp = (edge[:, k, :] for k in range(5))
                for src, dst in ((b, bl), (cm, cl)):
                    nc.vector.tensor_copy(dst[fwd], src[fwd, MC - 1::MC])
                    nc.vector.tensor_copy(dst[bwd, ::-1], src[bwd, 0::MC])
                chain.link(nc.vector.memset(mb[:, 0:1], NEG))
                for s in range(NCH):
                    one = slice(s, s + 1)
                    chain.link(nc.vector.tensor_tensor(ma[:, one], cl[:, one], mb[:, one], ALU.max))
                    if s + 1 < NCH:
                        chain.link(nc.vector.tensor_tensor(mb[:, s + 1:s + 2], bl[:, one], ma[:, one], ALU.add))
                nc.vector.tensor_tensor(kp, mb, ma, ALU.subtract).then_inc(edge_done, 1)

                def chunks(v, r):
                    return v[r].rearrange("p (c t) -> p c t", c=NCH)

                def spread(v, r):
                    return (v[r, ::-1] if r is bwd else v[r]).unsqueeze(2).to_broadcast([32, NCH, MC])

                for r in (fwd, bwd):
                    ins = nc.vector.tensor_tensor(chunks(raw_m, r), chunks(cm, r), spread(mb, r), ALU.max)
                chain.link(ins)
                for r in (fwd, bwd):
                    nc.vector.tensor_tensor(chunks(raw_i, r), spread(mb, r), chunks(raw_m, r), ALU.subtract)
                    nc.vector.tensor_tensor(chunks(rows_of[2], r), chunks(a, r), spread(ma, r), ALU.subtract)
                chain.link(nc.vector.tensor_tensor(raw_f, b[0:64], raw_m, ALU.add))
                nc.vector.tensor_scalar(raw_f, raw_f, -1.0, 88.0, ALU.mult, ALU.min)
                nc.vector.tensor_scalar(raw_m, raw_m, -1.0, None, ALU.mult).then_inc(row_args, 1)

            def row_columns():
                dve.wait_ge(row_exp, 1)
                for row, raw in ((row_m, raw_m), (row_i, raw_i), (row_f, raw_f)):
                    nc.vector.tensor_tensor(row[64:P, :], raw, row[0:64, :].bitcast(F32), ALU.subtract)
                for n, dst in enumerate((a_tok, wk_tok)):
                    dve.wait_ge(tokrow_ready, n + 1)
                    nc.vector.tensor_copy(dst[:, :, :].rearrange("p c r -> p (c r)"), ps[:, 5 + n, 0:NCH * 64])
                dve.wait_ge(tokrow_ready, 3)
                nc.vector.tensor_copy(keep_bc[:, :], ps[:, 7, 0:2 * MH * NCH]).then_inc(tokrow_done, 1)
                dve.wait_ge(tokrow_done, 1)

            def mlstm(h, units=True, core=True):
                p = h - 1

                def convolve(j):
                    dve.wait_ge(ev_done, HEAD_UNITS * h + j + 3)
                    if j >= 2:
                        dve.wait_ge(qk_done, 4 * h + j - 1)
                    acc = scr[:, 2 + j % 2, :]
                    at = (2 * h + j if j < 2 else 2 * h + DC + j - 2) * CONV
                    for k in range(CONV):
                        tap, w = qk_pad[:, j % 2, k:k + T], p_("conv_w")[:, bass.ds(at + k, 1)]
                        if k == 0:
                            ins = nc.vector.tensor_scalar(acc, tap, w, None, ALU.mult)
                        else:
                            ins = nc.vector.scalar_tensor_tensor(acc, tap, w, acc, ALU.mult, ALU.add)
                        if k < CONV - 1:
                            chain.link(ins)
                    ins.then_inc(conv_done, 1)

                def gate_product(e):
                    dve.wait_ge(ev_done, HEAD_UNITS * h + 8 + e + 3)
                    og = merged[:, bass.ds(2 * h + e, 1), :].rearrange("p a t -> p (a t)")
                    nc.vector.tensor_tensor(og, og, scr[:, 4 + e, :], ALU.mult).then_inc(og_done, 1)

                def weigh_keys(n):
                    s, d = STEPS[n]
                    c = chunk_of(s, d)
                    if n >= 2:
                        dve.wait_ge(cadd_ready, 6 * p + n - 1)
                    nc.vector.tensor_scalar(k_w[:, d, :], k_tok[:, c, :], wk_tok[:, c, bass.ds(p + 32 * d, 1)], None,
                                            ALU.mult).then_inc(kw_done, 1)

                def keys():
                    for d in range(2):
                        ins = nc.vector.tensor_tensor(sel[:, d, :], ident[:, bass.ds(p + 32 * d, 1)].to_broadcast([P, P]),
                                                      ident[:, bass.ds(p + 32 * d + 64, 1)].to_broadcast([P, P]), ALU.add)
                    ins.then_inc(sel_done, 1)
                    for e in range(2):
                        dve.wait_ge(kt_ready, 2 * p + e + 1)
                        nc.vector.tensor_copy(k_tok[:, :, e * P:(e + 1) * P],
                                              ps[:, 2 + e, :].rearrange("p (c d) -> p c d", c=NCH)).then_inc(kt_done, 1)
                    dve.wait_ge(kt_done, 2 * p + 2)
                    weigh_keys(0)
                    weigh_keys(1)

                def decays(d):
                    dve.wait_ge(nm_ready, 2 * p + d + 1)
                    for c in range(NCH):
                        at = slice(c * MC, (c + 1) * MC)
                        ins = nc.vector.scalar_tensor_tensor(d_mat[:, d, at], ps[:, 7, at], a_tok[:, c, bass.ds(p + 32 * d, 1)],
                                                             c_(("upper", "lower")[d]), ALU.add, ALU.add)
                    ins.then_inc(dlog_done, 1)
                    dve.wait_ge(in_ready, 2 * p + d + 1)
                    for e in range(2):
                        ins = nc.vector.scalar_tensor_tensor(q_sc[:, d, e, :], qk[:, e, :], MD ** -0.5, ps[:, 2, :],
                                                             ALU.mult, ALU.mult)
                    ins.then_inc(qs_done, 1)

                def weigh_scores():
                    dve.wait_ge(sc_ready, p + 1)
                    for d in range(2):
                        dve.wait_ge(dexp_done, 2 * p + d + 1)
                        nc.vector.scalar_tensor_tensor(d_mat[:, d, :], ps[:, 6, :], MD ** -0.5, d_mat[:, d, :],
                                                       ALU.mult, ALU.mult).then_inc(sct_done, 1)

                def step(n):
                    s, d = STEPS[n]
                    c = chunk_of(s, d)
                    if s < NCH - 1:
                        if n + 2 < 6:
                            weigh_keys(n + 2)
                        dve.wait_ge(cadd_ready, 6 * p + n + 1)
                        dve.wait_ge(num_ready, 8 * p + n + 1)
                        for e in range(2):
                            new, add = c_state[:, d, e, :], ps[:, 4 + e, 0:MD + P]
                            if s == 0:
                                ins = nc.vector.tensor_copy(new, add)
                            else:
                                at = bass.ds(p * NCH + d * MH * NCH + s, 1)
                                ins = nc.vector.scalar_tensor_tensor(new, new, keep_bc[:, at], add, ALU.mult, ALU.add)
                        ins.then_inc(c_done, 1)
                    dve.wait_ge(num_ready, 8 * p + n + 1)
                    dve.wait_ge(fl_done, 2 * p + d + 1)
                    at = slice(c * MC, (c + 1) * MC)
                    q_n = ps[:, 6 + d, MD:MD + P]
                    chain.link(nc.vector.scalar_tensor_tensor(den[:, d, :], q_n, -1.0, floor[:, d, at], ALU.mult, ALU.max))
                    chain.link(nc.vector.tensor_tensor(den[:, d, :], den[:, d, :], q_n, ALU.max))
                    chain.link(nc.vector.reciprocal(den[:, d, :], den[:, d, :]))
                    num = ps[:, 6 + d, 0:MD].rearrange("p (e t) -> p e t", e=2)
                    rden = den[:, d, :].unsqueeze(1).to_broadcast([P, 2, MC])
                    if n in FIRST_OF:
                        nc.vector.tensor_tensor(h_sum[:, :, at], num, rden, ALU.mult).then_inc(num_done, 1)
                    else:
                        chain.link(nc.vector.tensor_tensor(h_tmp[:, :, :], num, rden, ALU.mult))
                        nc.vector.tensor_tensor(h_sum[:, :, at], h_sum[:, :, at], h_tmp[:, :, :], ALU.add
                                                ).then_inc(num_done, 1)

                def roots():
                    dve.wait_ge(hrms_done, p + 2)
                    nc.vector.reciprocal(r_col[:, :], r_col[:, :]).then_inc(hrstd_done, 1)

                def gated():
                    dve.wait_ge(hspread_done, p + 1)
                    dve.wait_ge(og_done, 2 * p + 2)
                    for e in range(2):
                        y, og = h_sum[:, e, :], merged[:, bass.ds(2 * p + e, 1), :].rearrange("p a t -> p (a t)")
                        chain.link(nc.vector.scalar_tensor_tensor(y, y, p_("g_mlstm")[:, bass.ds(2 * p + e, 1)],
                                                                  ps[:, 7, :], ALU.mult, ALU.mult))
                        nc.vector.tensor_tensor(y, y, og, ALU.mult).then_inc(y_done, 1)

                def y_tail():
                    for e in range(2):
                        dve.wait_ge(y_hi_done, 2 * p + e + 1)
                        at = bass.ds(2 * p + e, 1)
                        nc.vector.tensor_tensor(y_lo[:, at, :].rearrange("p a t -> p (a t)"), h_sum[:, e, :],
                                                y_hi[:, at, :].rearrange("p a t -> p (a t)").bitcast(F32), ALU.subtract
                                                ).then_inc(y_lo_done, 1)

                def run(needed, *parts):
                    for part, *arg in parts if needed else ():
                        part(*arg)

                run(core, (keys,), (decays, 0))
                run(units, (convolve, 0))
                run(core, (decays, 1))
                run(units, (convolve, 1))
                run(not core, (row_ends,))
                run(core, (weigh_scores,))
                run(units, (convolve, 2))
                run(core, (step, 0), (step, 1))
                run(units, (convolve, 3))
                run(core, (step, 2), (step, 3))
                run(core, (step, 4), (step, 5), (step, 6), (step, 7))
                run(units, (gate_product, 0))
                run(core, (roots,))
                run(not core, (row_columns,))
                run(units, (gate_product, 1))
                run(core, (gated,), (y_tail,))

            def merge_b():
                dve.wait_ge(ev_done, HEAD_UNITS * MH + DC + 2)
                with dve.Fori(0, DC // 2) as i:
                    for j in range(2):
                        dve.wait_ge(unit_done, U_PB + 2 * i + j + 1)
                        m = merged[:, bass.ds(2 * i + j, 1), :].rearrange("p a t -> p (a t)")
                        nc.vector.tensor_tensor(m, m, ps[:, 5 + 2 * j, :], ALU.mult).then_inc(mg_done, 1)

            def merge_a():
                with dve.Fori(0, DC // 2) as i:
                    chain.enter(i, 2)
                    for j in range(2):
                        dve.wait_ge(unit_done, U_PA + 4 * i + 2 * j + 2)
                        dve.wait_ge(mg_sig, 2 * i + j + 1)
                        at = bass.ds(2 * i + j, 1)
                        m = merged[:, at, :].rearrange("p a t -> p (a t)")
                        chain.link(nc.vector.tensor_tensor(gate[:, j, :], gate[:, j, :], ps[:, 5 + 2 * j, :], ALU.mult))
                        nc.vector.tensor_tensor(m, m, gate[:, j, :], ALU.add).then_inc(mg_done, 1)
                        dve.wait_ge(m_hi_done, 2 * i + j + 1)
                        nc.vector.tensor_tensor(m_lo[:, at, :], merged[:, at, :], m_hi[:, at, :].bitcast(F32),
                                                ALU.subtract).then_inc(m_lo_done, 1)
                    chain.leave(DC // 2)

            def pooled():
                nc.vector.memset(u_pad[:, :, 0:8], 0.0)
                nc.vector.memset(u_pad[:, :, 8 + T:], 0.0).then_inc(upad_done, 1)
                dve.wait_ge(inv_in, 16)

                def tail(c, first):
                    dve.wait_ge(y_hi_done, first + c + 1)
                    nc.vector.tensor_tensor(y_lo[:, c, :], scr[:, c, :], y_hi[:, c, :].bitcast(F32), ALU.subtract
                                            ).then_inc(y_lo_done, 1)

                for c in range(DC):
                    g = c // 2
                    w = POOL_W[g]
                    dve.wait_ge(ev_done, EV_POOL + 2 + c + 1)
                    u = u_pad[:, c % 2, :]
                    src, span, turn = u, 1, 0
                    while span < w:
                        dst = win[:, turn, :]
                        chain.link(nc.vector.tensor_tensor(dst[:, 2 * span - 1:], src[:, 2 * span - 1:],
                                                           src[:, span - 1:T + 16 - span], ALU.add))
                        src, span, turn = dst, 2 * span, 1 - turn
                    off = 8 + w // 2 - 1
                    chain.link(nc.vector.tensor_tensor(scr[:, c, :], src[:, off:off + T], inv_count[:, g, :], ALU.mult))
                    nc.vector.tensor_tensor(scr[:, c, :], scr[:, c, :], u[:, 8:8 + T], ALU.subtract).then_inc(pool_done, 1)
                    if c >= 1:
                        tail(c - 1, DC)
                tail(DC - 1, DC)
                for n in range(2):
                    dve.wait_ge(unit_done, U_MIX2 + n + 1)
                    dve.wait_ge(ev_done, EV_POOL + 2 + 2 * DC)
                    for c in range(4 * n, 4 * n + 4):
                        nc.vector.scalar_tensor_tensor(scr[:, c, :], ps[:, 4 - 4 * n + c % 4, :], p_("pool_scale", c, c + 1),
                                                       silu_z[:, c, :], ALU.mult, ALU.mult).then_inc(y_done, 1)
                    for c in range(4 * n, 4 * n + 4):
                        tail(c, 2 * DC)

            def output():
                for i in range(DC):
                    dve.wait_ge(unit_done, U_OUT + i + 1)
                    if i == 0:
                        dve.wait_ge(m_hi_done, DC)
                    nc.vector.tensor_copy(merged[:, i, :], ps[:, 2 + i % 2, :]).then_inc(out_done, 1)
                    if i == DC - 3:
                        norm_sum(5)
                dve.wait_ge(rms_done, 6)
                nc.vector.reciprocal(r_col[:, :], r_col[:, :]).then_inc(rstd_done, 1)
                dve.wait_ge(spread_done, 6)
                dve.wait_ge(ssq_done, 6)
                for c in range(DC):
                    nc.vector.scalar_tensor_tensor(scr[:, c, :], merged[:, c, :], p_("g_post", c, c + 1), ps[:, 1, :],
                                                   ALU.mult, ALU.mult).then_inc(sum_done, 1)
                for c in range(POOL_ADDS, DC):
                    add(c)

            def add(c):
                dve.wait_ge(sum_done, c + 1)
                nc.vector.tensor_tensor(x[:, c, :], x[:, c, :], scr[:, c, :], ALU.add).then_inc(x_out, 1)

            for credit in (ev_done, mg_done, out_done):
                dve.sem_inc(credit, 2)
            dve.sem_inc(hid_done, 2)
            dve.sem_inc(proj_done, 2)
            dve.sem_inc(o_lo_done, 1)
            dve.wait_ge(small_in, 32)
            dve.sem_inc(x_done, DC)
            norm_sum(0)
            norm(0, "g_ffn1")
            ffn(U_FFN1, 0, 1)
            norm(1, "g_mix")
            compressed()
            attention()
            linear()
            to_stream(U_MIXOUT, 2)
            norm(2, "g_ffn2")
            ffn(U_FFN2, 1, 3)
            dve.wait_ge(rms_done, 4)
            nc.vector.reciprocal(r_col[:, :], r_col[:, :]).then_inc(rstd_done, 1)
            dve.wait_ge(spread_done, 4)
            for c in range(DC):
                nc.vector.scalar_tensor_tensor(x[:, c, :], x[:, c, :], p_("g_final", c, c + 1), ps[:, 1, :],
                                               ALU.mult, ALU.mult).then_inc(x_done, 1)
            norm_sum(4)
            norm(4, "g_pre", at=3)
            gates()
            mlstm(0, core=False)
            with dve.Fori(1, MH) as h:
                chain.enter(h - 1, MLSTM_LINKS)
                mlstm(h)
                chain.leave(MH - 1)
            mlstm(MH, units=False)
            merge_b()
            pooled()
            merge_a()
            output()



def constants():
    c = np.zeros((P, CONST_COLS), np.float32)

    def put(name, value):
        at, width = CONSTS[name]
        c[:, at:at + width] = value

    p = np.arange(P)
    put("ident", np.eye(P))
    put("ones", 1.0)
    put("eps", EPS)
    put("one", 1.0)
    dist = p[:, None] - (np.arange(T)[None, :] - (T - P))
    put("dist", np.where(dist >= 0, dist, 256 * -NEG))
    put("keep", (np.arange(T) % GC != 0)[None, :])
    k, q = p[:, None], p[None, :]
    put("gmask", (k <= q) & (k // GC == q // GC))
    t = np.arange(T).reshape(TT, P).T
    end = np.arange(NCMP) * CMP_STRIDE + CMP_BLOCK - 1
    valid = end[None, None, :] <= t[:, :, None]
    put("cvalid", valid.reshape(P, -1))
    slopes = np.exp2(-8.0 * np.arange(1, NH + 1) / NH)
    put("slope", -slopes[None, :])
    put("upper", np.where(k <= q, 0.0, NEG))
    put("lower", np.where(k >= q, 0.0, NEG))
    center = np.arange(NCMP) * CMP_STRIDE + (CMP_BLOCK - 1) / 2.0
    cbias = -slopes[None, None, :, None] * (t[:, :, None, None] - center[None, None, None, :])
    cbias = np.where(valid[:, :, None, :], cbias, NEG).astype(np.float32).reshape(P, -1)
    tok = np.arange(T)
    inv = np.stack([1.0 / (np.clip(tok + (w - 1 - w // 2), 0, T - 1) - np.clip(tok - w // 2, 0, T - 1) + 1)
                    for w in POOL_W]).astype(np.float32)
    inv = np.ascontiguousarray(np.broadcast_to(inv.reshape(1, -1), (P, len(POOL_W) * T)))
    start = np.where(p[:, None] % 64 < 32, tok % MC == 0, tok % MC == MC - 1)
    row_const = np.concatenate([1.0 - start, np.where(start, NEG, 0.0)], axis=1).astype(np.float32)
    return c, cbias, inv, row_const


def tiled(w):
    K, N = w.shape
    return w.reshape(K // P, P, N // P, P).transpose(2, 1, 0, 3).reshape(N // P, P, K)


def ffNUNITS(w_gate, w_up, w_down):
    gu = np.stack([tiled(w_gate), tiled(w_up)], 1).reshape(2 * FT, P, D)
    down = w_down.reshape(FT // 2, 2, P, 2, 4, P).transpose(3, 0, 2, 1, 4, 5).reshape(FT, P, D)
    return [gu, down]


def columns(v):
    return np.asarray(v).reshape(-1, P).T


def layout(i):
    i = {k: np.asarray(v) for k, v in i.items()}
    split = np.cumsum([NH * DH] + [NG * DH] * 6 + [NH * 3, GH * GDK, GH * GDK, GH * GDV, GH * GDV, LOWR])
    q, kc, vc, ks, vs, kw, vw, gn, gq, gk, gv, gr, ga = np.split(i["w_in"][0], split[:-1], axis=1)
    q = q.reshape(D, NG, HPG, DH).transpose(0, 2, 1, 3).reshape(D, NH * DH)
    small = np.concatenate([gn, gn[:, :8], ga, gq[:, :P - 48]], axis=1)
    proj = np.concatenate([q, kc, vc, ks, vs, kw, vw, small, gq, gk, gv, gr], axis=1)
    w_out = i["w_out"][0]
    w_out = np.concatenate([w_out[:NH * DH].reshape(NG, HPG, DH, D).transpose(1, 0, 2, 3).reshape(NH * DH, D),
                            w_out[NH * DH:]], axis=0)
    w2 = i["w_in_2"][0]
    sizes = [D] * 7 + [16, D, D]
    u_a, z_a, q2, k2, v2, o2, z_b, gates, g_a, g_b = np.split(w2, np.cumsum(sizes)[:-1], axis=1)
    g4 = gates.reshape(D, 2, 2, MH)
    fill = gates[:, :1]
    cols = []
    for kind in range(2):
        for direction in range(2):
            cols += [g4[:, direction, kind], np.repeat(fill, 32 - MH, axis=1)]
    gates_w = np.concatenate(cols, axis=1)
    mix = i["pool_mix_w_2"][0].reshape(2, 2, 2, P, 2, P).transpose(0, 3, 1, 4, 2, 5).reshape(2, P, D)
    ga_t, gb_t = tiled(g_a), tiled(g_b)
    heads = np.stack([tiled(w).reshape(MH, 2, P, D) for w in (q2, k2, v2, o2, z_b)], 1).reshape(-1, P, D)
    units = np.concatenate(
        ffNUNITS(i["ffn1_w_gate"][0], i["ffn1_w_up"][0], i["ffn1_w_down"][0])
        + [tiled(proj), tiled(w_out)]
        + ffNUNITS(i["ffn2_w_gate"][0], i["ffn2_w_up"][0], i["ffn2_w_down"][0])
        + [tiled(gates_w), heads,
           gb_t, tiled(i["w_proj_mlstm_2"][0]),
           tiled(u_a), tiled(z_a), mix,
           np.stack([ga_t, tiled(i["w_proj_pool_2"][0])], 1).reshape(-1, P, D),
           tiled(i["w_out_2"][0])], axis=0)
    assert units.shape[0] == NUNITS, (units.shape, NUNITS)
    param = np.zeros((P, PARAM_COLS), np.float32)

    def put(name, value, rows=slice(None)):
        at, width = PARAMS[name]
        param[rows, at:at + width] = value

    put("g_ffn1", columns(i["ffn1_norm"][0]))
    put("g_mix", columns(i["mix_norm"][0]))
    put("g_ffn2", columns(i["ffn2_norm"][0]))
    put("g_final", columns(i["final_norm"]))
    put("g_pre", columns(i["norm_pre_g_2"][0]))
    put("g_post", columns(i["norm_post_g_2"][0]))
    put("b_a", columns(i["gla_b_a"][0]))
    put("g_gla", columns(i["gla_norm"][0]))
    put("pool_scale", columns(i["pool_scale_2"][0]))
    put("conv_w", i["conv_qk_w_2"][0].reshape(CONV, 16, P).transpose(2, 1, 0).reshape(P, 16 * CONV))
    put("conv_b", columns(i["conv_qk_b_2"][0]))
    put("g_mlstm", columns(i["mlstm_norm_g_2"][0]))
    put("b_merge", np.concatenate([columns(i["b_merge_2"][0, 0]), columns(i["b_merge_2"][0, 1])], axis=1))
    for direction in range(2):
        put("b_if", i["b_igate_2"][0, direction][:, None], slice(32 * direction, 32 * direction + MH))
        put("b_if", i["b_fgate_2"][0, direction][:, None], slice(64 + 32 * direction, 64 + 32 * direction + MH))
    pe = np.stack([i["nsa_pe_k"][0], i["nsa_pe_v"][0]]).reshape(2, CMP_BLOCK // 2, 2 * DH)
    put("pe", pe.transpose(2, 0, 1).reshape(P, 32))
    put("w2", np.concatenate([i["nsa_w2_k"][0], i["nsa_w2_v"][0]], axis=1))
    put("w_a2", i["gla_w_a2"][0], slice(32, 32 + LOWR))
    w1 = np.stack([i["nsa_w1_k"][0], i["nsa_w1_v"][0]]).reshape(2, CMP_BLOCK // 2, P, CMP_HID)
    w1 = w1.transpose(2, 0, 1, 3).reshape(P, -1)
    const, cbias, inv, row_const = constants()
    return {"x": i["x"][0].T, "units": units, "param": param, "const": const, "w1": w1, "cbias": cbias,
            "inv_count": inv, "row_const": row_const}


def kernel(**inputs):
    import concourse.bacc as bacc
    from concourse.bass_utils import run_bass_kernel_spmd

    nc = bacc.Bacc("TRN2", target_bir_lowering=False, num_devices=1)
    arrays = {f"in_{k}": np.ascontiguousarray(v) for k, v in layout(inputs).items()}
    dram = {k[3:]: nc.dram_tensor(k, a.shape, mybir.dt.from_np(a.dtype), kind="ExternalInput").ap()
            for k, a in arrays.items()}
    out = nc.dram_tensor("out", (D, T), F32, kind="ExternalOutput").ap()
    build(nc, dram, out)
    r = run_bass_kernel_spmd(nc, [arrays], core_ids=[0])
    return np.ascontiguousarray(r.results[0]["out"].T)[None]
```
